# Optimizing a Trainium2 kernel written in Bass

```python
import math
import jax, jax.numpy as jnp
from jax import lax
import numpy as np

D_MODEL = 2048
BATCH = 1
SEQ = 512
DEPTH = 1

N_MIXERS = 4
N_SWA = (DEPTH + 3) // N_MIXERS
N_RWKV = (DEPTH + 2) // N_MIXERS
N_MLSTM = (DEPTH + 1) // N_MIXERS
N_FOX = DEPTH // N_MIXERS

SWA_HEAD_DIM = 64
SWA_HEADS = D_MODEL // SWA_HEAD_DIM
SWA_KV_HEADS = SWA_HEADS // 8
SWA_GROUP = SWA_HEADS // SWA_KV_HEADS
SWA_WIDTH = SWA_HEADS * SWA_HEAD_DIM
SWA_KV_WIDTH = SWA_KV_HEADS * SWA_HEAD_DIM
SWA_IN = 2 * SWA_WIDTH + 2 * SWA_KV_WIDTH
SWA_WINDOW = 128
SWA_BLOCK = 128
REL_BUCKETS = 32
REL_MAX_DIST = 128
RWKV_HEAD_DIM = 64
RWKV_HEADS = D_MODEL // RWKV_HEAD_DIM
RWKV_DECAY_LORA = 96
RWKV_AAA_LORA = 96
RWKV_N_MIX = 6
MLSTM_HEADS = 8
MLSTM_V_DIM = D_MODEL // MLSTM_HEADS
MLSTM_QK_DIM = MLSTM_V_DIM // 2
MLSTM_QK_WIDTH = MLSTM_HEADS * MLSTM_QK_DIM
MLSTM_V_WIDTH = MLSTM_HEADS * MLSTM_V_DIM
MLSTM_IN = 2 * MLSTM_QK_WIDTH + 3 * MLSTM_V_WIDTH + 2 * MLSTM_HEADS
MLSTM_CHUNK = 128
FOX_HEAD_DIM = 64
FOX_HEADS = D_MODEL // FOX_HEAD_DIM
FOX_WIDTH = FOX_HEADS * FOX_HEAD_DIM
FOX_IN = 4 * FOX_WIDTH + FOX_HEADS
FOX_BLOCK = 128

RMS_EPS = 1e-6
GN_EPS = 64e-5


def rms_norm(x, g):
    xf = x.astype(jnp.float32)
    y = xf * lax.rsqrt(jnp.mean(xf * xf, axis=-1, keepdims=True) + RMS_EPS)
    return (y * g.astype(jnp.float32)).astype(x.dtype)

def t5_bucket(dist):
    max_exact = REL_BUCKETS // 2
    d_f = jnp.maximum(dist, 1).astype(jnp.float32)
    large = max_exact + (jnp.log(d_f / max_exact) / math.log(REL_MAX_DIST / max_exact)
                         * (REL_BUCKETS - max_exact)).astype(jnp.int32)
    large = jnp.minimum(large, REL_BUCKETS - 1)
    return jnp.where(dist < max_exact, dist, large)

def swa_sink_mixer(h, w_in, q_gain, k_gain, sinks, rel_table, w_out):
    bsz, seq, _ = h.shape
    L = SWA_BLOCK
    nb = seq // L
    q, k, v, gate = jnp.split(h @ w_in, [SWA_WIDTH, SWA_WIDTH + SWA_KV_WIDTH,
                                         SWA_WIDTH + 2 * SWA_KV_WIDTH], axis=-1)
    q = rms_norm(q.reshape(bsz, seq, SWA_KV_HEADS, SWA_GROUP, SWA_HEAD_DIM), q_gain)
    k = rms_norm(k.reshape(bsz, seq, SWA_KV_HEADS, SWA_HEAD_DIM), k_gain)
    v = v.reshape(bsz, seq, SWA_KV_HEADS, SWA_HEAD_DIM)
    pad = ((0, 0), (L, 0), (0, 0), (0, 0))
    k_pad = jnp.pad(k, pad)
    v_pad = jnp.pad(v, pad)
    qi = jnp.arange(L)[:, None]
    kj = jnp.arange(2 * L)[None, :]
    dist = qi + L - kj
    in_band = (dist >= 0) & (dist < SWA_WINDOW)
    bias = rel_table.astype(jnp.float32)[t5_bucket(jnp.maximum(dist, 0))]
    bias = bias.transpose(2, 0, 1).reshape(SWA_KV_HEADS, SWA_GROUP, L, 2 * L)
    sink = sinks.astype(jnp.float32).reshape(SWA_KV_HEADS, SWA_GROUP, 1, 1)
    scale = SWA_HEAD_DIM ** -0.5
    q_blocks = q.reshape(bsz, nb, L, SWA_KV_HEADS, SWA_GROUP, SWA_HEAD_DIM).transpose(1, 0, 2, 3, 4, 5)

    def one_block(args):
        j, qj = args
        start = j * L
        kb = lax.dynamic_slice_in_dim(k_pad, start, 2 * L, axis=1)
        vb = lax.dynamic_slice_in_dim(v_pad, start, 2 * L, axis=1)
        s = jnp.einsum('bqhgd,bkhd->bhgqk', qj, kb).astype(jnp.float32) * scale + bias
        valid = in_band & (start - L + kj >= 0)
        s = jnp.where(valid, s, -jnp.inf)
        m = jnp.maximum(jnp.max(s, axis=-1, keepdims=True), sink)
        p = jnp.exp(s - m)
        p = p / (jnp.sum(p, axis=-1, keepdims=True) + jnp.exp(sink - m))
        return jnp.einsum('bhgqk,bkhd->bqhgd', p.astype(vb.dtype), vb)

    o = lax.map(one_block, (jnp.arange(nb), q_blocks))
    o = o.transpose(1, 0, 2, 3, 4, 5).reshape(bsz, seq, SWA_WIDTH)
    return (o * jax.nn.silu(gate)) @ w_out

def rwkv7_mixer(h, mix, w_in, w0, w_lora1, w_lora2, a0, a_lora1, a_lora2,
                k_k, k_a, r_k, gn_w, gn_b, w_out):
    bsz, seq, d = h.shape
    H, N = RWKV_HEADS, RWKV_HEAD_DIM
    f32 = jnp.float32
    xx = jnp.pad(h, ((0, 0), (1, 0), (0, 0)))[:, :-1] - h
    xm = h[None] + xx[None] * mix[:, None, None, :]
    r, k, v, g = jnp.einsum('cbsd,cde->cbse', xm[:4], w_in)
    w_pre = (w0 + jnp.tanh(xm[4] @ w_lora1) @ w_lora2).astype(f32)
    log_w = -jnp.exp(-jax.nn.softplus(-w_pre) - 0.5)
    a = jax.nn.sigmoid((a0 + (xm[5] @ a_lora1) @ a_lora2).astype(f32))

    def heads(t):
        return t.astype(f32).reshape(bsz, seq, H, N)

    r, k, v, a, log_w = heads(r), heads(k), heads(v), heads(a), heads(log_w)
    kk = k * k_k.astype(f32).reshape(H, N)
    kk = kk / jnp.maximum(jnp.sqrt(jnp.sum(kk * kk, axis=-1, keepdims=True)), 1e-12)
    k = k * (1.0 + (a - 1.0) * k_a.astype(f32).reshape(H, N))

    def step(state, inp):
        r_t, w_t, k_t, v_t, kk_t, a_t = inp
        sa = jnp.einsum('bhvk,bhk->bhv', state, -kk_t)
        state = (state * w_t[:, :, None, :]
                 + sa[..., None] * (kk_t * a_t)[:, :, None, :]
                 + v_t[..., None] * k_t[:, :, None, :])
        return state, jnp.einsum('bhvk,bhk->bhv', state, r_t)

    def tm(t):
        return t.transpose(1, 0, 2, 3)

    state0 = jnp.zeros((bsz, H, N, N), f32)
    _, y = lax.scan(step, state0, (tm(r), tm(jnp.exp(log_w)), tm(k), tm(v), tm(kk), tm(a)))
    y = tm(y)
    mu = jnp.mean(y, axis=-1, keepdims=True)
    var = jnp.mean(jnp.square(y - mu), axis=-1, keepdims=True)
    y = ((y - mu) * lax.rsqrt(var + GN_EPS)).reshape(bsz, seq, d) * gn_w + gn_b
    bonus = jnp.sum(r * k * r_k.astype(f32), axis=-1, keepdims=True) * v
    y = y + bonus.reshape(bsz, seq, d)
    return (y.astype(h.dtype) * jax.nn.silu(g)) @ w_out

def mlstm_mixer(h, w_in, b_i, b_f, h_gain, w_out):
    bsz, seq, _ = h.shape
    H, dk, dv, L = MLSTM_HEADS, MLSTM_QK_DIM, MLSTM_V_DIM, MLSTM_CHUNK
    nc = seq // L
    f32 = jnp.float32
    s1 = MLSTM_QK_WIDTH
    s2 = s1 + MLSTM_QK_WIDTH
    s3 = s2 + MLSTM_V_WIDTH
    s4 = s3 + MLSTM_V_WIDTH
    s5 = s4 + MLSTM_V_WIDTH
    s6 = s5 + H
    q, k, v, o_pre, gate, i_pre, f_pre = jnp.split(h @ w_in, [s1, s2, s3, s4, s5, s6], axis=-1)
    q = q.astype(f32).reshape(bsz, seq, H, dk) * dk ** -0.5
    k = k.astype(f32).reshape(bsz, seq, H, dk)
    v = v.astype(f32).reshape(bsz, seq, H, dv)
    i_log = (i_pre + b_i).astype(f32)
    f_log = jax.nn.log_sigmoid((f_pre + b_f).astype(f32))

    def chunks(t):
        t = t.reshape((bsz, nc, L) + t.shape[2:])
        return jnp.moveaxis(t, (1, 3), (0, 2))

    tri = jnp.tril(jnp.ones((L, L), dtype=bool))

    def chunk_step(carry, inp):
        C, n, m = carry
        qc, kc, vc, ic, fc = inp
        b = jnp.cumsum(fc, axis=-1)
        g = b[..., -1]
        dmat = jnp.where(tri, b[..., :, None] - b[..., None, :] + ic[..., None, :], -jnp.inf)
        inter = b + m[..., None]
        m_t = jnp.maximum(inter, jnp.max(dmat, axis=-1))
        w_intra = jnp.exp(dmat - m_t[..., None])
        w_inter = jnp.exp(inter - m_t)
        sw = jnp.einsum('bhtd,bhsd->bhts', qc, kc) * w_intra
        num = (w_inter[..., None] * jnp.einsum('bhvk,bhtk->bhtv', C, qc)
               + jnp.einsum('bhts,bhsv->bhtv', sw, vc))
        den = w_inter * jnp.einsum('bhk,bhtk->bht', n, qc) + jnp.sum(sw, axis=-1)
        h_t = num / jnp.maximum(jnp.abs(den), jnp.exp(-m_t))[..., None]
        decay_s = g[..., None] - b + ic
        m_new = jnp.maximum(g + m, jnp.max(decay_s, axis=-1))
        ws = jnp.exp(decay_s - m_new[..., None])
        carry_scale = jnp.exp(g + m - m_new)
        C = carry_scale[..., None, None] * C + jnp.einsum('bhs,bhsv,bhsk->bhvk', ws, vc, kc)
        n = carry_scale[..., None] * n + jnp.einsum('bhs,bhsk->bhk', ws, kc)
        return (C, n, m_new), h_t

    carry0 = (jnp.zeros((bsz, H, dv, dk), f32), jnp.zeros((bsz, H, dk), f32), jnp.zeros((bsz, H), f32))
    _, hs = lax.scan(chunk_step, carry0, (chunks(q), chunks(k), chunks(v), chunks(i_log), chunks(f_log)))
    hs = jnp.moveaxis(hs, (0, 2), (1, 3)).reshape(bsz, seq, H, dv)
    hs = rms_norm(hs, h_gain).reshape(bsz, seq, MLSTM_V_WIDTH).astype(h.dtype)
    return (hs * jax.nn.sigmoid(o_pre) * jax.nn.silu(gate)) @ w_out

def fox_mixer(h, w_in, b_f, q_gain, k_gain, w_out):
    bsz, seq, _ = h.shape
    H, dh, L = FOX_HEADS, FOX_HEAD_DIM, FOX_BLOCK
    nb = seq // L
    W = FOX_WIDTH
    q, k, v, gate, f_pre = jnp.split(h @ w_in, [W, 2 * W, 3 * W, 4 * W], axis=-1)
    q = rms_norm(q.reshape(bsz, seq, H, dh), q_gain)
    k = rms_norm(k.reshape(bsz, seq, H, dh), k_gain)
    v = v.reshape(bsz, seq, H, dh)
    log_f = jax.nn.log_sigmoid((f_pre + b_f).astype(jnp.float32))
    F = jnp.cumsum(log_f, axis=1).transpose(0, 2, 1)
    q_blocks = q.reshape(bsz, nb, L, H, dh).transpose(1, 0, 2, 3, 4)
    F_blocks = F.reshape(bsz, H, nb, L).transpose(2, 0, 1, 3)
    key_pos = jnp.arange(seq)
    scale = dh ** -0.5

    def one_block(args):
        j, qj, Fj = args
        s = (jnp.einsum('bqhd,bkhd->bhqk', qj, k).astype(jnp.float32) * scale
             + (Fj[..., :, None] - F[:, :, None, :]))
        q_pos = j * L + jnp.arange(L)
        s = jnp.where(key_pos[None, :] <= q_pos[:, None], s, -jnp.inf)
        p = jax.nn.softmax(s, axis=-1)
        return jnp.einsum('bhqk,bkhd->bqhd', p.astype(v.dtype), v)

    o = lax.map(one_block, (jnp.arange(nb), q_blocks, F_blocks))
    o = o.transpose(1, 0, 2, 3, 4).reshape(bsz, seq, W)
    return (o * jax.nn.silu(gate)) @ w_out

def first_inputs(seed: int = 0) -> dict:
    key = jax.random.key(seed)
    keys = jax.random.split(key, 48)
    counter = [0]

    def next_key():
        kk = keys[counter[0]]
        counter[0] += 1
        return kk

    def nrm(shape, scale):
        return jax.random.normal(next_key(), shape, jnp.float32) * scale

    def gain(shape):
        return 1.0 + nrm(shape, 0.05)

    D = D_MODEL
    return {
        "x": nrm((BATCH, SEQ, D), 1.0),
        "rel_bias": nrm((REL_BUCKETS, SWA_HEADS), 0.2),
        "swa_norm": gain((N_SWA, D)),
        "swa_w_in": nrm((N_SWA, D, SWA_IN), D ** -0.5),
        "swa_q_gain": gain((N_SWA, SWA_HEAD_DIM)),
        "swa_k_gain": gain((N_SWA, SWA_HEAD_DIM)),
        "swa_sinks": nrm((N_SWA, SWA_HEADS), 0.5),
        "swa_w_out": nrm((N_SWA, SWA_WIDTH, D), SWA_WIDTH ** -0.5),
        "rwkv_norm": gain((N_RWKV, D)),
        "rwkv_mix": jax.random.uniform(next_key(), (N_RWKV, RWKV_N_MIX, D), jnp.float32),
        "rwkv_w_in": nrm((N_RWKV, 4, D, D), D ** -0.5),
        "rwkv_w0": -2.0 + nrm((N_RWKV, D), 1.0),
        "rwkv_w_lora1": nrm((N_RWKV, D, RWKV_DECAY_LORA), D ** -0.5),
        "rwkv_w_lora2": nrm((N_RWKV, RWKV_DECAY_LORA, D), 0.5 * RWKV_DECAY_LORA ** -0.5),
        "rwkv_a0": nrm((N_RWKV, D), 0.1),
        "rwkv_a_lora1": nrm((N_RWKV, D, RWKV_AAA_LORA), D ** -0.5),
        "rwkv_a_lora2": nrm((N_RWKV, RWKV_AAA_LORA, D), 0.5 * RWKV_AAA_LORA ** -0.5),
        "rwkv_k_k": 0.85 + nrm((N_RWKV, D), 0.05),
        "rwkv_k_a": 1.0 + nrm((N_RWKV, D), 0.05),
        "rwkv_r_k": nrm((N_RWKV, RWKV_HEADS, RWKV_HEAD_DIM), 0.1),
        "rwkv_gn_w": gain((N_RWKV, D)),
        "rwkv_gn_b": nrm((N_RWKV, D), 0.02),
        "rwkv_w_out": nrm((N_RWKV, D, D), D ** -0.5),
        "mlstm_norm": gain((N_MLSTM, D)),
        "mlstm_w_in": nrm((N_MLSTM, D, MLSTM_IN), D ** -0.5),
        "mlstm_b_i": nrm((N_MLSTM, MLSTM_HEADS), 0.1),
        "mlstm_b_f": 3.0 + nrm((N_MLSTM, MLSTM_HEADS), 0.5),
        "mlstm_h_gain": gain((N_MLSTM, MLSTM_HEADS, MLSTM_V_DIM)),
        "mlstm_w_out": nrm((N_MLSTM, MLSTM_V_WIDTH, D), MLSTM_V_WIDTH ** -0.5),
        "fox_norm": gain((N_FOX, D)),
        "fox_w_in": nrm((N_FOX, D, FOX_IN), D ** -0.5),
        "fox_b_f": 3.0 + nrm((N_FOX, FOX_HEADS), 0.5),
        "fox_q_gain": gain((N_FOX, FOX_HEAD_DIM)),
        "fox_k_gain": gain((N_FOX, FOX_HEAD_DIM)),
        "fox_w_out": nrm((N_FOX, FOX_WIDTH, D), FOX_WIDTH ** -0.5),
    }

def first_block(x, rel_bias, swa_norm, swa_w_in, swa_q_gain, swa_k_gain, swa_sinks, swa_w_out,
              rwkv_norm, rwkv_mix, rwkv_w_in, rwkv_w0, rwkv_w_lora1, rwkv_w_lora2, rwkv_a0,
              rwkv_a_lora1, rwkv_a_lora2, rwkv_k_k, rwkv_k_a, rwkv_r_k, rwkv_gn_w, rwkv_gn_b,
              rwkv_w_out, mlstm_norm, mlstm_w_in, mlstm_b_i, mlstm_b_f, mlstm_h_gain, mlstm_w_out,
              fox_norm, fox_w_in, fox_b_f, fox_q_gain, fox_k_gain, fox_w_out):
    for layer in range(DEPTH):
        kind, idx = layer % N_MIXERS, layer // N_MIXERS
        if kind == 0:
            x = x + swa_sink_mixer(rms_norm(x, swa_norm[idx]), swa_w_in[idx], swa_q_gain[idx],
                                   swa_k_gain[idx], swa_sinks[idx], rel_bias, swa_w_out[idx])
        elif kind == 1:
            x = x + rwkv7_mixer(rms_norm(x, rwkv_norm[idx]), rwkv_mix[idx], rwkv_w_in[idx],
                                rwkv_w0[idx], rwkv_w_lora1[idx], rwkv_w_lora2[idx], rwkv_a0[idx],
                                rwkv_a_lora1[idx], rwkv_a_lora2[idx], rwkv_k_k[idx], rwkv_k_a[idx],
                                rwkv_r_k[idx], rwkv_gn_w[idx], rwkv_gn_b[idx], rwkv_w_out[idx])
        elif kind == 2:
            x = x + mlstm_mixer(rms_norm(x, mlstm_norm[idx]), mlstm_w_in[idx], mlstm_b_i[idx],
                                mlstm_b_f[idx], mlstm_h_gain[idx], mlstm_w_out[idx])
        else:
            x = x + fox_mixer(rms_norm(x, fox_norm[idx]), fox_w_in[idx], fox_b_f[idx],
                              fox_q_gain[idx], fox_k_gain[idx], fox_w_out[idx])
    return x


N_META = 16
D_MIX = D_MODEL
Q_BLOCK = 128
ROPE_THETA = 10000.0

A_HEADS = 8
A_QK_DIM = 64
A_V_DIM = 2 * A_QK_DIM
A_WIDTH = A_HEADS * A_V_DIM
B_HEADS = 8
B_Q_LORA = 512
B_KV_LORA = 256
B_NOPE = 128
B_ROPE = 64
B_V_DIM = 128
B_WIDTH = B_HEADS * B_V_DIM

A_Q_COLS = A_HEADS * 2 * A_QK_DIM
A_K_COLS = A_HEADS * 2 * A_QK_DIM
A_V_COLS = A_WIDTH
A_G_COLS = A_WIDTH
B_CQ_COLS = B_Q_LORA
B_CKV_COLS = B_KV_LORA
B_KR_COLS = B_ROPE
B_G_COLS = B_WIDTH
IN_COLS = A_Q_COLS + A_K_COLS + A_V_COLS + A_G_COLS + B_CQ_COLS + B_CKV_COLS + B_KR_COLS + B_G_COLS
UQ_COLS = B_HEADS * (B_NOPE + B_ROPE)
UKV_COLS = B_HEADS * (B_NOPE + B_V_DIM)


def _rmsnorm(x, w):
    xf = x.astype(jnp.float32)
    xf = xf * lax.rsqrt(jnp.mean(xf * xf, axis=-1, keepdims=True) + RMS_EPS)
    return xf.astype(x.dtype) * w

def _rope(x, pos):
    half = x.shape[-1] // 2
    inv = ROPE_THETA ** (-jnp.arange(half, dtype=jnp.float32) / half)
    ang = pos.astype(jnp.float32)[:, None] * inv[None, :]
    cos, sin = jnp.cos(ang), jnp.sin(ang)
    xf = x.astype(jnp.float32)
    x1, x2 = xf[..., :half], xf[..., half:]
    return jnp.concatenate([x1 * cos - x2 * sin, x1 * sin + x2 * cos], axis=-1).astype(x.dtype)

def _sweep(block_fn, n_blocks):
    out = lax.map(block_fn, jnp.arange(n_blocks, dtype=jnp.int32) * Q_BLOCK)
    nb, b, h, qb, dv = out.shape
    return jnp.moveaxis(out, 0, 2).reshape(b, h, nb * qb, dv)

def _diff_attention(q, k, v, lam, slopes):
    L = k.shape[3]
    scale = A_QK_DIM ** -0.5
    k_pos = jnp.arange(L, dtype=jnp.int32)

    def block(start):
        qb = lax.dynamic_slice_in_dim(q, start, Q_BLOCK, axis=3)
        rel = (start + jnp.arange(Q_BLOCK, dtype=jnp.int32))[:, None] - k_pos[None, :]
        s = jnp.einsum('bhcqd,bhckd->bhcqk', qb, k).astype(jnp.float32) * scale
        s = s - slopes[:, None, None, None] * rel.astype(jnp.float32)
        s = jnp.where(rel >= 0, s, -jnp.inf)
        p = jax.nn.softmax(s, axis=-1)
        w = p[:, :, 0] - lam * p[:, :, 1]
        return jnp.einsum('bhqk,bhkd->bhqd', w.astype(v.dtype), v)

    return _sweep(block, L // Q_BLOCK)

def _mla_attention(q_nope, q_pe, k_nope, k_pe, v):
    L = k_nope.shape[2]
    scale = (B_NOPE + B_ROPE) ** -0.5
    k_pos = jnp.arange(L, dtype=jnp.int32)

    def block(start):
        qn = lax.dynamic_slice_in_dim(q_nope, start, Q_BLOCK, axis=2)
        qp = lax.dynamic_slice_in_dim(q_pe, start, Q_BLOCK, axis=2)
        rel = (start + jnp.arange(Q_BLOCK, dtype=jnp.int32))[:, None] - k_pos[None, :]
        s = (jnp.einsum('bhqd,bhkd->bhqk', qn, k_nope) + jnp.einsum('bhqd,bkd->bhqk', qp, k_pe)).astype(jnp.float32) * scale
        s = jnp.where(rel >= 0, s, -jnp.inf)
        p = jax.nn.softmax(s, axis=-1)
        return jnp.einsum('bhqk,bhkd->bhqd', p.astype(v.dtype), v)

    return _sweep(block, L // Q_BLOCK)

def second_inputs(seed: int = 0) -> dict:
    key = jax.random.key(seed)
    ks = jax.random.split(key, 13)
    f32 = jnp.float32
    n = lambda k, shp: jax.random.normal(k, shp, dtype=f32)
    return {
        "x": n(ks[0], (BATCH, SEQ, D_MODEL)),
        "meta_tokens": n(ks[1], (N_META, D_MODEL)),
        "attn_norm_w": 1.0 + 0.02 * n(ks[2], (DEPTH, D_MODEL)),
        "w_in": n(ks[3], (DEPTH, D_MODEL, IN_COLS)) * D_MODEL ** -0.5,
        "diff_lambda": 0.1 * n(ks[4], (DEPTH, 4, A_QK_DIM)),
        "diff_subln_w": 1.0 + 0.02 * n(ks[5], (DEPTH, A_V_DIM)),
        "mla_q_norm_w": 1.0 + 0.02 * n(ks[6], (DEPTH, B_Q_LORA)),
        "w_uq": n(ks[7], (DEPTH, B_Q_LORA, UQ_COLS)) * B_Q_LORA ** -0.5,
        "mla_kv_norm_w": 1.0 + 0.02 * n(ks[8], (DEPTH, B_KV_LORA)),
        "w_ukv": n(ks[9], (DEPTH, B_KV_LORA, UKV_COLS)) * B_KV_LORA ** -0.5,
        "w_out": n(ks[10], (DEPTH, D_MIX, D_MODEL)) * D_MIX ** -0.5,
        "final_norm_w": 1.0 + 0.02 * n(ks[11], (D_MODEL,)),
    }

def second_block(x, meta_tokens, attn_norm_w, w_in, diff_lambda, diff_subln_w,
              mla_q_norm_w, w_uq, mla_kv_norm_w, w_ukv, w_out, final_norm_w):
    B, S, D = x.shape
    L = S + N_META
    L_pad = -(-L // Q_BLOCK) * Q_BLOCK
    meta = jnp.broadcast_to(meta_tokens[None].astype(x.dtype), (B, N_META, D))
    h = jnp.concatenate([meta, x], axis=1)
    h = jnp.pad(h, ((0, 0), (0, L_pad - L), (0, 0)))
    pos = jnp.arange(L_pad, dtype=jnp.int32)
    slopes = jnp.exp2(-8.0 * jnp.arange(1, A_HEADS + 1, dtype=jnp.float32) / A_HEADS)
    splits = np.cumsum([A_Q_COLS, A_K_COLS, A_V_COLS, A_G_COLS, B_CQ_COLS, B_CKV_COLS, B_KR_COLS])

    for l in range(DEPTH):
        hn = _rmsnorm(h, attn_norm_w[l])
        proj = hn @ w_in[l]
        a_q, a_k, a_v, a_g, b_cq, b_ckv, b_kr, b_g = jnp.split(proj, list(splits), axis=-1)

        qA = a_q.reshape(B, L_pad, A_HEADS, 2, A_QK_DIM).transpose(0, 2, 3, 1, 4)
        kA = a_k.reshape(B, L_pad, A_HEADS, 2, A_QK_DIM).transpose(0, 2, 3, 1, 4)
        vA = a_v.reshape(B, L_pad, A_HEADS, A_V_DIM).transpose(0, 2, 1, 3)
        lam_init = 0.8 - 0.6 * math.exp(-0.3 * l)
        lp = diff_lambda[l].astype(jnp.float32)
        lam = jnp.exp(jnp.sum(lp[0] * lp[1])) - jnp.exp(jnp.sum(lp[2] * lp[3])) + lam_init
        oA = _diff_attention(qA, kA, vA, lam, slopes)
        oA = _rmsnorm(oA, diff_subln_w[l]) * (1.0 - lam_init)
        oA = oA.transpose(0, 2, 1, 3).reshape(B, L_pad, A_WIDTH) * jax.nn.silu(a_g)

        qB = (_rmsnorm(b_cq, mla_q_norm_w[l]) @ w_uq[l]).reshape(B, L_pad, B_HEADS, B_NOPE + B_ROPE).transpose(0, 2, 1, 3)
        q_nope, q_pe = qB[..., :B_NOPE], _rope(qB[..., B_NOPE:], pos)
        kvB = (_rmsnorm(b_ckv, mla_kv_norm_w[l]) @ w_ukv[l]).reshape(B, L_pad, B_HEADS, B_NOPE + B_V_DIM).transpose(0, 2, 1, 3)
        k_nope, vB = kvB[..., :B_NOPE], kvB[..., B_NOPE:]
        k_pe = _rope(b_kr, pos)
        oB = _mla_attention(q_nope, q_pe, k_nope, k_pe, vB)
        oB = oB.transpose(0, 2, 1, 3).reshape(B, L_pad, B_WIDTH) * jax.nn.silu(b_g)

        h = h + jnp.concatenate([oA, oB], axis=-1) @ w_out[l]

    y = _rmsnorm(h, final_norm_w)
    return y[:, N_META:N_META + S]


def setup_inputs(seed=0):
    out = dict(first_inputs(seed))
    for name, value in second_inputs(seed + 1).items():
        if name != "x":
            out[name + "_2"] = value
    return out


def reference(
    x, rel_bias, swa_norm, swa_w_in, swa_q_gain, swa_k_gain, swa_sinks, swa_w_out, rwkv_norm,
    rwkv_mix, rwkv_w_in, rwkv_w0, rwkv_w_lora1, rwkv_w_lora2, rwkv_a0, rwkv_a_lora1,
    rwkv_a_lora2, rwkv_k_k, rwkv_k_a, rwkv_r_k, rwkv_gn_w, rwkv_gn_b, rwkv_w_out, mlstm_norm,
    mlstm_w_in, mlstm_b_i, mlstm_b_f, mlstm_h_gain, mlstm_w_out, fox_norm, fox_w_in, fox_b_f,
    fox_q_gain, fox_k_gain, fox_w_out, meta_tokens_2, attn_norm_w_2, w_in_2, diff_lambda_2,
    diff_subln_w_2, mla_q_norm_w_2, w_uq_2, mla_kv_norm_w_2, w_ukv_2, w_out_2, final_norm_w_2,
):
    x = first_block(
        x, rel_bias, swa_norm, swa_w_in, swa_q_gain, swa_k_gain, swa_sinks, swa_w_out,
        rwkv_norm, rwkv_mix, rwkv_w_in, rwkv_w0, rwkv_w_lora1, rwkv_w_lora2, rwkv_a0,
        rwkv_a_lora1, rwkv_a_lora2, rwkv_k_k, rwkv_k_a, rwkv_r_k, rwkv_gn_w, rwkv_gn_b,
        rwkv_w_out, mlstm_norm, mlstm_w_in, mlstm_b_i, mlstm_b_f, mlstm_h_gain, mlstm_w_out,
        fox_norm, fox_w_in, fox_b_f, fox_q_gain, fox_k_gain, fox_w_out,
    )
    return second_block(
        x, meta_tokens_2, attn_norm_w_2, w_in_2, diff_lambda_2, diff_subln_w_2, mla_q_norm_w_2,
        w_uq_2, mla_kv_norm_w_2, w_ukv_2, w_out_2, final_norm_w_2,
    )


_drawn_inputs = setup_inputs


def setup_inputs(seed=0):
    import zlib

    import numpy as np

    out = dict(_drawn_inputs(seed))
    spreads = {}
    factors = {'swa_norm': 4.766,
     'swa_q_gain': 8.0,
     'swa_k_gain': 8.0,
     'swa_sinks': 8.0,
     'attn_norm_w_2': 4.489,
     'diff_subln_w_2': 7.967,
     'mla_q_norm_w_2': 8.0,
     'mla_kv_norm_w_2': 8.0,
     'final_norm_w_2': 2.865}
    for name, (base, spread) in spreads.items():
        noise = np.random.default_rng([zlib.crc32(name.encode()), seed]).standard_normal(out[name].shape)
        drawn = base * np.exp(spread * noise) if base else spread * noise
        out[name] = __import__('jax').numpy.asarray(drawn.astype(out[name].dtype))
    for name, factor in factors.items():
        out[name] = (out[name] * factor).astype(out[name].dtype)
    return out
```

```python
from contextlib import ExitStack
import math

import numpy as np
import concourse.bass as bass
from concourse import mybir

F32 = mybir.dt.float32
F32R = mybir.dt.float32r
ALU = mybir.AluOpType
ACT = mybir.ActivationFunctionType
AX = mybir.AxisListType

P = 128
D = 2048
S = 512
NT = S // P
KC = D // P
CW = 512
EPS = 1e-6
AHEAD = 3
HD = 64
KVH = 4
GROUP = 8
SKEW = 32
BIAS_W = 384
BANNED = -1e30
UNITS = (GROUP // 2) * NT
EARLY = 2


META = 16
KEYS = S + META
HEADS = 8
QKD = 64
VD = 128
ROPE = 64
QB = VD + ROPE
CKV = 256
CQ = 512
FULL = 96
LAM0 = 0.8 - 0.6 * math.exp(-0.3 * 0)
FLOOR = -3.0e38
A_SCALE = QKD ** -0.5
B_SCALE = QB ** -0.5
NU = 16
ORDER = [0, 1, 2, 3, 8, 9, 10, 11, 12, 13, 14, 15, 4, 5, 6, 7]


def width(j):
    return (j + 1) * P + META


ALIBI_AT = [sum(width(i) for i in range(j)) for j in range(NT + 1)]


def alibi_distance():
    q = np.arange(P)[:, None]
    tiles = []
    for j in range(NT):
        rel = P * j + q - np.arange((j + 1) * P)[None, :]
        far = np.where(rel >= 0, -rel.astype(np.float32), np.float32(BANNED * 1e4))
        tiles += [far, -(META + P * j + q - np.arange(META)[None, :]).astype(np.float32)]
    return np.concatenate(tiles, 1).astype(np.float32)


def causal_mask():
    mask = np.zeros((P, KEYS), np.float32)
    mask[:, S - P:S] = np.where(np.arange(P)[None, :] > np.arange(P)[:, None], BANNED, 0.0)
    return mask


def rotations():
    freq = np.float32(10000.0) ** (-np.arange(ROPE // 2, dtype=np.float32) / np.float32(ROPE // 2))
    angle = np.arange(KEYS, dtype=np.float32)[:, None] * freq[None, :]
    out = []
    for f in (np.cos(angle), np.sin(angle)):
        out.append(np.ascontiguousarray(f[META:].reshape(NT, P, ROPE // 2).transpose(1, 0, 2).reshape(P, -1)))
        out.append(np.ascontiguousarray(f[:META]))
    return out


def t5_onehot():
    dist = 255 - np.arange(BIAS_W)
    inside = (dist >= 0) & (dist < 128)
    near = np.maximum(dist, 1).astype(np.float32)
    large = 16 + (np.log(near / np.float32(16)) / np.float32(math.log(8.0)) * np.float32(16)).astype(np.int32)
    bucket = np.where(dist < 16, dist, np.minimum(large, 31))
    marks = np.zeros((33, BIAS_W), np.float32)
    marks[bucket[inside], np.nonzero(inside)[0]] = 1.0
    marks[32, ~inside] = 1.0
    return marks


def build(nc, a, out):
    with ExitStack() as ctx:
        at = [nc.sbuf_base + (-nc.sbuf_base) % 64]

        def place(name, shape, dt=F32, offset=None):
            size = 4
            for n in shape[1:]:
                size *= n
            if offset is None:
                offset = at[0]
                at[0] += size + (-size) % 32
            return nc.alloc_sbuf_tensor_at(name, shape, dt, offset=offset), offset

        def sb(name, shape, dt=F32):
            return place(name, shape, dt)[0]

        def over(name, shape, offset, dt=F32):
            return place(name, shape, dt, offset)[0]

        def sem(name):
            return ctx.enter_context(nc.semaphore(name))

        setA_hi, SETA = place("setA_hi", [P, KC, S], F32R)
        setA_lo = sb("setA_lo", [P, KC, S], F32R)
        setB_hi, B_HI = place("setB_hi", [P, KC, S], F32R)
        setB_lo, B_LO = place("setB_lo", [P, KC, S], F32R)
        x_nat = over("x_nat", [P, NT, D], B_HI)
        o_nat = over("o_nat", [P, 4, NT, CW], B_LO)
        bias = over("bias", [P, GROUP, 256], B_HI)
        qT = over("qT", [P, GROUP // 2, S], B_HI + 16384)
        kT = over("kT", [P, S], B_HI + 24576)
        k_twice = over("k_twice", [P, NT, 2, HD], B_HI + 26624)
        sm = over("sm", [P, 2, 2, 256], B_HI + 28672)
        w_raw = sb("w_raw", [P, 2, 4, CW])
        w_hi = sb("w_hi", [P, 4, CW], F32R)
        w_lo = sb("w_lo", [P, 4, CW], F32R)
        stage = sb("stage", [P, NT, CW])
        work, WORK = place("work", [P, NT, CW])
        x_in = over("x_in", [P, NT, CW], WORK)
        ident = sb("ident", [P, P])
        kn, MISC = place("kn", [P, NT, KVH, HD])
        v_nat = sb("v_nat", [P, NT, KVH, HD])
        vg = sb("vg", [P, NT, HD])
        p_w, P_W = place("p_w", [P, 2, 2, 256])
        pT = sb("pT", [P, 2, 4, P])
        gain_in = sb("gain_in", [P, KC])
        gain_qk = over("gain_qk", [P, 2, HD], B_LO + 4096)
        sinks = sb("sinks", [P, KVH * GROUP])
        sink_g = sb("sink_g", [P, GROUP])
        rel = over("rel", [33, KVH * GROUP], B_LO + 5120)
        marks = over("marks", [33, BIAS_W], B_LO)
        bias_row = over("bias_row", [KVH * GROUP, BIAS_W], B_LO + 2048)
        half = sb("half", [P, 32])
        ss_x = sb("ss_x", [P, NT])
        r_x = sb("r_x", [P, NT])
        ss_q = sb("ss_q", [P, 32])
        r_q = sb("r_q", [P, 32])
        m_w = sb("m_w", [P, 2, 2])
        negm = sb("negm", [P, 2, 2])
        sink_p = sb("sink_p", [P, 2, 2])
        sink_d = sb("sink_d", [P, 2, 2])
        sink_e = sb("sink_e", [P, 2, 2])
        den = sb("den", [P, 2, 2])
        rden = sb("rden", [P, 2, 2])
        ss_1 = sb("ss_1", [P, NT])
        ss_c = sb("ss_c", [P, NT])
        gain_2 = sb("gain_2", [P, KC])
        gain_c = sb("gain_c", [P, 4])

        meta_nat = over("meta_nat", [META, D], P_W)
        meta_sq = over("meta_sq", [META, D], MISC)
        sm2 = over("sm2", [P, 2, KEYS], MISC)
        p2 = over("p2", [P, 2, 2, KEYS], MISC + 4224)
        o_sq = over("o_sq", [P, NT, CW], MISC + 4224)
        natm_k = over("natm_k", [META, 2, VD], MISC + 12672)
        natm_v = over("natm_v", [P, 2, VD], MISC + 13696)
        stage_m = over("stage_m", [META, CW], MISC + 14720)
        mask = sb("mask", [P, KEYS])
        cqT_hi = over("cqT_hi", [P, 4, S], B_HI, F32R)
        cqT_lo = over("cqT_lo", [P, 4, S], B_HI + 8192, F32R)
        ckvT_hi = over("ckvT_hi", [P, 2, S], B_HI + 16384, F32R)
        ckvT_lo = over("ckvT_lo", [P, 2, S], B_HI + 20480, F32R)
        kpe = over("kpe", [P, NT, ROPE], B_HI + 24576)
        kpe_m = over("kpe_m", [META, ROPE], B_HI + 25600)
        tmp_m = over("tmp_m", [META, CW], B_HI + 25856)
        sum_m = over("sum_m", [META, CW], B_HI + 27904)
        nat_q = over("nat_q", [P, 2, NT, QB], B_HI)
        nat_k = over("nat_k", [P, 2, NT, VD], B_HI + 6144)
        nat_v = over("nat_v", [P, 2, NT, VD], B_HI + 10240)
        qnT = over("qnT", [P, 2, S], B_HI + 14336)
        qpT = over("qpT", [P, 2, S], B_HI + 18432)
        knT = over("knT", [P, 2, KEYS], B_HI + 22528)
        alibi = over("alibi", [P, ALIBI_AT[NT]], B_HI + 26752)
        pT2 = over("pT2", [P, 2, S], WORK)
        pTm = over("pTm", [P, 2, P], WORK + 4096)
        rope_t = over("rope_t", [P, 4, NT, ROPE // 2], WORK + 5120)
        metaT, METAT = place("metaT", [P, KC, FULL], F32R)
        alibi_h = over("alibi_h", [P, ALIBI_AT[NT]], METAT)
        ckvmT = sb("ckvmT", [P, 2, FULL], F32R)
        kpeT = sb("kpeT", [P, KEYS])
        cos = sb("cos", [P, NT, ROPE // 2])
        sin = sb("sin", [P, NT, ROPE // 2])
        cos_m = sb("cos_m", [META, ROPE // 2])
        sin_m = sb("sin_m", [META, ROPE // 2])
        gain_cq = sb("gain_cq", [P, 4])
        gain_ckv = sb("gain_ckv", [P, 2])
        subln = sb("subln", [P, VD])
        meta_f = over("meta_f", [P, KC, META], MISC + 8192)
        lam_in = over("lam_in", [P, 4, QKD], MISC + 8192)
        lam_s = sb("lam_s", [P, 2])
        neglam = sb("neglam", [P, 1])
        slopes = sb("slopes", [P, HEADS])
        slope_i = sb("slope_i", [P, 4])
        ss_m, r_m = sb("ss_m", [META, 1]), sb("r_m", [META, 1])
        r_2 = sb("r_2", [P, NT])
        tick = sb("tick", [P, 1])
        ss_kv, r_kv = sb("ss_kv", [P, NT + 1]), sb("r_kv", [P, NT + 1])
        ss_cq, r_cq = sb("ss_cq", [P, NT]), sb("r_cq", [P, NT])
        m_2, negm_2 = sb("m_2", [P, 2, 2]), sb("negm_2", [P, 2, 2])
        den_2, rden_2 = sb("den_2", [P, 2, 2]), sb("rden_2", [P, 2, 2])
        coef = sb("coef", [P, 2])
        ss_o, r_o = ss_q[:, 0:NT * 4], r_q[:, 0:NT * 4]
        ss_2, r_3 = sb("ss_2", [P, NT]), sb("r_3", [P, NT])
        h2 = over("h2", [P, 4, NT, CW], SETA)
        w_final = over("w_final", [P, D], SETA + 32768)

        acc = [ctx.enter_context(nc.psum_tensor(f"acc{t}", [P, CW], F32)) for t in range(NT)]
        sc2 = ctx.enter_context(nc.psum_tensor("sc2", [P, 2 * CW], F32))
        sc = [sc2[:, 0:CW], sc2[:, CW:2 * CW]]
        turn = [ctx.enter_context(nc.psum_tensor(f"turn{t}", [P, CW], F32)) for t in range(2)]
        o_ps = turn[1]

        x1_d = nc.dram_tensor("x1_d", (S, D), F32).ap()
        kv_d = nc.dram_tensor("kv_d", (KEYS, D), F32).ap()
        qa_d = nc.dram_tensor("qa_d", (S, HEADS * VD), F32).ap()
        qb_d = nc.dram_tensor("qb_d", (S, HEADS * QB), F32).ap()
        kvb_d = nc.dram_tensor("kvb_d", (KEYS, D), F32).ap()
        gate_d = nc.dram_tensor("gate_d", (S, HEADS * VD), F32).ap()
        row_d = nc.dram_tensor("row_d", (KVH * GROUP, SKEW + 1, BIAS_W), F32).ap()

        s_raw = [sem(f"s_raw{i}") for i in range(2)]
        s_raw_2nd = [sem(f"s_raw_2nd{i}") for i in range(2)]
        s_hi, s_lo, s_used = sem("s_hi"), sem("s_lo"), sem("s_used")
        s_acc, s_evac, s_stage_free = sem("s_acc"), sem("s_evac"), sem("s_stage_free")
        s_turned, s_turn_hi, s_turn_lo = sem("s_turned"), sem("s_turn_hi"), sem("s_turn_lo")
        s_x = [sem(f"s_x_in{j}") for j in range(4)]
        s_small, s_ident = sem("s_small"), sem("s_ident")
        s_half, s_rel = sem("s_half"), sem("s_rel")
        s_row_ps, s_row, s_row_d = sem("s_row_ps"), sem("s_row"), sem("s_row_d")
        s_bias = sem("s_bias")
        s_var, s_root = sem("s_var"), sem("s_root")
        s_d = sem("s_d")
        s_kn, s_qn, s_kdup = sem("s_kn"), sem("s_qn"), sem("s_kdup")
        s_qturn, s_qT = sem("s_qturn"), sem("s_qT")
        s_score, s_m, s_p = sem("s_score"), sem("s_m"), sem("s_p")
        s_tr, s_pT, s_pv, s_o = sem("s_tr"), sem("s_pT"), sem("s_pv"), sem("s_o")
        s_silu, s_og = sem("s_silu"), sem("s_og")
        s_xin, s_x1, s_x1d, s_gain_c = sem("s_xin"), sem("s_x1"), sem("s_x1d"), sem("s_gain_c")
        s_small2, s_out = sem("s_small2"), sem("s_out")
        s_meta_in, s_mturn, s_metaF, s_metaH, s_metaT = (sem("s_" + n) for n in ("meta_in", "mturn", "metaF", "metaH", "metaT"))
        s_meta, s_mtmp, s_mevac, s_mstage, s_mst = (sem("s_" + n) for n in ("meta", "mtmp", "mevac", "mstage", "mst"))
        s_kpe, s_kpe_ps, s_kpeT, s_ckvm = sem("s_kpe"), sem("s_kpe_ps"), sem("s_kpeT"), sem("s_ckvm")
        s_short = [sem(f"s_short{i}") for i in range(2)]
        s_st, s_gld, s_zero = sem("s_st"), sem("s_gld"), sem("s_zero")
        s_lam, s_alibi, s_fin_w, s_x1in, s_h2, s_fin = (sem("s_" + n) for n in ("lam", "alibi", "fin_w", "x1in", "h2", "fin"))

        class Attend:

            def __init__(self, kind):
                self.mla = kind == "mla"
                self.comps = 1 if self.mla else 2
                self.batches = 3 if self.mla else 2
                self.turn_after, self.values_after = (3, 5) if self.mla else (4, 6)
                self.ld_qk = [sem(f"s_{kind}_ld_qk{i}") for i in range(2)]
                self.ld_v = [sem(f"s_{kind}_ld_v{i}") for i in range(2)]
                (self.rope, self.full, self.free, self.score, self.m, self.p, self.w, self.pv, self.o, self.slope) = (
                    sem(f"s_{kind}_{n}") for n in ("rope", "full", "free", "score", "m", "p", "w", "pv", "o", "slope"))

        MLA, DIFF = Attend("mla"), Attend("diff")

        class Link:
            base, n = 0, 0

        link = Link()

        def after(eng, ins):
            link.n += 1
            ins.then_inc(s_d, 1)
            eng.wait_ge(s_d, link.base + link.n)

        x2 = a["x"]

        def unit_time(u):
            return 12 + 3 * u

        def turn_time(A, head, b):
            if head == 0:
                return 6 + b
            return 12 * head + ((2, 5, 7)[b] if A.mla else (5, 8)[b])

        block = ctx.enter_context(nc.Block())

        @block.sync
        def _(sp):
            w_in = a["swa_w_in"].rearrange("(q k p) c -> p q k c", p=P, k=4)
            w_out = a["swa_w_out"].rearrange("(q k p) c -> p q k c", p=P, k=4)

            def small(dst, src):
                sp.dma_start(dst, src).then_inc(s_small, 16)

            def load_chunk(w, col, q0, quads=(0, 1, 2, 3), odd=0):
                for q, rows in enumerate(quads):
                    col_ = sp.snap(col) if not isinstance(col, int) else col
                    sp.wait_ge(s_lo, 4 * (q0 + q) + 4)
                    sp.dma_start(w_raw[:, (q + odd) % 2], w[:, rows, :, bass.ds(col_, CW)]).then_inc(s_raw[(q + odd) % 2], 16)

            def load_x(j):
                cols = slice(j * CW, (j + 1) * CW)
                sp.dma_start(x_nat[:, :, cols], x2.rearrange("(t p) c -> p t c", p=P)[:, :, cols]).then_inc(s_x[j], 16)

            load_x(0)
            small(gain_in[:], a["swa_norm"])
            load_chunk(w_in, 2048, 0, quads=(0,))
            load_x(1)
            load_chunk(w_in, 2048, 1, quads=(1,), odd=1)
            load_x(2)
            load_x(3)
            load_chunk(w_in, 2048, 2, quads=(2, 3))
            small(rel[0:32, :], a["rel_bias"])
            small(marks[:], a["t5_marks"])
            small(sinks[:], a["swa_sinks"].partition_broadcast(P))
            small(gain_qk[:, 0], a["swa_q_gain"].partition_broadcast(P))
            small(gain_qk[:, 1], a["swa_k_gain"].partition_broadcast(P))
            with sp.Fori(0, 4) as i:
                load_chunk(w_in, i * CW, i * 4 + 4)
            with sp.Fori(0, 4) as i:
                load_chunk(w_in, i * CW + 2560, i * 4 + 20)
            small(gain_2[:], a["attn_norm_w"])
            with sp.Fori(0, 4) as i:
                load_chunk(w_out, i * CW, i * 4 + 36)
            for dst, name in ((gain_cq, "mla_q_norm_w"), (gain_ckv, "mla_kv_norm_w"), (cos, "cos"), (sin, "sin"),
                              (cos_m, "cos_m"), (sin_m, "sin_m"), (slopes, "slopes")):
                sp.dma_start(dst[:] if name not in ("cos", "sin") else dst[:].rearrange("p t d -> p (t d)"),
                             a[name]).then_inc(s_small2, 16)
            sp.dma_start(subln[:], a["diff_subln_w"].partition_broadcast(P)).then_inc(s_small2, 16)
            sp.wait_ge(s_row_d, 16)
            sp.dma_start(mask[:], a["mask"]).then_inc(s_small2, 16)
            w_in2 = a["w_in"].rearrange("(q k p) c -> p q k c", p=P, k=4)
            w_out2 = a["w_out"].rearrange("(q k p) c -> p q k c", p=P, k=4)
            load_chunk(w_in2, 4608, 52)
            load_chunk(w_in2, 4096, 56)
            with sp.Fori(0, 4) as i:
                load_chunk(w_in2, i * CW + 1024, i * 4 + 60)
            w_uq = a["w_uq"].rearrange("(k p) c -> p k c", p=P)
            w_ukv = a["w_ukv"].rearrange("(k p) c -> p k c", p=P)
            for j in range(3):
                q = 76 + j
                sp.wait_ge(s_lo, 4 * q + 4)
                sp.dma_start(w_raw[:, q % 2], w_uq[:, :, j * CW:(j + 1) * CW]).then_inc(s_raw[q % 2], 16)
            for j in range(2):
                q = 79 + j
                sp.wait_ge(s_lo, 4 * q + 4)
                sp.dma_start(w_raw[:, q % 2, 0:2], w_ukv[:, :, 2 * j * CW:(2 * j + 1) * CW]).then_inc(s_raw[q % 2], 16)
                sp.dma_start(w_raw[:, q % 2, 2:4], w_ukv[:, :, (2 * j + 1) * CW:(2 * j + 2) * CW]).then_inc(s_raw_2nd[j], 16)
            with sp.Fori(0, 2) as i:
                load_chunk(w_in2, i * CW, i * 4 + 81, odd=1)
            with sp.Fori(0, 2) as i:
                load_chunk(w_in2, i * CW + 4928, i * 4 + 89, odd=1)
            with sp.Fori(0, 2) as i:
                load_chunk(w_in2, i * CW + 3072, i * 4 + 97, odd=1)
            with sp.Fori(0, 4) as i:
                load_chunk(w_out2, i * CW, i * 4 + 105, quads=[k // 4 for k in ORDER[::4]], odd=1)
            for c in range(4):
                sp.wait_ge(s_fin, c + 1)
                sp.dma_start(out[:, c * CW:(c + 1) * CW].rearrange("(t p) c -> p t c", p=P), h2[:, c]).then_inc(s_out, 16)
            sp.wait_ge(s_out, 64)

        PIECES = 484
        Q_BASE, UQ, UKV = 324, 304, 316

        @block.tensor
        def _(pe):
            mm = nc.tensor.matmul

            def project(n, c, k, t, hi, lo, cols=CW, K=KC, slot=None, kc=None):
                if t == 0:
                    pe.wait_ge(s_lo, n + 8 + 1)
                if k == 0:
                    pe.wait_ge(s_evac, 4 * c + t + 1)
                rows = slice(t * P, (t + 1) * P)
                slot = k % 4 if slot is None else slot
                kc = k if kc is None else kc
                wh, wl = w_hi[:, slot, 0:cols], w_lo[:, slot, 0:cols]
                mm(acc[t][:, 0:cols], hi[:, kc, rows], wh, start=(k == 0), stop=False)
                mm(acc[t][:, 0:cols], hi[:, kc, rows], wl, start=False, stop=False)
                last = mm(acc[t][:, 0:cols], lo[:, kc, rows], wh, start=False, stop=(k == K - 1))
                if t == NT - 1:
                    last.then_inc(s_used, 1)
                elif k == K - 1:
                    last.then_inc(s_acc, 1)

            def project_meta(n, m, k, lhs, cols=CW, K=KC, slot=None):
                if k == 0:
                    pe.wait_ge(s_mevac, m + 1)
                slot = k % 4 if slot is None else slot
                mm(sc[0][0:FULL, 0:cols], lhs[:, k], w_hi[:, slot, 0:cols], start=(k == 0), stop=False)
                last = mm(sc[0][0:FULL, 0:cols], lhs[:, k], w_lo[:, slot, 0:cols], start=False, stop=(k == K - 1))
                if k == K - 1:
                    last.then_inc(s_meta, 1)

            def turn4(b, bank, tiles):
                pe.wait_ge(s_turn_lo, b + 1)
                for t, tile in enumerate(tiles):
                    last = nc.tensor.transpose(turn[bank][:, t * P:(t + 1) * P], tile, ident[:])
                last.then_inc(s_turned, 1)
                return last

            pe.sem_inc(s_used, 4)
            pe.sem_inc(s_tr, EARLY)
            pe.sem_inc(s_pv, EARLY)
            pe.sem_inc(MLA.pv, EARLY)
            pe.sem_inc(DIFF.pv, EARLY)
            pe.wait_ge(s_ident, 2)
            for k in range(KC):
                for b in ([0, 1] if k == 0 else [k + 1] if k + 1 < KC else []):
                    if b % 4 == 0:
                        pe.wait_ge(s_x[b // 4], 16)
                    turn4(b, b % 2, [x_nat[:, t, b * P:(b + 1) * P] for t in range(NT)])
                pe.wait_ge(s_turn_lo, k + 1 + EARLY)
                for t in range(NT):
                    project(k, 0, k, t, setA_hi, setA_lo)
            pe.wait_ge(s_rel, 1)
            pe.wait_ge(s_small, 96)
            mm(sc[0][0:32, 0:BIAS_W], rel[:], marks[:], start=True, stop=True).then_inc(s_row_ps, 1)
            for k in range(KC):
                for t in range(NT):
                    project(KC + k, 1, k, t, setA_hi, setA_lo)

            def q_turn(g, b):
                if b == 0:
                    pe.wait_ge(s_kdup, g + 1)
                else:
                    pe.wait_ge(s_qn, g + 1)
                pe.wait_ge(s_qT, g * 5 + b + 1)
                for t in range(NT):
                    tile = k_twice[:, t].rearrange("p a d -> p (a d)") if b == 0 else stage[:, t, (b - 1) * P:b * P]
                    last = nc.tensor.transpose(turn[0][:, t * P:(t + 1) * P], tile, ident[:])
                last.then_inc(s_qturn, 1)

            def scores(g, u):
                hp, j = u // NT, u % NT
                if j == 0:
                    pe.wait_ge(s_qT, g * 5 + hp + 2 + 1)
                pe.wait_ge(s_m, g * UNITS + u + EARLY)
                lo = max(j - 1, 0) * P
                for h in range(2):
                    rows = slice(h * HD, (h + 1) * HD)
                    last = mm(sc[h][:, (P if j == 0 else 0):256],
                              qT[rows, hp, j * P:(j + 1) * P], kT[rows, lo:(j + 1) * P], start=True, stop=True)
                last.then_inc(s_score, 1)

            def turn_p(g, u):
                j = u % NT
                pe.wait_ge(s_p, g * UNITS + u + 1)
                if u == 0:
                    pe.wait_ge(s_qT, g * 5 + 5 + 1)
                else:
                    pe.wait_ge(s_pT, g * UNITS + u)
                for h in range(2):
                    for c in range(1 if j == 0 else 0, 2):
                        last = nc.tensor.transpose(turn[0][:, (2 * h + c) * P:(2 * h + c + 1) * P],
                                                   p_w[:, u % 2, h, c * P:(c + 1) * P], ident[:])
                last.then_inc(s_tr, 1)

            def values(g, u):
                j = u % NT
                pe.wait_ge(s_pT, g * UNITS + u + 1)
                pe.wait_ge(s_o, g * UNITS + u + 1)
                for h in range(2):
                    for c in range(1 if j == 0 else 0, 2):
                        last = mm(o_ps[:, h * HD:(h + 1) * HD], pT[:, u % 2, 2 * h + c], vg[:, j - 1 + c],
                                  start=(c == (1 if j == 0 else 0)), stop=(c == 1))
                last.then_inc(s_pv, 1)

            with pe.Fori(0, 4) as g:
                for H in range(32):
                    for t in (0, 1) if H % 2 == 0 else (2, 3):
                        project(g * KC + (2 * KC + H // 2), g + 2, H // 2, t, setA_hi, setA_lo)
                    if 8 <= H < 13:
                        q_turn(g, H - 8)
                    if 0 <= H - 16 < UNITS:
                        values(g, H - 16)
                    if 0 <= H - 14 < UNITS:
                        turn_p(g, H - 14)
                    if 0 <= H - 12 < UNITS:
                        scores(g, H - 12)
            pe.wait_ge(s_o, 4 * UNITS + 1)

            def og_turn(g, f):
                if f == 0:
                    pe.wait_ge(s_og, g + 1)
                last = turn4(g * 4 + (16 + f), f % 2, [stage[:, t, f * P:(f + 1) * P] for t in range(NT)])

            with pe.Fori(0, 3) as i:
                for k in range(KC):
                    for t in range(NT):
                        project(i * KC + (6 * KC + k), i + 6, k, t, setA_hi, setA_lo)
                    if 8 <= k < 12:
                        og_turn(i, k - 8)
            for k in range(KC):
                if 8 <= k < 12:
                    og_turn(3, k - 8)
                if k >= 12:
                    pe.wait_ge(s_turn_lo, 28 + (k - 12) + 1 + EARLY)
                elif k == 0:
                    pe.wait_ge(s_turn_lo, 28 + EARLY)
                for t in range(NT):
                    project(9 * KC + k, 9, k, t, setB_hi, setB_lo)
                if k == 12:
                    pe.wait_ge(s_meta_in, 16)
                    for f in range(KC):
                        last = nc.tensor.transpose(sc[1][:, f * META:(f + 1) * META], meta_nat[:, f * P:(f + 1) * P],
                                                   ident[0:META, 0:META])
                    last.then_inc(s_mturn, 1)

            def x1_turn(c, f):
                if f == 0:
                    pe.wait_ge(s_x1, c + 1)
                turn4(c * 4 + (32 + f), f % 2, [stage[:, t, f * P:(f + 1) * P] for t in range(NT)])

            with pe.Fori(0, 3) as i:
                for k in range(KC):
                    for t in range(NT):
                        project(i * KC + (10 * KC + k), i + 10, k, t, setB_hi, setB_lo)
                    if 4 <= k < 8:
                        x1_turn(i, k - 4)
            pe.wait_ge(s_turn_lo, 44 + EARLY)
            pe.wait_ge(s_metaT, 1)
            for k in range(KC):
                if 4 <= k < 8:
                    x1_turn(3, k - 4)
                if k >= 12:
                    pe.wait_ge(s_turn_lo, 44 + (k - 12) + 1 + EARLY)
                for t in range(NT):
                    if t == NT - 1:
                        project_meta(13 * KC + k, 0, k, metaT, 320)
                    project(13 * KC + k, 13, k, t, setA_hi, setA_lo, 320)
            for k in range(KC):
                for t in range(NT):
                    project(14 * KC + k, 14, k, t, setA_hi, setA_lo)
                if k == 4:
                    pe.wait_ge(s_kpe, 1)
                    for t in range(NT):
                        last = nc.tensor.transpose(sc[1][0:ROPE, t * P:(t + 1) * P], kpe[:, t], ident[:])
                    last.then_inc(s_kpe_ps, 1)
                    pe.wait_ge(s_mstage, 1)
                    pe.wait_ge(s_mevac, 2)
                    nc.tensor.transpose(sc[0][0:ROPE, 0:META], kpe_m[:], ident[0:META, 0:META])
                    for f in range(2):
                        last = nc.tensor.transpose(sc[0][:, (f + 1) * META:(f + 2) * META],
                                                   stage_m[:, f * P:(f + 1) * P], ident[0:META, 0:META])
                    last.then_inc(s_kpe_ps, 1)
                if 5 <= k < 7:
                    turn4(48 + k - 5, (k - 5) % 2, [stage[:, t, (k - 5) * P:(k - 4) * P] for t in range(NT)])
            pe.wait_ge(s_ckvm, 2)
            for k in range(KC):
                for t in range(NT):
                    if t == NT - 1:
                        project_meta(15 * KC + k, 1, k, metaT)
                    project(15 * KC + k, 15, k, t, setA_hi, setA_lo)
                if 5 <= k < 9:
                    if k == 5:
                        pe.wait_ge(s_evac, 4 * 14 + 8)
                    turn4(50 + k - 5, (k - 5) % 2, [stage[:, t, (k - 5) * P:(k - 4) * P] for t in range(NT)])
            with pe.Fori(0, 3) as i:
                for k in range(KC):
                    for t in range(NT):
                        if t == NT - 1:
                            project_meta(i * KC + (16 * KC + k), i + 2, k, metaT)
                        project(i * KC + (16 * KC + k), i + 16, k, t, setA_hi, setA_lo)
            pe.wait_ge(s_turn_lo, 54 + EARLY)
            for c in range(3):
                for k in range(4):
                    for t in range(NT):
                        project(UQ + 4 * c + k, 19 + c, k, t, cqT_hi, cqT_lo, K=4)
            for c in range(4):
                for k in range(2):
                    for t in range(NT):
                        if t == NT - 1:
                            project_meta(UKV + 2 * c + k, 5 + c, k, ckvmT, K=2, slot=(2 * c + k) % 4)
                        project(UKV + 2 * c + k, 22 + c, k, t, ckvT_hi, ckvT_lo, K=2, slot=(2 * c + k) % 4)

            def head_turn(A, i, head, b):
                buf, use = head % 2, i * 2 + (head // 2 + 1)
                if b == 0:
                    pe.wait_ge(A.rope if A.mla else A.ld_qk[buf], i * 4 + (head + 1) if A.mla else use * 48)
                t0_use(A, i)
                if b == A.batches - 1:
                    pe.wait_ge(A.o, i * NU + (done(A) + 1))
                    for t in range(NT):
                        nc.tensor.transpose(turn[0][:, t * P:(t + 1) * P], nat_k[:, buf, t], ident[:])
                    last = nc.tensor.transpose(turn[1][:, 0:META], natm_k[:, buf], ident[0:META, 0:META])
                elif b == 0:
                    for t in range(NT):
                        last = nc.tensor.transpose(turn[0][:, t * P:(t + 1) * P], nat_q[:, buf, t, 0:VD], ident[:])
                else:
                    for t in range(NT):
                        last = nc.tensor.transpose(turn[0][:, t * P:(t + 1) * P], nat_q[:, buf, t, QB - P:QB], ident[:])
                last.then_inc(A.full, 1)

            count = {"t0": 0, "pv": 0}

            def done(A):
                return count["pv"]

            def t0_use(A, i):
                pe.wait_ge(A.free, i * (4 * A.batches + NU) + (count["t0"] + 1))
                count["t0"] += 1

            def scores2(A, i, u, comp):
                head, j = u // NT, u % NT
                buf, lo = head % 2, S - (j + 1) * P
                if j == 0 and comp == 0:
                    pe.wait_ge(A.free, i * (4 * A.batches + NU) + (ready_at[head] + 1))
                pe.wait_ge(A.m, i * NU * A.comps + (u * A.comps + comp + 1))
                q = slice(j * P, (j + 1) * P)
                rows = slice(0, P) if A.mla else slice(comp * QKD, (comp + 1) * QKD)
                for dst, keys in ((sc2[:, lo:S], slice(0, (j + 1) * P)), (sc2[:, S:KEYS], slice(S, KEYS))):
                    last = mm(dst, qnT[rows, buf, q], knT[rows, buf, keys], start=True, stop=not A.mla)
                    if A.mla:
                        last = mm(dst, qpT[:, buf, q], kpeT[:, keys], start=False, stop=True)
                last.then_inc(A.score, 1)

            def turn_p2(A, i, u):
                j = u % NT
                pe.wait_ge(A.p if A.mla else A.w, i * NU + (u + 1))
                t0_use(A, i)
                pe.wait_ge(A.o, i * NU + (u + 1))
                src = p2[:, u % 2, 0]
                nc.tensor.transpose(turn[1][0:META, P:2 * P], src[:, S:KEYS], ident[:])
                for b in range(j + 1):
                    at_ = S - (j + 1 - b) * P
                    last = nc.tensor.transpose(turn[0][:, b * P:(b + 1) * P], src[:, at_:at_ + P], ident[:])
                last.then_inc(A.full, 1)

            def values2(A, i, u):
                head, j = u // NT, u % NT
                buf = head % 2
                pe.wait_ge(A.free, i * (4 * A.batches + NU) + (count["t0"] + 1))
                if j == 0:
                    pe.wait_ge(A.ld_v[buf], (i * 2 + (head // 2 + 1)) * 32)
                dst = turn[1][:, 2 * P:3 * P]
                for b in range(j + 1):
                    mm(dst, pT2[:, u % 2, b * P:(b + 1) * P], nat_v[:, buf, b], start=(b == 0), stop=False)
                mm(dst, pTm[:, u % 2], natm_v[:, buf], start=False, stop=True).then_inc(A.pv, 1)
                count["pv"] += 1

            def attend_body(A, i, n0, c0):
                count["t0"] = count["pv"] = 0
                ready_at.clear()
                for Q in range(4 * KC):
                    k, t = Q // 4, Q % 4
                    project(i * KC + (n0 + k), i + c0, k, t, setA_hi, setA_lo)
                    if A.mla and Q == 5:
                        pe.wait_ge(s_zero, 1)
                    for u in range(NU):
                        if Q == unit_time(u) + A.values_after:
                            values2(A, i, u)
                    for head in range(4):
                        for b in range(A.batches):
                            if Q == turn_time(A, head, b):
                                head_turn(A, i, head, b)
                                ready_at[head] = count["t0"]
                    for u in range(NU):
                        if Q == unit_time(u):
                            scores2(A, i, u, 0)
                        if not A.mla and Q == unit_time(u) + 1:
                            scores2(A, i, u, 1)
                    for u in range(NU):
                        if Q == unit_time(u) + A.turn_after:
                            turn_p2(A, i, u)

            ready_at = {}
            with pe.Fori(0, 2) as i:
                attend_body(MLA, i, Q_BASE, 26)
            pe.wait_ge(MLA.o, 2 * NU + 1)
            with pe.Fori(0, 2) as i:
                attend_body(DIFF, i, Q_BASE + 2 * KC, 28)
            pe.wait_ge(DIFF.o, 2 * NU + 1)

            def gate_turn(b, f, og):
                if f == 0:
                    pe.wait_ge(s_og, og)
                turn4(b + f, f % 2, [stage[:, t, f * P:(f + 1) * P] for t in range(NT)])

            for k in range(KC):
                for t in range(NT):
                    project(Q_BASE + 4 * KC + k, 30, k, t, setA_hi, setA_lo)
                if 5 <= k < 9:
                    gate_turn(54, k - 5, 5)
                if k >= 14:
                    gate_turn(58, 2 * (k - 14), 6)
                    gate_turn(58, 2 * (k - 14) + 1, 6)
            for k in range(KC):
                for t in range(NT):
                    project(Q_BASE + 5 * KC + k, 31, k, t, setA_hi, setA_lo)
                if 8 <= k < 12:
                    gate_turn(62, k - 8, 7)
            pe.wait_ge(s_turn_lo, 66 + EARLY)
            for k in range(KC):
                if 7 <= k < 11:
                    gate_turn(66, k - 7, 8)
                if k >= 12:
                    pe.wait_ge(s_turn_lo, 66 + (k - 12) + 1 + EARLY)
                for t in range(NT):
                    project(Q_BASE + 6 * KC + k, 32, k, t, setB_hi, setB_lo, kc=ORDER[k])
            with pe.Fori(0, 3) as i:
                for k in range(KC):
                    for t in range(NT):
                        project(i * KC + (Q_BASE + 7 * KC + k), i + 33, k, t, setB_hi, setB_lo, kc=ORDER[k])

        @block.scalar
        def _(act):
            def split_hi(n0, i, k):
                f = n0 + k + AHEAD
                if isinstance(i, int) and f + i * KC >= PIECES:
                    return
                q = f // 4
                if f % 4 == 0:
                    act.wait_ge(s_raw[q % 2], i * 32 + 16 * (q // 2 + 1))
                    if f in (UKV, UKV + 4):
                        act.wait_ge(s_raw_2nd[(f - UKV) // 4], 16)
                act.wait_ge(s_used, i * KC + f + 1)
                nc.scalar.activation(w_hi[:, f % 4], w_raw[:, q % 2, f % 4], ACT.Copy).then_inc(s_hi, 1)

            def evacuate(c, scale, end=None, cols=CW, dst=stage):
                end = (c + 1) * KC if end is None else end
                for t in range(NT):
                    if t < NT - 1:
                        act.wait_ge(s_acc, 3 * c + t + 1)
                    else:
                        act.wait_ge(s_used, end + 4)
                    nc.scalar.activation(dst[:, t, 0:cols], acc[t][:, 0:cols], ACT.Copy,
                                         scale=scale[:, t:t + 1] if scale is not None else 1.0).then_inc(s_evac, 1)

            def evacuate_meta(m, cols=CW):
                act.wait_ge(s_meta, m + 1)
                nc.scalar.activation(tmp_m[:, 0:cols], sc[0][32:32 + META, 0:cols], ACT.Copy).then_inc(s_mtmp, 1)

            def stored(chunk):
                act.wait_ge(s_short[chunk % 2], 16 * ((chunk - 18) // 2 + 1))

            def store(c, dst, col, m=None, src=stage, signal=s_st):
                cols = slice(col, col + CW) if isinstance(col, int) else bass.ds(act.snap(col), CW)
                act.wait_ge(s_evac, 4 * c + 8)
                act.dma_start(dst[0:S, :].rearrange("(t p) c -> p t c", p=P)[:, :, cols], src[:]).then_inc(signal, 16)
                if m is not None:
                    cols = slice(col, col + CW) if isinstance(col, int) else bass.ds(act.snap(col), CW)
                    act.wait_ge(s_mstage, m + 1)
                    act.dma_start(dst[S:KEYS, cols], stage_m[:]).then_inc(s_mst, 16)

            def turn_hi(b, bank, dst, gain):
                act.wait_ge(s_turned, b + 1)
                nc.scalar.activation(dst, turn[bank][:], ACT.Copy, scale=gain).then_inc(s_turn_hi, 1)

            act.sem_inc(s_evac, 4)
            act.sem_inc(s_qT, 1)
            act.sem_inc(MLA.free, 1)
            act.sem_inc(DIFF.free, 1)
            for f in range(AHEAD):
                if f == 0:
                    act.wait_ge(s_raw[0], 16)
                nc.scalar.activation(w_hi[:, f], w_raw[:, 0, f], ACT.Copy).then_inc(s_hi, 1)
            act.wait_ge(s_small, 16)
            for k in range(KC):
                for b in ([0, 1] if k == 0 else [k + 1] if k + 1 < KC else []):
                    turn_hi(b, b % 2, setA_hi[:, b], gain_in[:, b:b + 1])
                split_hi(0, 0, k)
            act.wait_ge(s_root, 1)
            evacuate(0, r_x)
            act.wait_ge(s_row_ps, 1)
            nc.scalar.activation(bias_row[:], sc[0][0:32, 0:BIAS_W], ACT.Copy).then_inc(s_row, 1)
            act.wait_ge(s_row, 1)
            act.dma_start(row_d, bias_row[:].unsqueeze(1).to_broadcast([32, SKEW + 1, BIAS_W])).then_inc(s_row_d, 16)
            for k in range(KC):
                split_hi(KC, 0, k)
            act.wait_ge(s_kn, 2)
            evacuate(1, r_x)

            def weigh(g, u):
                act.wait_ge(s_m, g * UNITS + u + 1 + EARLY)
                act.wait_ge(s_tr, g * UNITS + u + 1)
                first = P if u % NT == 0 else 0
                for h in range(2):
                    nc.scalar.activation(p_w[:, u % 2, h, first:], sm[:, u % 2, h, first:], ACT.Exp,
                                         bias=negm[:, u % 2, h:h + 1], accum_out=den[:, u % 2, h:h + 1])
                nc.scalar.activation(sink_e[:, u % 2], sink_d[:, u % 2], ACT.Exp).then_inc(s_p, 1)

            def keep_pT(g, u):
                act.wait_ge(s_tr, g * UNITS + u + 1 + EARLY)
                act.wait_ge(s_pv, g * UNITS + u + 1)
                nc.scalar.activation(pT[:, u % 2].rearrange("p a q -> p (a q)"), turn[0][:], ACT.Copy).then_inc(s_pT, 1)

            def keep_qT(g, b):
                act.wait_ge(s_qturn, g * 5 + b + 1)
                nc.scalar.activation(kT[:] if b == 0 else qT[:, b - 1], turn[0][:], ACT.Copy).then_inc(s_qT, 1)

            with act.Fori(0, 4) as g:
                for H in range(32):
                    if 0 <= H - 13 < UNITS:
                        weigh(g, H - 13)
                    if 8 <= H < 13:
                        keep_qT(g, H - 8)
                    if H % 2 == 0:
                        split_hi(2 * KC, g, H // 2)
                    if 0 <= H - 14 < UNITS:
                        keep_pT(g, H - 14)
                evacuate(g + 2, r_x)

            def gate_exp(g):
                act.wait_ge(s_evac, 4 * (g + 5) + 8)
                nc.scalar.activation(work[:], stage[:], ACT.Exp, scale=-1.0).then_inc(s_silu, 1)

            with act.Fori(0, 3) as i:
                for k in range(KC):
                    if k == 0:
                        gate_exp(i)
                    split_hi(6 * KC, i, k)
                    if 8 <= k < 12:
                        turn_hi(i * 4 + (16 + k - 8), k % 2, setB_hi[:, bass.ds(i * 4 + (k - 8), 1)].rearrange("p o s -> p (o s)"), 1.0)
                evacuate(i + 6, r_x)
            def load_residual(c):
                if isinstance(c, int):
                    act.wait_ge(s_og, 4)
                    cols = slice(c * CW, (c + 1) * CW)
                else:
                    act.wait_ge(s_x1, c)
                    cols = bass.ds(act.snap(c * CW), CW)
                act.dma_start(x_in[:], a["x"].rearrange("(t p) c -> p t c", p=P)[:, :, cols]).then_inc(s_xin, 16)

            def store_x1(c):
                cols = slice(c * CW, (c + 1) * CW) if isinstance(c, int) else bass.ds(act.snap(c * CW), CW)
                act.wait_ge(s_x1, c + 1)
                act.dma_start(x1_d.rearrange("(t p) c -> p t c", p=P)[:, :, cols], stage[:]).then_inc(s_x1d, 16)

            def x1_hi(c, f):
                if isinstance(c, int):
                    dst = setA_hi[:, 4 * c + f]
                else:
                    dst = setA_hi[:, bass.ds(c * 4 + f, 1)].rearrange("p o s -> p (o s)")
                act.wait_ge(s_gain_c, c + 1)
                turn_hi(c * 4 + (32 + f), f % 2, dst, gain_c[:, f:f + 1])

            for k in range(KC):
                if k == 0:
                    gate_exp(3)
                split_hi(9 * KC, 0, k)
                if 8 <= k < 12:
                    turn_hi(28 + k - 8, k % 2, setB_hi[:, 12 + k - 8], 1.0)
                if k == 0:
                    act.wait_ge(s_pv, 4 * UNITS + EARLY)
                    act.dma_start(meta_nat[:], a["meta_tokens"]).then_inc(s_meta_in, 16)
                if k == 11:
                    load_residual(0)
                if k == 14:
                    act.wait_ge(s_metaF, 1)
                    nc.scalar.activation(metaT[:, :, 0:META], meta_f[:], ACT.Copy).then_inc(s_metaH, 1)
            evacuate(9, None)
            with act.Fori(0, 3) as i:
                for k in range(KC):
                    split_hi(10 * KC, i, k)
                    if k == 3:
                        store_x1(i)
                    if 4 <= k < 8:
                        x1_hi(i, k - 4)
                    if k == 11:
                        load_residual(i + 1)
                act.wait_ge(s_x1d, i * 16 + 16)
                evacuate(i + 10, None)
            for k in range(KC):
                split_hi(13 * KC, 0, k)
                if k == 0:
                    act.wait_ge(s_metaT, 1)
                    act.dma_start(lam_in[:].rearrange("p a d -> p (a d)"),
                                  a["diff_lambda"].rearrange("a d -> (a d)").partition_broadcast(P)).then_inc(s_lam, 16)
                if k == 3:
                    store_x1(3)
                if 4 <= k < 8:
                    x1_hi(3, k - 4)
            act.wait_ge(s_x1d, 64)
            act.wait_ge(s_root, 8)
            evacuate(13, r_2, cols=320)
            evacuate_meta(0, 320)
            for k in range(KC):
                split_hi(14 * KC, 0, k)
                if k == 2:
                    act.wait_ge(s_lam, 17)
                    nc.scalar.activation(lam_s[:], lam_s[:], ACT.Exp).then_inc(s_lam, 1)
                if k == 5:
                    act.wait_ge(s_kpe_ps, 1)
                    nc.scalar.activation(kpeT[P - ROPE:P, 0:S], sc[1][0:ROPE, :], ACT.Copy)
                    act.wait_ge(s_kpe_ps, 2)
                    nc.scalar.activation(kpeT[P - ROPE:P, S:KEYS], sc[0][0:ROPE, 0:META], ACT.Copy).then_inc(s_kpeT, 1)
                    for f in range(2):
                        last = nc.scalar.activation(ckvmT[:, f, 0:META], sc[0][:, (f + 1) * META:(f + 2) * META], ACT.Copy,
                                                    scale=gain_ckv[:, f:f + 1])
                    last.then_inc(s_kpeT, 1)
                if 6 <= k < 8:
                    turn_hi(48 + k - 6, k % 2, ckvT_hi[:, k - 6], gain_ckv[:, k - 6:k - 5])
            evacuate(14, r_2)
            for k in range(KC):
                split_hi(15 * KC, 0, k)
                if 6 <= k < 10:
                    turn_hi(50 + k - 6, k % 2, cqT_hi[:, k - 6], gain_cq[:, k - 6:k - 5])
            evacuate(15, r_2)
            evacuate_meta(1)
            with act.Fori(0, 3) as i:
                for k in range(KC):
                    split_hi(16 * KC, i, k)
                    if k == 1:
                        store(i + 15, kv_d, i * CW, i + 1)
                act.wait_ge(s_st, i * 16 + 16)
                act.wait_ge(s_mst, i * 16 + 16)
                evacuate(i + 16, r_2)
                evacuate_meta(i + 2)
            act.wait_ge(s_root, 10)
            stages = (stage, work)
            for c in range(3):
                for k in range(4):
                    split_hi(UQ + 4 * c, 0, k)
                    if k == 0:
                        if c == 0:
                            store(18, kv_d, 3 * CW, 4, signal=s_short[0])
                        else:
                            store(18 + c, qb_d, (c - 1) * CW, src=stages[(c - 1) % 2], signal=s_short[c % 2])
                stored(max(18, 17 + c))
                evacuate(19 + c, r_cq, end=UQ + 4 * c + 4, dst=stages[c % 2])
            for c in range(4):
                for k in range(2):
                    split_hi(UKV + 2 * c, 0, k)
                    if k == 0:
                        if c == 0:
                            store(21, qb_d, 2 * CW, src=stages[0], signal=s_short[1])
                        else:
                            store(21 + c, kvb_d, (c - 1) * CW, 4 + c, src=stages[c % 2], signal=s_short[(21 + c) % 2])
                stored(20 + c)
                evacuate(22 + c, r_kv, end=UKV + 2 * c + 2, dst=stages[(c + 1) % 2])
                evacuate_meta(5 + c)
            store(25, kvb_d, 3 * CW, 8, signal=s_short[1])

            def keep_head(A, i, head, b):
                buf = head % 2
                act.wait_ge(A.full, i * (4 * A.batches + NU) + (count["t0"] + 1))
                count["t0"] += 1
                scale = B_SCALE if A.mla else A_SCALE
                if b == 0:
                    last = nc.scalar.activation(qnT[:, buf], turn[0][:], ACT.Copy, scale=scale)
                elif b < A.batches - 1:
                    last = nc.scalar.activation(qpT[P - ROPE:P, buf], turn[0][P - ROPE:P, :], ACT.Copy, scale=scale)
                else:
                    nc.scalar.activation(knT[:, buf, 0:S], turn[0][:], ACT.Copy)
                    last = nc.scalar.activation(knT[:, buf, S:KEYS], turn[1][:, 0:META], ACT.Copy)
                last.then_inc(A.free, 1)

            def weigh2(A, i, u, comp):
                lo, slot = S - (u % NT + 1) * P, u % 2 if A.mla else comp
                act.wait_ge(A.m, i * NU * A.comps + (u * A.comps + comp + 2))
                nc.scalar.activation(p2[:, u % 2, comp, lo:], sm2[:, slot, lo:], ACT.Exp, bias=negm_2[:, u % 2, comp:comp + 1],
                                     accum_out=den_2[:, u % 2, comp:comp + 1]).then_inc(A.p, 1)

            def keep_pT2(A, i, u):
                n = (u % NT + 1) * P
                act.wait_ge(A.full, i * (4 * A.batches + NU) + (count["t0"] + 1))
                count["t0"] += 1
                act.wait_ge(A.pv, i * NU + (u + 1))
                nc.scalar.activation(pT2[:, u % 2, 0:n], turn[0][:, 0:n], ACT.Copy)
                nc.scalar.activation(pTm[0:META, u % 2], turn[1][0:META, P:2 * P], ACT.Copy).then_inc(A.free, 1)

            count = {"t0": 0}

            def attend_body(A, i, n0, c0, n_store, dst):
                count["t0"] = 0
                for Q in range(4 * KC):
                    if Q % 4 == 0:
                        split_hi(n0, i, Q // 4)
                    if A.mla and Q == 5:
                        act.wait_ge(s_zero, 1)
                    for u in range(NU):
                        for comp in range(A.comps):
                            if Q == unit_time(u) + 1 + comp:
                                weigh2(A, i, u, comp)
                    for head in range(4):
                        for b in range(A.batches):
                            if Q == turn_time(A, head, b):
                                keep_head(A, i, head, b)
                    for u in range(NU):
                        if Q == unit_time(u) + A.turn_after:
                            keep_pT2(A, i, u)
                stored(25)
                act.wait_ge(s_st, (i + n_store) * 16)
                evacuate(i + c0, r_2, end=i * KC + (n0 + KC))
                store(i + c0, dst, i * CW)

            with act.Fori(0, 2) as i:
                attend_body(MLA, i, Q_BASE, 26, 3, qa_d)
            with act.Fori(0, 2) as i:
                attend_body(DIFF, i, Q_BASE + 2 * KC, 28, 5, gate_d)

            def load_gate(c):
                act.dma_start(stage[:], gate_d.rearrange("(t p) c -> p t c", p=P)[:, :, c * CW:(c + 1) * CW]).then_inc(s_gld, 16)

            def gate_exp2():
                nc.scalar.activation(work[:], stage[:], ACT.Exp, scale=-1.0).then_inc(s_silu, 1)

            act.wait_ge(DIFF.pv, 2 * NU + EARLY)
            for k in range(KC):
                split_hi(Q_BASE + 4 * KC, 0, k)
                if k == 0:
                    act.wait_ge(s_st, 7 * 16)
                    load_gate(0)
                if k == 2:
                    act.wait_ge(s_gld, 16)
                    gate_exp2()
                if 5 <= k < 9:
                    turn_hi(54 + k - 5, (k - 5) % 2, setB_hi[:, 8 + k - 5], 1.0)
                if k == 9:
                    load_gate(1)
                if k == 11:
                    act.wait_ge(s_gld, 32)
                    gate_exp2()
                if k >= 14:
                    for f in (2 * (k - 14), 2 * (k - 14) + 1):
                        turn_hi(58 + f, f % 2, setB_hi[:, 12 + f], 1.0)
            evacuate(30, r_2, end=Q_BASE + 5 * KC)
            for k in range(KC):
                split_hi(Q_BASE + 5 * KC, 0, k)
                if k == 1:
                    act.wait_ge(s_evac, 4 * 30 + 8)
                    gate_exp2()
                if 8 <= k < 12:
                    turn_hi(62 + k - 8, k % 2, setB_hi[:, k - 8], 1.0)
            evacuate(31, r_2, end=Q_BASE + 6 * KC)

            def load_x1(c):
                cols = slice(c * CW, (c + 1) * CW) if isinstance(c, int) else bass.ds(act.snap(c * CW), CW)
                act.dma_start(x_in[:], x1_d.rearrange("(t p) c -> p t c", p=P)[:, :, cols]).then_inc(s_x1in, 16)

            for k in range(KC):
                split_hi(Q_BASE + 6 * KC, 0, k)
                if k == 0:
                    act.wait_ge(s_evac, 4 * 31 + 8)
                    gate_exp2()
                    act.dma_start(w_final[:], a["final_norm_w"].partition_broadcast(P)).then_inc(s_fin_w, 16)
                if 7 <= k < 11:
                    turn_hi(66 + k - 7, (k - 7) % 2, setB_hi[:, 4 + k - 7], 1.0)
                if k == 11:
                    act.wait_ge(s_og, 8)
                    load_x1(0)
            evacuate(32, None, end=Q_BASE + 7 * KC)
            with act.Fori(0, 2) as i:
                for k in range(KC):
                    split_hi(Q_BASE + 7 * KC, i, k)
                    if k == 11:
                        act.wait_ge(s_h2, i + 1)
                        load_x1(i + 1)
                act.wait_ge(s_h2, i + 1)
                evacuate(i + 33, None, end=i * KC + (Q_BASE + 8 * KC))
            for k in range(KC):
                split_hi(Q_BASE + 9 * KC, 0, k)
                if k == 11:
                    act.wait_ge(s_h2, 3)
                    load_x1(3)
            act.wait_ge(s_h2, 3)
            evacuate(35, None, end=Q_BASE + 10 * KC)

        @block.gpsimd
        def _(pool):
            def split_lo(n0, i, k):
                f = n0 + k + AHEAD
                if isinstance(i, int) and f + i * KC >= PIECES:
                    return
                pool.wait_ge(s_hi, i * KC + f + 1)
                nc.gpsimd.tensor_tensor(w_lo[:, f % 4], w_raw[:, (f // 4) % 2, f % 4], w_hi[:, f % 4].bitcast(F32),
                                        ALU.subtract).then_inc(s_lo, 1)

            def root(dst, src, n, count, rows=P):
                pool.wait_ge(s_var, count)
                nc.gpsimd.tensor_tensor(dst, src, half[0:rows, 0:n], ALU.pow).then_inc(s_root, 1)

            pool.sem_inc(s_lo, 8)
            nc.gpsimd.memset(ident[:], 0.0).then_inc(s_ident, 1)
            nc.gpsimd.memset(half[:], -0.5).then_inc(s_half, 1)
            pool.wait_ge(s_ident, 1)
            nc.gpsimd.affine_select(out=ident[:], in_=ident[:], compare_op=ALU.not_equal, fill=1.0, base=0,
                                    pattern=[[-1, P]], channel_multiplier=1).then_inc(s_ident, 1)
            for f in range(AHEAD):
                pool.wait_ge(s_hi, f + 1)
                nc.gpsimd.tensor_tensor(w_lo[:, f], w_raw[:, 0, f], w_hi[:, f].bitcast(F32), ALU.subtract).then_inc(s_lo, 1)
            for k in range(KC):
                split_lo(0, 0, k)
            pool.wait_ge(s_half, 1)
            root(r_x[:], ss_x[:], NT, 1)
            for k in range(KC):
                split_lo(KC, 0, k)
                if k == 8:
                    root(r_q[:, 0:16], ss_q[:, 0:16], 16, 2)

            with pool.Fori(0, 4) as g:
                for H in range(32):
                    if H % 2 == 0:
                        split_lo(2 * KC, g, H // 2)
                    if H == 1:
                        pool.wait_ge(s_row_d, 16)
                        pool.wait_ge(s_o, g * UNITS + 1)
                        flat, heads = row_d.rearrange("h q m -> h (q m)"), bass.ds(pool.snap(g * GROUP), GROUP)
                        for q in range(0, P, SKEW):
                            skew = flat[:, P - 1 - q:P - 1 - q + SKEW * (BIAS_W - 1)].rearrange("h (q m) -> q h m", q=SKEW)
                            pool.dma_start(bias[q:q + SKEW], skew[:, heads, 0:256]).then_inc(s_bias, 16)
                    if H == 4:
                        root(r_q[:], ss_q[:], 32, g + 3)
            with pool.Fori(0, 3) as i:
                for k in range(KC):
                    split_lo(6 * KC, i, k)
            for k in range(KC):
                split_lo(9 * KC, 0, k)
                if k == 8:
                    root(r_m[:], ss_m[:], 1, 7, META)
            with pool.Fori(0, 3) as i:
                for k in range(KC):
                    split_lo(10 * KC, i, k)
            for c in (13, 14, 15):
                for k in range(KC):
                    split_lo(c * KC, 0, k)
                    if c == 13 and k == 9:
                        root(r_2[:], ss_1[:], NT, 8)
                    if c == 14 and k == 3:
                        root(r_kv[:], ss_kv[:], NT + 1, 9)
                    if c == 15 and k == 3:
                        root(r_cq[:], ss_cq[:], NT, 10)
            with pool.Fori(0, 3) as i:
                for k in range(KC):
                    split_lo(16 * KC, i, k)
            for k in range(Q_BASE - UQ):
                split_lo(UQ, 0, k)

            def by_rows(d, cols):
                return d[0:S, cols].rearrange("(t p) c -> p t c", p=P)

            def load_qk(A, i, head):
                buf = head % 2
                if not (A.mla and i == 0 and head < 2):
                    B, n, last = before(A, i, head)
                    pool.wait_ge(B.free, n * (4 * B.batches + NU) + (turned_by[B][last] + 1))
                q, k = (QB, 2 * VD) if A.mla else (VD, VD)
                qd, kd = (qb_d, kvb_d) if A.mla else (qa_d, kv_d)
                head += 4 * i
                pool.dma_start(nat_q[:, buf, :, 0:q], by_rows(qd, slice(head * q, (head + 1) * q))).then_inc(A.ld_qk[buf], 16)
                keys = slice(head * k, head * k + VD)
                pool.dma_start(nat_k[:, buf], by_rows(kd, keys)).then_inc(A.ld_qk[buf], 16)
                pool.dma_start(natm_k[:, buf], kd[S:KEYS, keys]).then_inc(A.ld_qk[buf], 16)

            def load_v(A, i, head):
                buf = head % 2
                if not (A.mla and i == 0 and head < 2):
                    B, n, last = before(A, i, head)
                    pool.wait_ge(B.pv, n * NU + ((last + 1) * NT + EARLY))
                kd, at_ = (kvb_d, (4 * i + head) * 2 * VD + VD) if A.mla else (kv_d, (HEADS + 4 * i + head) * VD)
                cols = slice(at_, at_ + VD)
                pool.dma_start(nat_v[:, buf], by_rows(kd, cols)).then_inc(A.ld_v[buf], 16)
                pool.dma_start(natm_v[0:META, buf], kd[S:KEYS, cols]).then_inc(A.ld_v[buf], 16)

            def before(A, i, head):
                if head >= 2:
                    return A, i, head - 2
                return (A, i - 1, head + 2) if i else (MLA, 1, head + 2)

            def turn_uses(A):
                uses = sorted([(turn_time(A, h, b), 0, h) for h in range(4) for b in range(A.batches)]
                              + [(unit_time(u) + A.turn_after, 1, u) for u in range(NU)])
                return [max(n for n, (_, kind, h) in enumerate(uses) if kind == 0 and h == head) + 1 for head in range(4)]

            turned_by = {A: turn_uses(A) for A in (MLA, DIFF)}

            def attend_loads(A, i, n0, then):
                for Q in range(4 * KC):
                    if Q % 4 == 0:
                        split_lo(n0 + i * KC, 0, Q // 4)
                    for n, head in enumerate([(A, i, 2), (A, i, 3)] + ([(*then, 0), (*then, 1)] if then else [])):
                        if Q == 12 * n + 12:
                            load_qk(*head)
                        if Q == 12 * n + 25:
                            load_v(*head)

            for signal in s_short:
                pool.wait_ge(signal, 4 * 16)
            pool.wait_ge(s_mst, 8 * 16)
            load_qk(MLA, 0, 0)
            pool.wait_ge(s_zero, 1)
            load_v(MLA, 0, 0)
            load_qk(MLA, 0, 1)
            load_v(MLA, 0, 1)
            pool.dma_start(alibi[:], a["alibi"]).then_inc(s_alibi, 16)
            attend_loads(MLA, 0, Q_BASE, (MLA, 1))
            pool.wait_ge(s_st, 4 * 16)
            attend_loads(MLA, 1, Q_BASE, (DIFF, 0))
            pool.wait_ge(s_st, 5 * 16)
            attend_loads(DIFF, 0, Q_BASE + 2 * KC, (DIFF, 1))
            attend_loads(DIFF, 1, Q_BASE + 2 * KC, None)
            for c in range(6):
                for k in range(KC):
                    split_lo(Q_BASE + 4 * KC, c, k)
                    if (c, k) == (1, 1):
                        root(r_o, ss_o, NT * 4, 11)
                    if (c, k) == (2, 0):
                        root(r_o, ss_o, NT * 4, 12)
            root(r_3[:], ss_2[:], NT, 13)

        @block.vector
        def _(dve):
            V = nc.vector

            def turn_lo(b, bank, dst, hi, gain):
                dve.wait_ge(s_turn_hi, b + 1)
                V.scalar_tensor_tensor(dst, turn[bank][:], gain, hi.bitcast(F32), ALU.mult, ALU.subtract).then_inc(s_turn_lo, 1)

            dve.sem_inc(s_turn_lo, EARLY)
            dve.sem_inc(s_m, EARLY)
            dve.sem_inc(s_o, 1)
            dve.sem_inc(s_mevac, 1)
            for A in (MLA, DIFF):
                dve.sem_inc(A.m, 1)
                dve.sem_inc(A.o, 1)
            V.memset(metaT[:].bitcast(F32), 0.0)
            V.memset(ckvmT[:].bitcast(F32), 0.0)
            V.memset(kpeT[:], 0.0)
            V.memset(ss_kv[:], 1.0)
            V.memset(rel[32:33, :], BANNED).then_inc(s_rel, 1)
            for b in range(KC):
                turn_lo(b, b % 2, setA_lo[:, b], setA_hi[:, b], gain_in[:, b:b + 1])
                if b % 3 == 0 and 0 < b < KC - 1:
                    if b == 3:
                        for j in range(4):
                            dve.wait_ge(s_x[j], 16)
                    t = b // 3 - 1
                    after(dve, V.tensor_tensor_reduce(work[:].rearrange("p t c -> p (t c)"), x_nat[:, t], x_nat[:, t], 1.0, 0.0,
                                                      ALU.mult, ALU.add, ss_x[:, t:t + 1]))
            V.tensor_scalar(ss_x[:], ss_x[:], 1.0 / D, EPS, ALU.mult, ALU.add).then_inc(s_var, 1)

            dve.wait_ge(s_small, 96)
            after(dve, V.tensor_tensor(gain_qk[:, 0], gain_qk[:, 0], gain_qk[:, 1], ALU.mult))
            after(dve, V.tensor_scalar(gain_qk[:, 0], gain_qk[:, 0], HD ** -0.5, None, ALU.mult))
            dve.wait_ge(s_evac, 8)
            k_st = stage[:, :, 0:256]
            after(dve, V.tensor_tensor(work[:, :, 0:256], k_st, k_st, ALU.mult))
            after(dve, V.tensor_reduce(ss_q[:, 0:16].rearrange("p (t h) -> p t h", t=NT),
                                       work[:, :, 0:256].rearrange("p t (h d) -> p t h d", d=HD), AX.X, ALU.add))
            V.tensor_scalar(ss_q[:, 0:16], ss_q[:, 0:16], 1.0 / HD, EPS, ALU.mult, ALU.add).then_inc(s_var, 1)
            V.tensor_copy(v_nat[:], stage[:, :, 256:512].rearrange("p t (h d) -> p t h d", d=HD)).then_inc(s_kn, 1)
            dve.wait_ge(s_root, 2)
            for t in range(NT):
                last = V.tensor_tensor(kn[:, t], stage[:, t, 0:256].rearrange("p (h d) -> p h d", d=HD),
                                       r_q[:, 4 * t:4 * t + 4].unsqueeze(2).to_broadcast([P, KVH, HD]), ALU.mult)
            last.then_inc(s_kn, 1)
            dve.wait_ge(s_kn, 2)
            for t in range(NT):
                last = V.tensor_tensor(kn[:, t], kn[:, t], gain_qk[:, 0].unsqueeze(1).to_broadcast([P, KVH, HD]), ALU.mult)
            after(dve, last)

            def soften(g, u):
                dve.wait_ge(s_score, g * UNITS + u + 1)
                if u == 0:
                    dve.wait_ge(s_bias, (g + 1) * (16 * P // SKEW))
                hp, first = u // NT, P if u % NT == 0 else 0
                V.tensor_copy(sink_p[:, u % 2], sink_g[:, 2 * hp:2 * hp + 2])
                for h in range(2):
                    head = 2 * hp + h
                    last = V.tensor_tensor_reduce(sm[:, u % 2, h, first:], sc[h][:, first:256],
                                                  bias[:, head, first:], 1.0, sink_g[:, head:head + 1],
                                                  ALU.add, ALU.max, m_w[:, u % 2, h:h + 1])
                after(dve, last)
                V.tensor_scalar(negm[:, u % 2], m_w[:, u % 2], -1.0, None, ALU.mult)
                V.tensor_tensor(sink_d[:, u % 2], sink_p[:, u % 2], m_w[:, u % 2], ALU.subtract).then_inc(s_m, 1)

            def denominators(g, u):
                dve.wait_ge(s_p, g * UNITS + u + 1)
                after(dve, V.tensor_tensor(den[:, u % 2], den[:, u % 2], sink_e[:, u % 2], ALU.add))
                after(dve, V.reciprocal(rden[:, u % 2], den[:, u % 2]))

            def keep_o(g, u):
                dve.wait_ge(s_pv, g * UNITS + u + 1 + EARLY)
                hp, j = u // NT, u % NT
                dst = o_nat[:, bass.ds(g, 1), j, hp * P:(hp + 1) * P].rearrange("p o (h d) -> p (o h) d", h=2)
                V.tensor_tensor(dst, o_ps[:, 0:P].rearrange("p (h d) -> p h d", h=2),
                                rden[:, u % 2].unsqueeze(2).to_broadcast([P, 2, HD]), ALU.mult).then_inc(s_o, 1)

            BODY = 3 + UNITS * 3
            start = link.n
            with dve.Fori(0, 4) as g:
                link.base, link.n = g * BODY + start, 0
                for H in range(32):
                    if H == 0:
                        dve.wait_ge(s_evac, 4 * g + 12)
                        after(dve, V.tensor_tensor(work[:], stage[:], stage[:], ALU.mult))
                        after(dve, V.tensor_reduce(ss_q[:].rearrange("p (t h) -> p t h", t=NT),
                                                   work[:].rearrange("p t (h d) -> p t h d", d=HD), AX.X, ALU.add))
                        V.tensor_scalar(ss_q[:], ss_q[:], 1.0 / HD, EPS, ALU.mult, ALU.add).then_inc(s_var, 1)
                        for h in range(2):
                            last = V.tensor_copy(k_twice[:, :, h:h + 1], kn[:, :, bass.ds(g, 1)])
                        last.then_inc(s_kdup, 1)
                        V.tensor_copy(vg[:].unsqueeze(2), v_nat[:, :, bass.ds(g, 1)])
                        after(dve, V.tensor_copy(sink_g[:], sinks[:, bass.ds(g * GROUP, GROUP)]))
                    if H == 4:
                        dve.wait_ge(s_root, g + 3)
                        for t in range(NT):
                            st = stage[:, t].rearrange("p (h d) -> p h d", d=HD)
                            last = V.tensor_tensor(st, st, r_q[:, 8 * t:8 * t + 8].unsqueeze(2).to_broadcast([P, GROUP, HD]), ALU.mult)
                        last.then_inc(s_qn, 1)
                    if 0 <= H - 16 < UNITS:
                        keep_o(g, H - 16)
                    if 0 <= H - 14 < UNITS:
                        denominators(g, H - 14)
                    if 0 <= H - 12 < UNITS:
                        soften(g, H - 12)
                n_body = link.n
            assert n_body == BODY
            link.base, link.n = 0, start + 4 * BODY

            def gate(g, o_g):
                dve.wait_ge(s_silu, g + 1)
                after(dve, V.tensor_scalar(work[:], work[:], 1.0, None, ALU.add))
                after(dve, V.reciprocal(work[:], work[:]))
                after(dve, V.tensor_tensor(stage[:], stage[:], work[:], ALU.mult))
                V.tensor_tensor(stage[:], stage[:], o_g, ALU.mult).then_inc(s_og, 1)

            start2 = link.n
            with dve.Fori(0, 3) as i:
                link.base, link.n = i * 3 + start2, 0
                gate(i, o_nat[:, bass.ds(i, 1)].rearrange("p o t c -> p (o t) c"))
                for f in range(4):
                    slot = bass.ds(i * 4 + f, 1)
                    turn_lo(i * 4 + (16 + f), f % 2, setB_lo[:, slot].rearrange("p o s -> p (o s)"),
                            setB_hi[:, slot].rearrange("p o s -> p (o s)"), 1.0)
            link.base, link.n = 0, start2 + 9
            gate(3, o_nat[:, 3])
            for f in range(4):
                turn_lo(28 + f, f % 2, setB_lo[:, 12 + f], setB_hi[:, 12 + f], 1.0)
            dve.wait_ge(s_meta_in, 16)
            after(dve, V.tensor_tensor_reduce(meta_sq[:], meta_nat[:], meta_nat[:], 1.0, 0.0, ALU.mult, ALU.add, ss_m[:]))
            V.tensor_scalar(ss_m[:], ss_m[:], 1.0 / D, EPS, ALU.mult, ALU.add).then_inc(s_var, 1)
            dve.wait_ge(s_mturn, 1)
            dve.wait_ge(s_small, 112)
            V.tensor_tensor(meta_f[:], sc[1][:, 0:KC * META].rearrange("p (k m) -> p k m", k=KC),
                            gain_2[:].unsqueeze(2).to_broadcast([P, KC, META]), ALU.mult).then_inc(s_metaF, 1)
            dve.wait_ge(s_metaH, 1)
            V.tensor_tensor(metaT[:, :, 32:32 + META], meta_f[:], metaT[:, :, 0:META].bitcast(F32),
                            ALU.subtract).then_inc(s_metaT, 1)
            def residual(c):
                dve.wait_ge(s_evac, 4 * c + 44)
                dve.wait_ge(s_xin, 16 * c + 16)
                after(dve, V.tensor_tensor(stage[:], stage[:], x_in[:], ALU.add))
                for t in range(NT):
                    last = V.tensor_tensor_reduce(x_in[:, t], stage[:, t], stage[:, t], 1.0, 0.0,
                                                  ALU.mult, ALU.add, ss_c[:, t:t + 1])
                last.then_inc(s_x1, 1)
                dve.wait_ge(s_x1, c + 1)
                after(dve, V.tensor_tensor(ss_1[:], ss_1[:], ss_c[:], ALU.add))
                if isinstance(c, int):
                    last = V.tensor_copy(gain_c[:], gain_2[:, 4 * c:4 * c + 4])
                else:
                    last = V.tensor_copy(gain_c[:], gain_2[:, bass.ds(c * 4, 4)])
                last.then_inc(s_gain_c, 1)
                dve.wait_ge(s_gain_c, c + 1)

            def x1_lo(c):
                for f in range(4):
                    if isinstance(c, int):
                        lo, hi = setA_lo[:, 4 * c + f], setA_hi[:, 4 * c + f]
                    else:
                        lo, hi = (s_[:, bass.ds(c * 4 + f, 1)].rearrange("p o s -> p (o s)") for s_ in (setA_lo, setA_hi))
                    turn_lo(c * 4 + (32 + f), f % 2, lo, hi, gain_c[:, f:f + 1])

            after(dve, V.memset(ss_1[:], 0.0))
            start3 = link.n
            with dve.Fori(0, 3) as i:
                link.base, link.n = i * 2 + start3, 0
                residual(i)
                x1_lo(i)
            link.base, link.n = 0, start3 + 6
            residual(3)
            V.tensor_scalar(ss_1[:], ss_1[:], 1.0 / D, EPS, ALU.mult, ALU.add).then_inc(s_var, 1)
            x1_lo(3)

            def keep_meta(m, r, cols=CW, stores=0):
                dve.wait_ge(s_mtmp, m + 1)
                V.tensor_tensor(sum_m[:, 0:cols], sc[0][0:META, 0:cols], tmp_m[:, 0:cols], ALU.add).then_inc(s_mevac, 1)
                dve.wait_ge(s_mevac, m + 2)
                dve.wait_ge(s_mst, stores * 16)
                V.tensor_scalar(stage_m[:, 0:cols], sum_m[:, 0:cols], r, None, ALU.mult).then_inc(s_mstage, 1)

            def rotate(dst, src, c, s_, tmp):
                x1, x2_ = src
                V.tensor_tensor(tmp[0], x1, c, ALU.mult)
                V.tensor_tensor(tmp[1], x2_, s_, ALU.mult)
                V.tensor_tensor(tmp[2], x1, s_, ALU.mult)
                after(dve, V.tensor_tensor(tmp[3], x2_, c, ALU.mult))
                V.tensor_tensor(dst[0], tmp[0], tmp[1], ALU.subtract)
                return V.tensor_tensor(dst[1], tmp[2], tmp[3], ALU.add)

            HR = ROPE // 2
            keep_meta(0, r_m[:, 0:1], 320)
            dve.wait_ge(s_mstage, 1)
            dve.wait_ge(s_evac, 4 * 13 + 8)
            for t in range(NT):
                V.tensor_tensor_reduce(work[:, t, 0:CKV], stage[:, t, 0:CKV], stage[:, t, 0:CKV], 1.0, 0.0,
                                       ALU.mult, ALU.add, ss_kv[:, t:t + 1])
            after(dve, V.tensor_tensor_reduce(sum_m[:, 0:CKV], stage_m[:, 0:CKV], stage_m[:, 0:CKV], 1.0, 0.0,
                                              ALU.mult, ALU.add, ss_kv[0:META, NT:NT + 1]))
            V.tensor_scalar(ss_kv[:], ss_kv[:], 1.0 / CKV, EPS, ALU.mult, ALU.add).then_inc(s_var, 1)
            dve.wait_ge(s_small2, 9 * 16)
            rotate((kpe[:, :, 0:HR], kpe[:, :, HR:ROPE]), (stage[:, :, CKV:CKV + HR], stage[:, :, CKV + HR:CKV + ROPE]),
                   cos[:], sin[:], [rope_t[:, n] for n in range(4)])
            after(dve, V.tensor_scalar(subln[:], subln[:], 1.0 - LAM0, None, ALU.mult))
            rotate((kpe_m[:, 0:HR], kpe_m[:, HR:ROPE]), (stage_m[:, CKV:CKV + HR], stage_m[:, CKV + HR:CKV + ROPE]),
                   cos_m[:], sin_m[:], [rope_t[0:META, n, 0] for n in range(4)]).then_inc(s_kpe, 1)
            dve.wait_ge(s_lam, 16)
            for n in range(2):
                last = V.tensor_tensor_reduce(work[:, n, 0:QKD], lam_in[:, 2 * n], lam_in[:, 2 * n + 1], 1.0, 0.0,
                                              ALU.mult, ALU.add, lam_s[:, n:n + 1])
            last.then_inc(s_lam, 1)
            for f in range(2):
                if f == 0:
                    dve.wait_ge(s_kpeT, 2)
                last = V.scalar_tensor_tensor(ckvmT[:, f, 32:32 + META], sc[0][:, (f + 1) * META:(f + 2) * META],
                                              gain_ckv[:, f:f + 1], ckvmT[:, f, 0:META].bitcast(F32), ALU.mult, ALU.subtract)
                last.then_inc(s_ckvm, 1)
            for f in range(2):
                turn_lo(48 + f, f % 2, ckvT_lo[:, f], ckvT_hi[:, f], gain_ckv[:, f:f + 1])
            dve.wait_ge(s_lam, 18)
            after(dve, V.tensor_tensor(neglam[:], lam_s[:, 1:2], lam_s[:, 0:1], ALU.subtract))
            V.tensor_scalar(neglam[:], neglam[:], LAM0, None, ALU.subtract)
            dve.wait_ge(s_evac, 4 * 14 + 8)
            for t in range(NT):
                last = V.tensor_tensor_reduce(work[:, t], stage[:, t], stage[:, t], 1.0, 0.0, ALU.mult, ALU.add, ss_cq[:, t:t + 1])
            after(dve, last)
            V.tensor_scalar(ss_cq[:], ss_cq[:], 1.0 / CQ, EPS, ALU.mult, ALU.add).then_inc(s_var, 1)
            for f in range(4):
                turn_lo(50 + f, f % 2, cqT_lo[:, f], cqT_hi[:, f], gain_cq[:, f:f + 1])
            for m in range(1, 9):
                keep_meta(m, r_m[:, 0:1] if m < 5 else r_kv[0:META, NT:NT + 1], stores=m - 1)

            dve.wait_ge(s_used, Q_BASE + 4)
            V.memset(qpT[:], 0.0)
            V.memset(natm_v[:], 0.0)
            dve.wait_ge(s_short[0], 4 * 16)
            after(dve, V.memset(pTm[:], 0.0))
            V.memset(tick[:], 0.0).then_inc(s_zero, 1)

            def soften2(A, i, u, comp):
                j = u % NT
                lo, slot = S - (j + 1) * P, u % 2 if A.mla else comp
                dve.wait_ge(A.score, i * NU * A.comps + (u * A.comps + comp + 1))
                V.memset(tick[:], 0.0)
                add = mask[:, lo:] if A.mla else alibi_h[:, ALIBI_AT[j]:ALIBI_AT[j + 1]]
                after(dve, V.tensor_tensor_reduce(sm2[:, slot, lo:], sc2[:, lo:KEYS], add, 1.0, FLOOR, ALU.add, ALU.max,
                                                  m_2[:, u % 2, comp:comp + 1]))
                V.tensor_scalar(negm_2[:, u % 2, comp:comp + 1], m_2[:, u % 2, comp:comp + 1], -1.0, None, ALU.mult).then_inc(A.m, 1)

            def combine(A, i, u):
                b, lo = u % 2, S - (u % NT + 1) * P
                dve.wait_ge(A.p, i * NU * A.comps + (u + 1) * A.comps)
                after(dve, V.reciprocal(rden_2[:, b, 0:A.comps], den_2[:, b, 0:A.comps]))
                if not A.mla:
                    after(dve, V.scalar_tensor_tensor(coef[:, b:b + 1], den_2[:, b, 0:1], neglam[:, 0:1], rden_2[:, b, 1:2],
                                                      ALU.mult, ALU.mult))
                    V.scalar_tensor_tensor(p2[:, b, 0, lo:], p2[:, b, 1, lo:], coef[:, b:b + 1], p2[:, b, 0, lo:],
                                           ALU.mult, ALU.add).then_inc(A.w, 1)

            def keep_o2(A, i, u):
                head, j = u // NT, u % NT
                dve.wait_ge(A.pv, i * NU + (u + 1 + EARLY))
                dst = o_nat[:, bass.ds(i + (2 if A.mla else 0), 1), j, head * VD:(head + 1) * VD].rearrange("p o c -> p (o c)")
                V.tensor_scalar(dst, turn[1][:, 2 * P:3 * P], rden_2[:, u % 2, 0:1], None, ALU.mult).then_inc(A.o, 1)

            def attend_body(A, i):
                for Q in range(4 * KC):
                    for u in range(NU):
                        if Q == unit_time(u) + A.values_after:
                            keep_o2(A, i, u)
                    for u in range(NU):
                        if Q == unit_time(u) + 2:
                            combine(A, i, u)
                    if not A.mla and Q == 4:
                        after(dve, V.tensor_copy(slope_i[:], slopes[:, bass.ds(i * 4, 4)]))
                    for head in range(4):
                        if A.mla and Q == max(12 * head, 4):
                            buf = head % 2
                            dve.wait_ge(MLA.ld_qk[buf], (i * 2 + (head // 2 + 1)) * 48)
                            x1, x2_ = nat_q[:, buf, :, VD:VD + HR], nat_q[:, buf, :, VD + HR:QB]
                            rotate((x1, x2_), (x1, x2_), cos[:], sin[:], [rope_t[:, n] for n in range(4)]).then_inc(MLA.rope, 1)
                            dve.wait_ge(MLA.rope, i * 4 + (head + 1))
                        if not A.mla and Q == unit_time(4 * head) - 1:
                            after(dve, V.tensor_scalar(alibi_h[:], alibi[:], slope_i[:, head:head + 1], None, ALU.mult))
                    for u in range(NU):
                        for comp in range(A.comps):
                            if Q == unit_time(u) + comp:
                                soften2(A, i, u, comp)

            for A, body in ((MLA, 4 + 2 * NU), (DIFF, 1 + 4 + NU * 4)):
                if A is DIFF:
                    dve.wait_ge(s_alibi, 16)
                first = link.n
                with dve.Fori(0, 2) as i:
                    link.base, link.n = i * body + first, 0
                    attend_body(A, i)
                    assert link.n == body, (link.n, body)
                link.base, link.n = 0, first + 2 * body

            def sub_norm(c, root):
                o = o_nat[:, c].rearrange("p t (h d) -> p t h d", d=VD)
                after(dve, V.tensor_tensor(o_sq[:], o_nat[:, c], o_nat[:, c], ALU.mult))
                after(dve, V.tensor_reduce(ss_o.rearrange("p (t h) -> p t h", t=NT),
                                           o_sq[:].rearrange("p t (h d) -> p t h d", d=VD), AX.X, ALU.add))
                V.tensor_scalar(ss_o, ss_o, 1.0 / VD, EPS, ALU.mult, ALU.add).then_inc(s_var, 1)
                dve.wait_ge(s_root, root)
                for t in range(NT):
                    last = V.tensor_tensor(o[:, t], o[:, t], r_o[:, 4 * t:4 * t + 4].unsqueeze(2).to_broadcast([P, 4, VD]), ALU.mult)
                after(dve, last)
                for t in range(NT):
                    last = V.tensor_tensor(o[:, t], o[:, t], subln[:].unsqueeze(1).to_broadcast([P, 4, VD]), ALU.mult)
                after(dve, last)

            def gated_lo(b, kc):
                for f in range(4):
                    turn_lo(b + f, f % 2, setB_lo[:, kc + f], setB_hi[:, kc + f], 1.0)

            gate(4, o_nat[:, 2])
            gated_lo(54, 8)
            gate(5, o_nat[:, 3])
            gated_lo(58, 12)
            sub_norm(0, 11)
            gate(6, o_nat[:, 0])
            gated_lo(62, 0)
            sub_norm(1, 12)
            gate(7, o_nat[:, 1])
            gated_lo(66, 4)

            def residual2(c):
                dst = h2[:, c] if isinstance(c, int) else h2[:, bass.ds(c, 1)].rearrange("p o t c -> p (o t) c")
                dve.wait_ge(s_evac, 4 * c + (4 * 32 + 8))
                dve.wait_ge(s_x1in, 16 * c + 16)
                after(dve, V.tensor_tensor(stage[:], stage[:], x_in[:], ALU.add))
                for t in range(NT):
                    V.tensor_tensor_reduce(x_in[:, t], stage[:, t], stage[:, t], 1.0, 0.0, ALU.mult, ALU.add, ss_c[:, t:t + 1])
                V.tensor_copy(dst, stage[:]).then_inc(s_h2, 1)
                dve.wait_ge(s_h2, c + 1)
                after(dve, V.tensor_tensor(ss_2[:], ss_2[:], ss_c[:], ALU.add))

            after(dve, V.memset(ss_2[:], 0.0))
            first = link.n
            with dve.Fori(0, 3) as i:
                link.base, link.n = i * 2 + first, 0
                residual2(i)
            link.base, link.n = 0, first + 6
            residual2(3)
            V.tensor_scalar(ss_2[:], ss_2[:], 1.0 / D, EPS, ALU.mult, ALU.add).then_inc(s_var, 1)
            dve.wait_ge(s_root, 13)
            dve.wait_ge(s_fin_w, 16)
            for c in range(4):
                for t in range(NT):
                    last = V.scalar_tensor_tensor(h2[:, c, t], h2[:, c, t], r_3[:, t:t + 1], w_final[:, c * CW:(c + 1) * CW],
                                                  ALU.mult, ALU.mult)
                last.then_inc(s_fin, 1)


_BY_PARTITION = ["swa_norm", "attn_norm_w", "mla_q_norm_w", "mla_kv_norm_w"]
_INS = ["x", "rel_bias", "swa_norm", "swa_w_in", "swa_q_gain", "swa_k_gain", "swa_sinks", "swa_w_out", "meta_tokens_2",
        "attn_norm_w_2", "w_in_2", "diff_lambda_2", "diff_subln_w_2", "mla_q_norm_w_2", "w_uq_2", "mla_kv_norm_w_2",
        "w_ukv_2", "w_out_2", "final_norm_w_2"]


def kernel(**inputs):
    import numpy as _np
    import concourse.bacc as _bacc
    from concourse import mybir as _mybir
    from concourse.bass_utils import run_bass_kernel_spmd as _run

    nc = _bacc.Bacc("TRN2", target_bir_lowering=False, num_devices=1)
    arrays, args = {}, {}

    def give(name, v):
        arrays[f"in_{name}"] = v
        args[name] = nc.dram_tensor(f"in_{name}", v.shape, _mybir.dt.float32, kind="ExternalInput").ap()

    for name in _INS:
        v = _np.ascontiguousarray(inputs[name])
        name = name.removesuffix("_2")
        v = v[0] if v.shape[0] == 1 else v
        give(name, _np.ascontiguousarray(v.reshape(-1, P).T) if name in _BY_PARTITION else v)
    give("t5_marks", t5_onehot())
    for name, v in zip(("cos", "cos_m", "sin", "sin_m"), rotations()):
        give(name, v)
    give("mask", causal_mask())
    give("alibi", alibi_distance())
    give("slopes", _np.tile(_np.exp2(-8.0 * _np.arange(1, HEADS + 1) / HEADS).astype(_np.float32), (P, 1)))
    out = nc.dram_tensor("out0", (S, D), _mybir.dt.float32, kind="ExternalOutput").ap()
    build(nc, args, out)
    r = _run(nc, [arrays], core_ids=[0])
    return r.results[0]["out0"].reshape(1, S, D)
```

```python
from contextlib import ExitStack
import math

import numpy as np
import concourse.bass as bass
from concourse import mybir

F32 = mybir.dt.float32
F32R = mybir.dt.float32r
ALU = mybir.AluOpType
ACT = mybir.ActivationFunctionType
AX = mybir.AxisListType

P = 128
D = 2048
S = 512
NT = S // P
KC = D // P
CW = 512
EPS = 1e-6
AHEAD = 3
HD = 64
KVH = 4
GROUP = 8
SKEW = 32
BIAS_W = 384
BANNED = -1e30
UNITS = (GROUP // 2) * NT
X_AT = [0, 256, 512, 1024, 1536, 2048]
EARLY = 2

BANK_CUT = 272
META = 16
KEYS = S + META
HEADS = 8
QKD = 64
VD = 128
ROPE = 64
QB = VD + ROPE
CKV = 256
CQ = 512
FULL = 96
LAM0 = 0.8 - 0.6 * math.exp(-0.3 * 0)
CEILING = 3.0e38
A_SCALE = QKD ** -0.5
B_SCALE = QB ** -0.5
NU = 16
ORDER = [0, 1, 2, 3, 8, 9, 10, 11, 12, 13, 14, 15, 4, 5, 6, 7]


def width(j):
    return (j + 1) * P + META


ALIBI_AT = [sum(width(i) for i in range(j)) for j in range(NT + 1)]


def alibi_distance():
    q = np.arange(P)[:, None]
    tiles = []
    for j in range(NT):
        rel = P * j + q - np.arange((j + 1) * P)[None, :]
        far = np.where(rel >= 0, -rel.astype(np.float32), np.float32(BANNED * 1e4))
        tiles += [-(META + P * j + q - np.arange(META)[None, :]).astype(np.float32), far]
    return np.concatenate(tiles, 1).astype(np.float32)


def causal_mask():
    mask = np.zeros((P, KEYS), np.float32)
    mask[:, KEYS - P:] = np.where(np.arange(P)[None, :] > np.arange(P)[:, None], BANNED, 0.0)
    return mask


def rotations():
    freq = np.float32(10000.0) ** (-np.arange(ROPE // 2, dtype=np.float32) / np.float32(ROPE // 2))
    angle = np.arange(KEYS, dtype=np.float32)[:, None] * freq[None, :]
    out = []
    for f in (np.cos(angle), np.sin(angle)):
        out.append(np.ascontiguousarray(f[META:].reshape(NT, P, ROPE // 2).transpose(1, 0, 2).reshape(P, -1)))
        out.append(np.ascontiguousarray(f[:META]))
    return out


def t5_onehot():
    dist = 255 - np.arange(BIAS_W)
    inside = (dist >= 0) & (dist < 128)
    near = np.maximum(dist, 1).astype(np.float32)
    large = 16 + (np.log(near / np.float32(16)) / np.float32(math.log(8.0)) * np.float32(16)).astype(np.int32)
    bucket = np.where(dist < 16, dist, np.minimum(large, 31))
    marks = np.zeros((33, BIAS_W), np.float32)
    marks[bucket[inside], np.nonzero(inside)[0]] = 1.0
    marks[32, ~inside] = 1.0
    return marks


def build(nc, a, out):
    with ExitStack() as ctx:
        at = [nc.sbuf_base + (-nc.sbuf_base) % 64]

        def place(name, shape, dt=F32, offset=None):
            size = 4
            for n in shape[1:]:
                size *= n
            if offset is None:
                offset = at[0]
                at[0] += size + (-size) % 32
            return nc.alloc_sbuf_tensor_at(name, shape, dt, offset=offset), offset

        def sb(name, shape, dt=F32):
            return place(name, shape, dt)[0]

        def over(name, shape, offset, dt=F32):
            return place(name, shape, dt, offset)[0]

        def sem(name):
            return ctx.enter_context(nc.semaphore(name))

        setA_hi, SETA = place("setA_hi", [P, KC, S], F32R)
        setA_lo = sb("setA_lo", [P, KC, S], F32R)
        setB_hi, B_HI = place("setB_hi", [P, KC, S], F32R)
        setB_lo, B_LO = place("setB_lo", [P, KC, S], F32R)
        x_nat = over("x_nat", [P, NT, D], B_HI)
        o_nat = over("o_nat", [P, 4, NT, CW], B_LO)
        bias = over("bias", [P, GROUP, 256], B_HI)
        qT_a = over("qT_a", [P, GROUP // 2, S], B_HI + 16384, F32R)
        kT_hi = over("kT_hi", [P, S], B_HI + 24576, F32R)
        k_twice = over("k_twice", [P, NT, 2, HD], B_HI + 26624)
        kT_lo = over("kT_lo", [P, S], B_HI + 26624, F32R)
        sm = over("sm", [P, 2, 2, 256], B_HI + 28672)
        w_raw = sb("w_raw", [P, 2, 4, CW])
        w_hi = sb("w_hi", [P, 4, CW], F32R)
        w_lo = sb("w_lo", [P, 4, CW], F32R)
        stage = sb("stage", [P, NT, CW])
        work, WORK = place("work", [P, NT, CW])
        x_in = over("x_in", [P, NT, CW], WORK)
        qT_b = over("qT_b", [P, GROUP // 2, S], WORK, F32R)
        ident = sb("ident", [P, P])
        kn, MISC = place("kn", [P, NT, KVH, HD])
        v_nat = sb("v_nat", [P, NT, KVH, HD])
        vg = sb("vg", [P, NT, HD])
        p_w, P_W = place("p_w", [P, 2, 2, 256])
        pT = sb("pT", [P, 2, 4, P])
        gain_in = sb("gain_in", [P, KC])
        gain_qk = over("gain_qk", [P, 2, HD], B_LO + 4096)
        sinks = sb("sinks", [P, KVH * GROUP])
        sink_g = sb("sink_g", [P, GROUP])
        rel = over("rel", [33, KVH * GROUP], B_LO + 5120)
        marks = over("marks", [33, BIAS_W], B_LO)
        bias_row = over("bias_row", [KVH * GROUP, BIAS_W], B_LO + 2048)
        half = sb("half", [P, 32])
        ss_x = sb("ss_x", [P, NT])
        r_x = sb("r_x", [P, NT])
        ss_q = sb("ss_q", [P, 32])
        r_q = sb("r_q", [P, 32])
        negm = sb("negm", [P, 2, 2])
        sink_p = sb("sink_p", [P, 2, 2])
        sink_d = sb("sink_d", [P, 2, 2])
        sink_e = sb("sink_e", [P, 2, 2])
        den = sb("den", [P, 2, 2])
        rden = sb("rden", [P, 2, 2])
        ss_1 = sb("ss_1", [P, NT])
        ss_c = sb("ss_c", [P, NT])
        gain_2 = sb("gain_2", [P, KC])
        gain_c = sb("gain_c", [P, 4])

        mask, MASK = place("mask", [P, KEYS])

        meta_nat = over("meta_nat", [META, D], P_W)
        meta_sq = over("meta_sq", [META, D], MISC)
        sm2 = over("sm2", [P, 2, KEYS], MISC)
        p2 = over("p2", [P, 2, 2, KEYS], MISC + 4224)
        o_sq = over("o_sq", [P, NT, CW], MISC + 4224)
        diff_km = over("diff_km", [META, HEADS * VD], MASK + 4 * KEYS)
        diff_kmT = over("diff_kmT", [P, HEADS * META], B_HI + 32128)
        natm_k = over("natm_k", [META, 2, VD], MISC + 12672)
        natm_v = over("natm_v", [P, 2, VD], MISC + 13696)
        stage_m = over("stage_m", [META, CW], MISC + 14720)
        cqT_hi = over("cqT_hi", [P, 4, S], B_HI, F32R)
        cqT_lo = over("cqT_lo", [P, 4, S], B_HI + 8192, F32R)
        ckvT_hi = over("ckvT_hi", [P, 2, S], B_HI + 16384, F32R)
        ckvT_lo = over("ckvT_lo", [P, 2, S], B_HI + 20480, F32R)
        kpe = over("kpe", [P, NT, ROPE], B_HI + 24576)
        kpe_m = over("kpe_m", [META, ROPE], B_HI + 25600)
        tmp_m = over("tmp_m", [META, CW], B_HI + 25856)
        sum_m = over("sum_m", [META, CW], B_HI + 27904)
        nat_q = over("nat_q", [P, 2, NT, QB], B_HI)
        gate_0 = over("gate_0", [P, NT, CW], B_HI)
        nat_k = over("nat_k", [P, 2, NT, VD], B_HI + 6144)
        nat_v = over("nat_v", [P, 2, NT, VD], B_HI + 10240)
        qnT = over("qnT", [P, 2, S], B_HI + 14336)
        qpT = over("qpT", [P, 2, S], B_HI + 18432, F32R)
        knT = over("knT", [P, 2, KEYS], B_HI + 22528)
        alibi = over("alibi", [P, ALIBI_AT[NT]], B_HI + 26752)
        kpeT_lo = over("kpeT_lo", [P, KEYS], B_HI + 29952, F32R)
        pT2 = over("pT2", [P, 2, S], WORK)
        pTm = over("pTm", [P, 2, P], WORK + 4096)
        rope_t = over("rope_t", [P, 4, NT, ROPE // 2], WORK + 5120)
        metaT = sb("metaT", [P, KC, FULL], F32R)
        alibi_h = over("alibi_h", [P, 2, ALIBI_AT[NT]], MASK)
        ckvmT = sb("ckvmT", [P, 2, FULL], F32R)
        kpeT_hi = sb("kpeT_hi", [P, KEYS], F32R)
        cos = sb("cos", [P, NT, ROPE // 2])
        sin = sb("sin", [P, NT, ROPE // 2])
        cos_m = sb("cos_m", [META, ROPE // 2])
        sin_m, SIN_M = place("sin_m", [META, ROPE // 2])
        assert MASK + 2 * 4 * ALIBI_AT[NT] <= SIN_M
        gain_cq = sb("gain_cq", [P, 4])
        gain_ckv = sb("gain_ckv", [P, 2])
        subln = sb("subln", [P, VD])
        meta_f = over("meta_f", [P, KC, META], MISC + 8192)
        lam_in = over("lam_in", [P, 4, QKD], MISC + 8192)
        lam_s = sb("lam_s", [P, 2])
        neglam = sb("neglam", [P, 1])
        slopes = sb("slopes", [P, HEADS])
        ss_m, r_m = sb("ss_m", [META, 1]), sb("r_m", [META, 1])
        r_2 = sb("r_2", [P, NT])
        tick = sb("tick", [P, 4])
        ss_kv, r_kv = sb("ss_kv", [P, NT + 1]), sb("r_kv", [P, NT + 1])
        ss_cq, r_cq = sb("ss_cq", [P, NT]), sb("r_cq", [P, NT])
        negm_2 = sb("negm_2", [P, 2, 2])
        den_2, rden_2 = sb("den_2", [P, 2, 2]), sb("rden_2", [P, 2, 2])
        coef = sb("coef", [P, 2])
        ss_o, r_o = ss_q[:, 0:NT * 4], r_q[:, 0:NT * 4]
        ss_2, r_3 = sb("ss_2", [P, NT]), sb("r_3", [P, NT])
        h2 = over("h2", [P, 4, NT, CW], SETA)
        w_final = over("w_final", [P, D], SETA + 32768)

        acc = [ctx.enter_context(nc.psum_tensor(f"acc{t}", [P, CW], F32)) for t in range(NT)]
        sc2 = ctx.enter_context(nc.psum_tensor("sc2", [P, 2 * CW], F32))
        sc = [sc2[:, 0:CW], sc2[:, CW:2 * CW]]
        turn = [ctx.enter_context(nc.psum_tensor(f"turn{t}", [P, CW], F32)) for t in range(2)]
        o_ps = turn[1]

        x1_d = nc.dram_tensor("x1_d", (S, D), F32).ap()
        kv_d = nc.dram_tensor("kv_d", (KEYS, D), F32).ap()
        qa_d = nc.dram_tensor("qa_d", (S, HEADS * VD), F32).ap()
        qb_d = nc.dram_tensor("qb_d", (S, HEADS * QB), F32).ap()
        kvb_d = nc.dram_tensor("kvb_d", (KEYS, D), F32).ap()
        gate_d = nc.dram_tensor("gate_d", (S, CW), F32).ap()
        row_d = nc.dram_tensor("row_d", (KVH * GROUP, SKEW + 1, BIAS_W), F32).ap()

        s_raw = [sem(f"s_raw{i}") for i in range(2)]
        s_raw_2nd = [sem(f"s_raw_2nd{i}") for i in range(2)]
        s_hi, s_lo, s_used = sem("s_hi"), sem("s_lo"), sem("s_used")
        s_acc, s_evac = sem("s_acc"), sem("s_evac")
        s_turned, s_turn_hi, s_turn_lo = sem("s_turned"), sem("s_turn_hi"), sem("s_turn_lo")
        s_x = [sem(f"s_x_in{j}") for j in range(len(X_AT) - 1)]
        s_small, s_ident = sem("s_small"), sem("s_ident")
        s_half, s_rel = sem("s_half"), sem("s_rel")
        s_row_ps, s_row, s_row_d = sem("s_row_ps"), sem("s_row"), sem("s_row_d")
        s_bias = sem("s_bias")
        s_var, s_root = sem("s_var"), sem("s_root")
        ROOT_X, ROOT_K, ROOT_Q, ROOT_M, ROOT_2, ROOT_KV, ROOT_CQ, ROOT_O, ROOT_3 = 1, 2, 3, 11, 12, 13, 14, 15, 17
        s_d = sem("s_d")
        s_kn, s_qn, s_kdup = sem("s_kn"), sem("s_qn"), sem("s_kdup")
        s_qturn, s_qhi, s_qT = sem("s_qturn"), sem("s_qhi"), sem("s_qT")
        s_score, s_m, s_p = sem("s_score"), sem("s_m"), sem("s_p")
        s_tr, s_pT, s_pv, s_o = sem("s_tr"), sem("s_pT"), sem("s_pv"), sem("s_o")
        s_silu, s_og = sem("s_silu"), sem("s_og")
        s_xin, s_x1, s_x1d, s_gain_c = sem("s_xin"), sem("s_x1"), sem("s_x1d"), sem("s_gain_c")
        s_small2, s_out = sem("s_small2"), sem("s_out")
        s_meta_in, s_mturn, s_metaF, s_metaH, s_metaT = (sem("s_" + n) for n in ("meta_in", "mturn", "metaF", "metaH", "metaT"))
        s_meta, s_mtmp, s_mevac, s_mstage, s_mst = (sem("s_" + n) for n in ("meta", "mtmp", "mevac", "mstage", "mst"))
        s_kpe, s_kpe_ps, s_kpeT, s_ckvm = sem("s_kpe"), sem("s_kpe_ps"), sem("s_kpeT"), sem("s_ckvm")
        s_short = [sem(f"s_short{i}") for i in range(2)]
        s_st, s_gld, s_zero = sem("s_st"), sem("s_gld"), sem("s_zero")
        s_lam, s_alibi, s_fin_w, s_x1in, s_h2, s_fin = (sem("s_" + n) for n in ("lam", "alibi", "fin_w", "x1in", "h2", "fin"))
        s_qp_hi = sem("s_qp_hi")
        s_km_in, s_km_ps, s_km = sem("s_km_in"), sem("s_km_ps"), sem("s_km")
        s_sum, s_sq, s_fin_last = sem("s_sum"), sem("s_sq"), sem("s_fin_last")

        class Attend:

            def __init__(self, kind):
                self.mla = kind == "mla"
                self.comps = 1 if self.mla else 2
                self.batches = 3 if self.mla else 2
                self.turn_after, self.values_after = (3, 5) if self.mla else (4, 6)
                self.ld_qk = [sem(f"s_{kind}_ld_qk{i}") for i in range(2)]
                self.ld_v = [sem(f"s_{kind}_ld_v{i}") for i in range(2)]
                (self.rope, self.full, self.free, self.score, self.m, self.p, self.w, self.pv, self.o, self.slope) = (
                    sem(f"s_{kind}_{n}") for n in ("rope", "full", "free", "score", "m", "p", "w", "pv", "o", "slope"))

        MLA, DIFF = Attend("mla"), Attend("diff")

        class Link:
            base, n = 0, 0

        link = Link()

        def after(eng, ins):
            link.n += 1
            ins.then_inc(s_d, 1)
            eng.wait_ge(s_d, link.base + link.n)

        x2 = a["x"]

        def unit_time(u):
            return 12 + 3 * u

        def turn_time(A, head, b):
            if head == 0:
                return 6 + b
            return 12 * head + ((2, 5, 7)[b] if A.mla else (5, 8)[b])

        def score_at(A, u, comp):
            return CW - BANK_CUT if u % NT == NT - 1 else CW * (u % NT % 2 if A.mla else comp)

        def head_T(b, h):
            head = 2 * (b - 1) + h
            return (qT_a, qT_b)[head // 4][:, head % 4]

        block = ctx.enter_context(nc.Block())

        @block.sync
        def _(sp):
            w_in = a["swa_w_in"].rearrange("(q k p) c -> p q k c", p=P, k=4)
            w_out = a["swa_w_out"].rearrange("(q k p) c -> p q k c", p=P, k=4)

            def small(dst, src):
                sp.dma_start(dst, src).then_inc(s_small, 16)

            def load_chunk(w, col, q0, quads=(0, 1, 2, 3), odd=0):
                for q, rows in enumerate(quads):
                    col_ = sp.snap(col) if not isinstance(col, int) else col
                    sp.wait_ge(s_lo, 4 * (q0 + q) + 4)
                    sp.dma_start(w_raw[:, (q + odd) % 2], w[:, rows, :, bass.ds(col_, CW)]).then_inc(s_raw[(q + odd) % 2], 16)

            def load_x(j):
                cols = slice(X_AT[j], X_AT[j + 1])
                sp.dma_start(x_nat[:, :, cols], x2.rearrange("(t p) c -> p t c", p=P)[:, :, cols]).then_inc(s_x[j], 16)

            load_x(0)
            small(gain_in[:], a["swa_norm"])
            load_chunk(w_in, 2048, 0, quads=(0,))
            load_x(1)
            load_x(2)
            load_chunk(w_in, 2048, 1, quads=(1,), odd=1)
            load_x(3)
            load_x(4)
            load_chunk(w_in, 2048, 2, quads=(2, 3))
            small(rel[0:32, :], a["rel_bias"])
            small(marks[:], a["t5_marks"])
            small(sinks[:], a["swa_sinks"].partition_broadcast(P))
            small(gain_qk[:, 0], a["swa_q_gain"].partition_broadcast(P))
            small(gain_qk[:, 1], a["swa_k_gain"].partition_broadcast(P))
            with sp.Fori(0, 4) as i:
                load_chunk(w_in, i * CW, i * 4 + 4)
            with sp.Fori(0, 4) as i:
                load_chunk(w_in, i * CW + 2560, i * 4 + 20)
            small(gain_2[:], a["attn_norm_w"])
            with sp.Fori(0, 4) as i:
                load_chunk(w_out, i * CW, i * 4 + 36)
            for dst, name in ((gain_cq, "mla_q_norm_w"), (gain_ckv, "mla_kv_norm_w"), (cos, "cos"), (sin, "sin"),
                              (cos_m, "cos_m"), (sin_m, "sin_m"), (slopes, "slopes")):
                sp.dma_start(dst[:] if name not in ("cos", "sin") else dst[:].rearrange("p t d -> p (t d)"),
                             a[name]).then_inc(s_small2, 16)
            sp.dma_start(subln[:], a["diff_subln_w"].partition_broadcast(P)).then_inc(s_small2, 16)
            sp.wait_ge(s_row_d, 16)
            sp.dma_start(mask[:], a["mask"]).then_inc(s_small2, 16)
            w_in2 = a["w_in"].rearrange("(q k p) c -> p q k c", p=P, k=4)
            w_out2 = a["w_out"].rearrange("(q k p) c -> p q k c", p=P, k=4)
            load_chunk(w_in2, 4608, 52)
            load_chunk(w_in2, 4096, 56)
            with sp.Fori(0, 4) as i:
                load_chunk(w_in2, i * CW + 1024, i * 4 + 60)
            w_uq = a["w_uq"].rearrange("(k p) c -> p k c", p=P)
            w_ukv = a["w_ukv"].rearrange("(k p) c -> p k c", p=P)
            for j in range(3):
                q = 76 + j
                sp.wait_ge(s_lo, 4 * q + 4)
                sp.dma_start(w_raw[:, q % 2], w_uq[:, :, j * CW:(j + 1) * CW]).then_inc(s_raw[q % 2], 16)
            for j in range(2):
                q = 79 + j
                sp.wait_ge(s_lo, 4 * q + 4)
                sp.dma_start(w_raw[:, q % 2, 0:2], w_ukv[:, :, 2 * j * CW:(2 * j + 1) * CW]).then_inc(s_raw[q % 2], 16)
                sp.dma_start(w_raw[:, q % 2, 2:4], w_ukv[:, :, (2 * j + 1) * CW:(2 * j + 2) * CW]).then_inc(s_raw_2nd[j], 16)
            with sp.Fori(0, 2) as i:
                load_chunk(w_in2, i * CW, i * 4 + 81, odd=1)
            with sp.Fori(0, 2) as i:
                load_chunk(w_in2, i * CW + 4928, i * 4 + 89, odd=1)
            with sp.Fori(0, 2) as i:
                load_chunk(w_in2, i * CW + 3072, i * 4 + 97, odd=1)
            with sp.Fori(0, 4) as i:
                load_chunk(w_out2, i * CW, i * 4 + 105, quads=[k // 4 for k in ORDER[::4]], odd=1)
            for t in range(NT - 1):
                sp.wait_ge(s_fin, t + 1)
                sp.dma_start(out[t * P:(t + 1) * P, :].rearrange("p (c w) -> p c w", c=4), h2[:, :, t]).then_inc(s_out, 16)
            sp.wait_ge(s_out, 16 * NT)

        PIECES = 484
        Q_BASE, UQ, UKV = 324, 304, 316

        @block.tensor
        def _(pe):
            mm = nc.tensor.matmul

            def project(n, c, k, t, hi, lo, cols=CW, K=KC, slot=None, kc=None):
                if t == 0:
                    pe.wait_ge(s_lo, n + 8 + 1)
                if k == 0:
                    pe.wait_ge(s_evac, 4 * c + t + 1)
                rows = slice(t * P, (t + 1) * P)
                slot = k % 4 if slot is None else slot
                kc = k if kc is None else kc
                wh, wl = w_hi[:, slot, 0:cols], w_lo[:, slot, 0:cols]
                mm(acc[t][:, 0:cols], hi[:, kc, rows], wh, start=(k == 0), stop=False)
                mm(acc[t][:, 0:cols], hi[:, kc, rows], wl, start=False, stop=False)
                last = mm(acc[t][:, 0:cols], lo[:, kc, rows], wh, start=False, stop=(k == K - 1))
                if t == NT - 1:
                    last.then_inc(s_used, 1)
                elif k == K - 1:
                    last.then_inc(s_acc, 1)

            def project_meta(n, m, k, lhs, cols=CW, K=KC, slot=None):
                if k == 0:
                    pe.wait_ge(s_mevac, m + 1)
                slot = k % 4 if slot is None else slot
                mm(sc[0][0:FULL, 0:cols], lhs[:, k], w_hi[:, slot, 0:cols], start=(k == 0), stop=False)
                last = mm(sc[0][0:FULL, 0:cols], lhs[:, k], w_lo[:, slot, 0:cols], start=False, stop=(k == K - 1))
                if k == K - 1:
                    last.then_inc(s_meta, 1)

            def turn4(b, bank, tiles):
                pe.wait_ge(s_turn_lo, b + 1)
                for t, tile in enumerate(tiles):
                    last = nc.tensor.transpose(turn[bank][:, t * P:(t + 1) * P], tile, ident[:])
                last.then_inc(s_turned, 1)
                return last

            pe.sem_inc(s_used, 4)
            pe.sem_inc(s_tr, EARLY)
            pe.sem_inc(s_pv, EARLY)
            pe.sem_inc(MLA.pv, EARLY)
            pe.sem_inc(DIFF.pv, EARLY)
            pe.wait_ge(s_ident, 2)
            for k in range(KC):
                for b in ([0, 1] if k == 0 else [k + 1] if k + 1 < KC else []):
                    if b * P in X_AT:
                        pe.wait_ge(s_x[X_AT.index(b * P)], 16)
                    turn4(b, b % 2, [x_nat[:, t, b * P:(b + 1) * P] for t in range(NT)])
                pe.wait_ge(s_turn_lo, k + 1 + EARLY)
                for t in range(NT):
                    project(k, 0, k, t, setA_hi, setA_lo)
            pe.wait_ge(s_rel, 1)
            pe.wait_ge(s_small, 96)
            mm(sc[0][0:32, 0:BIAS_W], rel[:], marks[:], start=True, stop=True).then_inc(s_row_ps, 1)
            for k in range(KC):
                for t in range(NT):
                    project(KC + k, 1, k, t, setA_hi, setA_lo)

            def q_turn(g, b):
                if b == 0:
                    pe.wait_ge(s_kdup, g + 1)
                else:
                    pe.wait_ge(s_qn, g + 1)
                pe.wait_ge(s_qT, g * 5 + (b + 1))
                for t in range(NT):
                    tile = k_twice[:, t].rearrange("p a d -> p (a d)") if b == 0 else stage[:, t, (b - 1) * P:b * P]
                    last = nc.tensor.transpose(turn[(b + 1) % 2][:, t * P:(t + 1) * P], tile, ident[:])
                last.then_inc(s_qturn, 1)

            def scores(g, u):
                hp, j = u // NT, u % NT
                if j == 0:
                    pe.wait_ge(s_qT, g * 5 + (hp + 2 + 2))
                pe.wait_ge(s_m, g * UNITS + u + EARLY)
                lo = max(j - 1, 0) * P
                for h in range(2):
                    dst, q = sc[h][:, (P if j == 0 else 0):256], (qT_a, qT_b)[hp // 2][:, hp % 2 * 2 + h, j * P:(j + 1) * P]
                    mm(dst, q, kT_hi[:, lo:(j + 1) * P], start=True, stop=False)
                    last = mm(dst, q, kT_lo[:, lo:(j + 1) * P], start=False, stop=True)
                last.then_inc(s_score, 1)

            def turn_p(g, u):
                j = u % NT
                pe.wait_ge(s_p, g * UNITS + u + 1)
                if u == 0:
                    pe.wait_ge(s_qT, g * 5 + (4 + 2))
                else:
                    pe.wait_ge(s_pT, g * UNITS + u)
                for h in range(2):
                    for c in range(1 if j == 0 else 0, 2):
                        last = nc.tensor.transpose(turn[0][:, (2 * h + c) * P:(2 * h + c + 1) * P],
                                                   p_w[:, u % 2, h, c * P:(c + 1) * P], ident[:])
                last.then_inc(s_tr, 1)

            def values(g, u):
                j = u % NT
                pe.wait_ge(s_pT, g * UNITS + u + 1)
                if u == 0:
                    pe.wait_ge(s_qT, g * 5 + (5 + 2))
                pe.wait_ge(s_o, g * UNITS + u + 1)
                for h in range(2):
                    for c in range(1 if j == 0 else 0, 2):
                        last = mm(o_ps[:, h * HD:(h + 1) * HD], pT[:, u % 2, 2 * h + c], vg[:, j - 1 + c],
                                  start=(c == (1 if j == 0 else 0)), stop=(c == 1))
                last.then_inc(s_pv, 1)

            with pe.Fori(0, 4) as g:
                for H in range(32):
                    for t in (0, 1) if H % 2 == 0 else (2, 3):
                        project(g * KC + (2 * KC + H // 2), g + 2, H // 2, t, setA_hi, setA_lo)
                    if 0 <= H - 16 < UNITS:
                        values(g, H - 16)
                    if 0 <= H - 14 < UNITS:
                        turn_p(g, H - 14)
                    if 0 <= H - 12 < UNITS:
                        scores(g, H - 12)
                    if H == 3 or 10 <= H < 14:
                        q_turn(g, max(H - 9, 0))
            pe.wait_ge(s_o, 4 * UNITS + 1)

            def og_turn(g, f):
                if f == 0:
                    pe.wait_ge(s_og, g + 1)
                last = turn4(g * 4 + (16 + f), f % 2, [stage[:, t, f * P:(f + 1) * P] for t in range(NT)])

            with pe.Fori(0, 3) as i:
                for k in range(KC):
                    for t in range(NT):
                        project(i * KC + (6 * KC + k), i + 6, k, t, setA_hi, setA_lo)
                    if 5 <= k < 9:
                        og_turn(i, k - 5)
            for k in range(KC):
                if 5 <= k < 9:
                    og_turn(3, k - 5)
                if k >= 12:
                    pe.wait_ge(s_turn_lo, 28 + (k - 12) + 1 + EARLY)
                elif k == 0:
                    pe.wait_ge(s_turn_lo, 28 + EARLY)
                for t in range(NT):
                    project(9 * KC + k, 9, k, t, setB_hi, setB_lo)
                if k == 12:
                    pe.wait_ge(s_meta_in, 16)
                    for f in range(KC):
                        last = nc.tensor.transpose(sc[1][:, f * META:(f + 1) * META], meta_nat[:, f * P:(f + 1) * P],
                                                   ident[0:META, 0:META])
                    last.then_inc(s_mturn, 1)

            def x1_turn(c, f):
                if f == 0:
                    pe.wait_ge(s_x1, c + 1)
                turn4(c * 4 + (32 + f), f % 2, [stage[:, t, f * P:(f + 1) * P] for t in range(NT)])

            with pe.Fori(0, 3) as i:
                for k in range(KC):
                    for t in range(NT):
                        project(i * KC + (10 * KC + k), i + 10, k, t, setB_hi, setB_lo)
                    if 4 <= k < 8:
                        x1_turn(i, k - 4)
            pe.wait_ge(s_turn_lo, 44 + EARLY)
            pe.wait_ge(s_metaT, 1)
            for k in range(KC):
                if 4 <= k < 8:
                    x1_turn(3, k - 4)
                if k >= 12:
                    pe.wait_ge(s_turn_lo, 44 + (k - 12) + 1 + EARLY)
                for t in range(NT):
                    if t == NT - 1:
                        project_meta(13 * KC + k, 0, k, metaT, 320)
                    project(13 * KC + k, 13, k, t, setA_hi, setA_lo, 320)
            for k in range(KC):
                for t in range(NT):
                    project(14 * KC + k, 14, k, t, setA_hi, setA_lo)
                if k == 4:
                    pe.wait_ge(s_kpe, 1)
                    for t in range(NT):
                        last = nc.tensor.transpose(sc[1][0:ROPE, t * P:(t + 1) * P], kpe[:, t], ident[:])
                    last.then_inc(s_kpe_ps, 1)
                    pe.wait_ge(s_mstage, 1)
                    pe.wait_ge(s_mevac, 2)
                    nc.tensor.transpose(sc[0][0:ROPE, 0:META], kpe_m[:], ident[0:META, 0:META])
                    for f in range(2):
                        last = nc.tensor.transpose(sc[0][:, (f + 1) * META:(f + 2) * META],
                                                   stage_m[:, f * P:(f + 1) * P], ident[0:META, 0:META])
                    last.then_inc(s_kpe_ps, 1)
                if 5 <= k < 7:
                    turn4(48 + k - 5, (k - 5) % 2, [stage[:, t, (k - 5) * P:(k - 4) * P] for t in range(NT)])
            pe.wait_ge(s_ckvm, 2)
            for k in range(KC):
                for t in range(NT):
                    if t == NT - 1:
                        project_meta(15 * KC + k, 1, k, metaT)
                    project(15 * KC + k, 15, k, t, setA_hi, setA_lo)
                if 5 <= k < 9:
                    if k == 5:
                        pe.wait_ge(s_evac, 4 * 14 + 8)
                    turn4(50 + k - 5, (k - 5) % 2, [stage[:, t, (k - 5) * P:(k - 4) * P] for t in range(NT)])
            with pe.Fori(0, 3) as i:
                for k in range(KC):
                    for t in range(NT):
                        if t == NT - 1:
                            project_meta(i * KC + (16 * KC + k), i + 2, k, metaT)
                        project(i * KC + (16 * KC + k), i + 16, k, t, setA_hi, setA_lo)
            pe.wait_ge(s_turn_lo, 54 + EARLY)
            for c in range(3):
                for k in range(4):
                    for t in range(NT):
                        project(UQ + 4 * c + k, 19 + c, k, t, cqT_hi, cqT_lo, K=4)
            for c in range(4):
                for k in range(2):
                    for t in range(NT):
                        if t == NT - 1:
                            project_meta(UKV + 2 * c + k, 5 + c, k, ckvmT, K=2, slot=(2 * c + k) % 4)
                        project(UKV + 2 * c + k, 22 + c, k, t, ckvT_hi, ckvT_lo, K=2, slot=(2 * c + k) % 4)

            def head_turn(A, i, head, b):
                buf, use = head % 2, i * 2 + (head // 2 + 1)
                if b == 0:
                    pe.wait_ge(A.rope if A.mla else A.ld_qk[buf], i * 4 + (head + 1) if A.mla else use * 32)
                t0_use(A, i)
                if b == A.batches - 1:
                    if A.mla:
                        pe.wait_ge(A.o, i * NU + (count["pv"] + 1))
                    for t in range(NT):
                        last = nc.tensor.transpose(turn[0][:, t * P:(t + 1) * P], nat_k[:, buf, t], ident[:])
                    if A.mla:
                        last = nc.tensor.transpose(turn[1][:, 0:META], natm_k[:, buf], ident[0:META, 0:META])
                elif b == 0:
                    for t in range(NT):
                        last = nc.tensor.transpose(turn[0][:, t * P:(t + 1) * P], nat_q[:, buf, t, 0:VD], ident[:])
                else:
                    for t in range(NT):
                        last = nc.tensor.transpose(turn[0][:, t * P:(t + 1) * P], nat_q[:, buf, t, QB - P:QB], ident[:])
                last.then_inc(A.full, 1)

            count = {"t0": 0, "pv": 0}

            def t0_use(A, i):
                pe.wait_ge(A.free, i * (4 * A.batches + NU) + (count["t0"] + 1))
                count["t0"] += 1

            def scores2(A, i, u, comp):
                head, j = u // NT, u % NT
                buf = head % 2
                if j == 0 and comp == 0:
                    pe.wait_ge(A.free, i * (4 * A.batches + NU) + (ready_at[head] + 1))
                other = j in (1, 2) or (comp == 1 and j < NT - 1)
                pe.wait_ge(A.m, i * NU * A.comps + (u * A.comps + comp + (0 if other else 1)))
                q = slice(j * P, (j + 1) * P)
                rows = slice(0, P) if A.mla else slice(comp * QKD, (comp + 1) * QKD)
                start = score_at(A, u, comp)
                cuts = [0, width(j)] if j < NT - 1 else [0, BANK_CUT, width(j)]
                for first, end in zip(cuts, cuts[1:]):
                    keys = slice(first, end)
                    dst = sc2[:, start + keys.start:start + keys.stop]
                    last = mm(dst, qnT[rows, buf, q], knT[rows, buf, keys], start=True, stop=not A.mla)
                    if A.mla:
                        mm(dst, qpT[:, buf, q], kpeT_hi[:, keys], start=False, stop=False)
                        last = mm(dst, qpT[:, buf, q], kpeT_lo[:, keys], start=False, stop=True)
                last.then_inc(A.score, 1)

            def turn_p2(A, i, u):
                j = u % NT
                pe.wait_ge(A.p if A.mla else A.w, i * NU + (u + 1))
                t0_use(A, i)
                pe.wait_ge(A.o, i * NU + (u + 1))
                src = p2[:, u % 2, 0, KEYS - width(j):]
                nc.tensor.transpose(turn[1][0:META, P:2 * P], src[:, 0:META], ident[:])
                for b in range(j + 1):
                    last = nc.tensor.transpose(turn[0][:, b * P:(b + 1) * P], src[:, META + b * P:META + (b + 1) * P], ident[:])
                last.then_inc(A.full, 1)

            def values2(A, i, u):
                head, j = u // NT, u % NT
                buf = head % 2
                pe.wait_ge(A.free, i * (4 * A.batches + NU) + ((count["t0"] if A.mla else turned_at[u]) + 1))
                if j == 0:
                    pe.wait_ge(A.ld_v[buf], (i * 2 + (head // 2 + 1)) * 32)
                dst = turn[1][:, 2 * P:3 * P]
                for b in range(j + 1):
                    mm(dst, pT2[:, u % 2, b * P:(b + 1) * P], nat_v[:, buf, b], start=(b == 0), stop=False)
                mm(dst, pTm[:, u % 2], natm_v[:, buf], start=False, stop=True).then_inc(A.pv, 1)
                count["pv"] += 1

            def attend_body(A, i, n0, c0):
                count["t0"] = count["pv"] = 0
                ready_at.clear()
                for Q in range(4 * KC):
                    k, t = Q // 4, Q % 4
                    project(i * KC + (n0 + k), i + c0, k, t, setA_hi, setA_lo)
                    if A.mla and Q == 5:
                        pe.wait_ge(s_zero, 1)
                    for u in range(NU):
                        if Q == unit_time(u) + A.values_after:
                            values2(A, i, u)
                    for head in range(4):
                        for b in range(A.batches):
                            if Q == turn_time(A, head, b):
                                head_turn(A, i, head, b)
                                ready_at[head] = count["t0"]
                    for u in range(NU):
                        if Q == unit_time(u):
                            scores2(A, i, u, 0)
                        if not A.mla and Q == unit_time(u) + 1:
                            scores2(A, i, u, 1)
                    for u in range(NU):
                        if Q == unit_time(u) + A.turn_after:
                            turn_p2(A, i, u)
                            turned_at[u] = count["t0"]
                    if not A.mla and Q == 5:
                        pe.wait_ge(s_km, 1)

            ready_at, turned_at = {}, {}
            with pe.Fori(0, 2) as i:
                attend_body(MLA, i, Q_BASE, 26)
            pe.wait_ge(MLA.o, 2 * NU + 1)
            pe.wait_ge(s_km_in, 16)
            for h in range(HEADS):
                last = nc.tensor.transpose(turn[1][:, h * META:(h + 1) * META], diff_km[:, h * VD:(h + 1) * VD],
                                           ident[0:META, 0:META])
            last.then_inc(s_km_ps, 1)
            with pe.Fori(0, 2) as i:
                attend_body(DIFF, i, Q_BASE + 2 * KC, 28)
            pe.wait_ge(DIFF.o, 2 * NU + 1)

            def gate_turn(b, f, og, src=stage):
                if f == 0:
                    pe.wait_ge(s_og, og)
                turn4(b + f, f % 2, [src[:, t, f * P:(f + 1) * P] for t in range(NT)])

            for k in range(KC):
                for t in range(NT):
                    project(Q_BASE + 4 * KC + k, 30, k, t, setA_hi, setA_lo)
                if 5 <= k < 9:
                    gate_turn(54, k - 5, 5)
                if 9 <= k < 13:
                    gate_turn(58, k - 9, 6, gate_0)
            for k in range(KC):
                for t in range(NT):
                    project(Q_BASE + 5 * KC + k, 31, k, t, setA_hi, setA_lo)
                if 8 <= k < 12:
                    gate_turn(62, k - 8, 7)
            pe.wait_ge(s_turn_lo, 66 + EARLY)
            for k in range(KC):
                if 5 <= k < 9:
                    gate_turn(66, k - 5, 8)
                if k >= 12:
                    pe.wait_ge(s_turn_lo, 66 + (k - 12) + 1 + EARLY)
                for t in range(NT):
                    project(Q_BASE + 6 * KC + k, 32, k, t, setB_hi, setB_lo, kc=ORDER[k])
            with pe.Fori(0, 3) as i:
                for k in range(KC):
                    for t in range(NT):
                        project(i * KC + (Q_BASE + 7 * KC + k), i + 33, k, t, setB_hi, setB_lo, kc=ORDER[k])

        @block.scalar
        def _(act):
            def split_hi(n0, i, k):
                f = n0 + k + AHEAD
                if isinstance(i, int) and f + i * KC >= PIECES:
                    return
                q = f // 4
                if f % 4 == 0:
                    act.wait_ge(s_raw[q % 2], i * 32 + 16 * (q // 2 + 1))
                    if f in (UKV, UKV + 4):
                        act.wait_ge(s_raw_2nd[(f - UKV) // 4], 16)
                act.wait_ge(s_used, i * KC + f + 1)
                nc.scalar.activation(w_hi[:, f % 4], w_raw[:, q % 2, f % 4], ACT.Copy).then_inc(s_hi, 1)

            def evacuate(c, scale, end=None, cols=CW, dst=stage):
                end = (c + 1) * KC if end is None else end
                for t in range(NT):
                    if t < NT - 1:
                        act.wait_ge(s_acc, 3 * c + t + 1)
                    else:
                        act.wait_ge(s_used, end + 4)
                    nc.scalar.activation(dst[:, t, 0:cols], acc[t][:, 0:cols], ACT.Copy,
                                         scale=scale[:, t:t + 1] if scale is not None else 1.0).then_inc(s_evac, 1)

            def evacuate_meta(m, cols=CW):
                act.wait_ge(s_meta, m + 1)
                nc.scalar.activation(tmp_m[:, 0:cols], sc[0][32:32 + META, 0:cols], ACT.Copy).then_inc(s_mtmp, 1)

            def stored(chunk):
                act.wait_ge(s_short[chunk % 2], 16 * ((chunk - 18) // 2 + 1))

            def store(c, dst, col, m=None, src=stage, signal=s_st):
                cols = slice(col, col + CW) if isinstance(col, int) else bass.ds(act.snap(col), CW)
                act.wait_ge(s_evac, 4 * c + 8)
                act.dma_start(dst[0:S, :].rearrange("(t p) c -> p t c", p=P)[:, :, cols], src[:]).then_inc(signal, 16)
                if m is not None:
                    cols = slice(col, col + CW) if isinstance(col, int) else bass.ds(act.snap(col), CW)
                    act.wait_ge(s_mstage, m + 1)
                    act.dma_start(dst[S:KEYS, cols], stage_m[:]).then_inc(s_mst, 16)

            def turn_hi(b, bank, dst, gain):
                act.wait_ge(s_turned, b + 1)
                nc.scalar.activation(dst, turn[bank][:], ACT.Copy, scale=gain).then_inc(s_turn_hi, 1)

            act.sem_inc(s_evac, 4)
            act.sem_inc(MLA.free, 1)
            act.sem_inc(DIFF.free, 1)
            act.wait_ge(s_small, 16)
            for k in range(KC):
                for b in ([0, 1] if k == 0 else [k + 1] if k + 1 < KC else []):
                    turn_hi(b, b % 2, setA_hi[:, b], gain_in[:, b:b + 1])
                if k == 0:
                    act.wait_ge(s_raw[0], 16)
                    for f in range(AHEAD):
                        nc.scalar.activation(w_hi[:, f], w_raw[:, 0, f], ACT.Copy).then_inc(s_hi, 1)
                split_hi(0, 0, k)
            act.wait_ge(s_root, ROOT_X)
            evacuate(0, r_x)
            act.wait_ge(s_row_ps, 1)
            nc.scalar.activation(bias_row[:], sc[0][0:32, 0:BIAS_W], ACT.Copy).then_inc(s_row, 1)
            act.wait_ge(s_row, 1)
            act.dma_start(row_d, bias_row[:].unsqueeze(1).to_broadcast([32, SKEW + 1, BIAS_W])).then_inc(s_row_d, 16)
            for k in range(KC):
                split_hi(KC, 0, k)
            act.wait_ge(s_kn, 2)
            evacuate(1, r_x)

            def weigh(g, u):
                act.wait_ge(s_m, g * UNITS + u + 1 + EARLY)
                act.wait_ge(s_tr, g * UNITS + u + 1)
                first = P if u % NT == 0 else 0
                for h in range(2):
                    nc.scalar.activation(p_w[:, u % 2, h, first:], sm[:, u % 2, h, first:], ACT.Exp,
                                         bias=negm[:, u % 2, h:h + 1], scale=-1.0, accum_out=den[:, u % 2, h:h + 1])
                nc.scalar.activation(sink_e[:, u % 2], sink_d[:, u % 2], ACT.Exp).then_inc(s_p, 1)

            def keep_pT(g, u):
                act.wait_ge(s_tr, g * UNITS + u + 1 + EARLY)
                act.wait_ge(s_pv, g * UNITS + u + 1)
                nc.scalar.activation(pT[:, u % 2].rearrange("p a q -> p (a q)"), turn[0][:], ACT.Copy).then_inc(s_pT, 1)

            def keep_qT(g, b):
                act.wait_ge(s_qturn, g * 5 + b + 1)
                if b == 0:
                    nc.scalar.activation(kT_hi[:], turn[1][:], ACT.Copy).then_inc(s_qhi, 1)
                    return
                for h in range(2):
                    rows = slice(h * HD, (h + 1) * HD)
                    last = nc.scalar.activation(head_T(b, h)[rows], turn[(b + 1) % 2][rows], ACT.Copy)
                last.then_inc(s_qhi, 1)

            with act.Fori(0, 4) as g:
                for H in range(32):
                    if H == 1:
                        act.wait_ge(s_row_d, 16)
                        act.wait_ge(s_o, g * UNITS + 1)
                        flat, heads = row_d.rearrange("h q m -> h (q m)"), bass.ds(act.snap(g * GROUP), GROUP)
                        for q in range(0, P, SKEW):
                            skew = flat[:, P - 1 - q:P - 1 - q + SKEW * (BIAS_W - 1)].rearrange("h (q m) -> q h m", q=SKEW)
                            act.dma_start(bias[q:q + SKEW], skew[:, heads, 0:256]).then_inc(s_bias, 16)
                    if 0 <= H - 13 < UNITS:
                        weigh(g, H - 13)
                    if H == 3 or 10 <= H < 14:
                        keep_qT(g, max(H - 9, 0))
                    if H % 2 == 0:
                        split_hi(2 * KC, g, H // 2)
                    if 0 <= H - 14 < UNITS:
                        keep_pT(g, H - 14)
                evacuate(g + 2, r_x)

            def gate_sigmoid(g):
                act.wait_ge(s_evac, 4 * (g + 5) + 8)
                nc.scalar.activation(work[:], stage[:], ACT.Sigmoid).then_inc(s_silu, 1)

            with act.Fori(0, 3) as i:
                for k in range(KC):
                    if k == 0:
                        gate_sigmoid(i)
                    split_hi(6 * KC, i, k)
                    if 5 <= k < 9:
                        turn_hi(i * 4 + (16 + k - 5), (k - 5) % 2, setB_hi[:, bass.ds(i * 4 + (k - 5), 1)].rearrange("p o s -> p (o s)"), 1.0)
                evacuate(i + 6, r_x)
            def load_residual(c):
                if isinstance(c, int):
                    act.wait_ge(s_og, 4)
                    cols = slice(c * CW, (c + 1) * CW)
                else:
                    act.wait_ge(s_x1, c)
                    cols = bass.ds(act.snap(c * CW), CW)
                act.dma_start(x_in[:], a["x"].rearrange("(t p) c -> p t c", p=P)[:, :, cols]).then_inc(s_xin, 16)

            def store_x1(c):
                cols = slice(c * CW, (c + 1) * CW) if isinstance(c, int) else bass.ds(act.snap(c * CW), CW)
                act.wait_ge(s_x1, c + 1)
                act.dma_start(x1_d.rearrange("(t p) c -> p t c", p=P)[:, :, cols], stage[:]).then_inc(s_x1d, 16)

            def x1_hi(c, f):
                if isinstance(c, int):
                    dst = setA_hi[:, 4 * c + f]
                else:
                    dst = setA_hi[:, bass.ds(c * 4 + f, 1)].rearrange("p o s -> p (o s)")
                act.wait_ge(s_gain_c, c + 1)
                turn_hi(c * 4 + (32 + f), f % 2, dst, gain_c[:, f:f + 1])

            for k in range(KC):
                if k == 0:
                    gate_sigmoid(3)
                split_hi(9 * KC, 0, k)
                if 5 <= k < 9:
                    turn_hi(28 + k - 5, (k - 5) % 2, setB_hi[:, 12 + k - 5], 1.0)
                if k == 0:
                    act.wait_ge(s_pv, 4 * UNITS + EARLY)
                    act.dma_start(meta_nat[:], a["meta_tokens"]).then_inc(s_meta_in, 16)
                if k == 11:
                    load_residual(0)
                if k == 14:
                    act.wait_ge(s_metaF, 1)
                    nc.scalar.activation(metaT[:, :, 0:META], meta_f[:], ACT.Copy).then_inc(s_metaH, 1)
            evacuate(9, None)
            with act.Fori(0, 3) as i:
                for k in range(KC):
                    split_hi(10 * KC, i, k)
                    if k == 3:
                        store_x1(i)
                    if 4 <= k < 8:
                        x1_hi(i, k - 4)
                    if k == 11:
                        load_residual(i + 1)
                act.wait_ge(s_x1d, i * 16 + 16)
                evacuate(i + 10, None)
            for k in range(KC):
                split_hi(13 * KC, 0, k)
                if k == 0:
                    act.wait_ge(s_metaT, 1)
                    act.dma_start(lam_in[:].rearrange("p a d -> p (a d)"),
                                  a["diff_lambda"].rearrange("a d -> (a d)").partition_broadcast(P)).then_inc(s_lam, 16)
                if k == 3:
                    store_x1(3)
                if 4 <= k < 8:
                    x1_hi(3, k - 4)
            act.wait_ge(s_x1d, 64)
            act.wait_ge(s_root, ROOT_2)
            evacuate(13, r_2, cols=320)
            evacuate_meta(0, 320)
            for k in range(KC):
                split_hi(14 * KC, 0, k)
                if k == 2:
                    act.wait_ge(s_lam, 17)
                    nc.scalar.activation(lam_s[:], lam_s[:], ACT.Exp).then_inc(s_lam, 1)
                if k == 5:
                    act.wait_ge(s_kpe_ps, 1)
                    for half in (slice(0, ROPE), slice(ROPE, P)):
                        nc.scalar.activation(kpeT_hi[half, META:KEYS], sc[1][0:ROPE, :], ACT.Copy)
                    act.wait_ge(s_kpe_ps, 2)
                    for half in (slice(0, ROPE), slice(ROPE, P)):
                        last = nc.scalar.activation(kpeT_hi[half, 0:META], sc[0][0:ROPE, 0:META], ACT.Copy)
                    last.then_inc(s_kpeT, 1)
                    for f in range(2):
                        last = nc.scalar.activation(ckvmT[:, f, 0:META], sc[0][:, (f + 1) * META:(f + 2) * META], ACT.Copy,
                                                    scale=gain_ckv[:, f:f + 1])
                    last.then_inc(s_kpeT, 1)
                if 6 <= k < 8:
                    turn_hi(48 + k - 6, k % 2, ckvT_hi[:, k - 6], gain_ckv[:, k - 6:k - 5])
            evacuate(14, r_2)
            for k in range(KC):
                split_hi(15 * KC, 0, k)
                if 6 <= k < 10:
                    turn_hi(50 + k - 6, k % 2, cqT_hi[:, k - 6], gain_cq[:, k - 6:k - 5])
            evacuate(15, r_2)
            evacuate_meta(1)
            with act.Fori(0, 3) as i:
                for k in range(KC):
                    split_hi(16 * KC, i, k)
                    if k == 1:
                        store(i + 15, kv_d, i * CW, i + 1)
                act.wait_ge(s_st, i * 16 + 16)
                act.wait_ge(s_mst, i * 16 + 16)
                evacuate(i + 16, r_2)
                evacuate_meta(i + 2)
            act.wait_ge(s_root, ROOT_CQ)
            stages = (stage, work)
            for c in range(3):
                for k in range(4):
                    split_hi(UQ + 4 * c, 0, k)
                    if k == 0:
                        if c == 0:
                            store(18, kv_d, 3 * CW, 4, signal=s_short[0])
                        else:
                            store(18 + c, qb_d, (c - 1) * CW, src=stages[(c - 1) % 2], signal=s_short[c % 2])
                stored(max(18, 17 + c))
                evacuate(19 + c, r_cq, end=UQ + 4 * c + 4, dst=stages[c % 2])
            for c in range(4):
                for k in range(2):
                    split_hi(UKV + 2 * c, 0, k)
                    if k == 0:
                        if c == 0:
                            store(21, qb_d, 2 * CW, src=stages[0], signal=s_short[1])
                        else:
                            store(21 + c, kvb_d, (c - 1) * CW, 4 + c, src=stages[c % 2], signal=s_short[(21 + c) % 2])
                stored(20 + c)
                evacuate(22 + c, r_kv, end=UKV + 2 * c + 2, dst=stages[(c + 1) % 2])
                evacuate_meta(5 + c)
            store(25, kvb_d, 3 * CW, 8, signal=s_short[1])

            def keep_head(A, i, head, b):
                buf = head % 2
                act.wait_ge(A.full, i * (4 * A.batches + NU) + (count["t0"] + 1))
                count["t0"] += 1
                scale = B_SCALE if A.mla else A_SCALE
                if b == 0:
                    last = nc.scalar.activation(qnT[:, buf], turn[0][:], ACT.Copy, scale=scale)
                elif b < A.batches - 1:
                    nc.scalar.activation(qpT[ROPE:P, buf], turn[0][ROPE:P, :], ACT.Copy, scale=scale).then_inc(s_qp_hi, 1)
                    return
                else:
                    nc.scalar.activation(knT[:, buf, META:KEYS], turn[0][:], ACT.Copy)
                    meta = turn[1][:, 0:META] if A.mla else diff_kmT[:, (4 * i + head) * META:(4 * i + head + 1) * META]
                    last = nc.scalar.activation(knT[:, buf, 0:META], meta, ACT.Copy)
                last.then_inc(A.free, 1)

            def weigh2(A, i, u, comp):
                lo, slot = S - (u % NT + 1) * P, u % 2 if A.mla else comp
                act.wait_ge(A.m, i * NU * A.comps + (u * A.comps + comp + 2))
                nc.scalar.activation(p2[:, u % 2, comp, lo:], sm2[:, slot, lo:], ACT.Exp, bias=negm_2[:, u % 2, comp:comp + 1], scale=-1.0,
                                     accum_out=den_2[:, u % 2, comp:comp + 1]).then_inc(A.p, 1)

            def keep_pT2(A, i, u):
                n = (u % NT + 1) * P
                act.wait_ge(A.full, i * (4 * A.batches + NU) + (count["t0"] + 1))
                count["t0"] += 1
                act.wait_ge(A.pv, i * NU + (u + 1))
                nc.scalar.activation(pT2[:, u % 2, 0:n], turn[0][:, 0:n], ACT.Copy)
                nc.scalar.activation(pTm[0:META, u % 2], turn[1][0:META, P:2 * P], ACT.Copy).then_inc(A.free, 1)

            count = {"t0": 0}

            def attend_body(A, i, n0, c0, n_store, dst):
                count["t0"] = 0
                for Q in range(4 * KC):
                    if Q % 4 == 0:
                        split_hi(n0, i, Q // 4)
                    if A.mla and Q == 5:
                        act.wait_ge(s_zero, 1)
                    for u in range(NU):
                        for comp in range(A.comps):
                            if Q == unit_time(u) + 1 + comp:
                                weigh2(A, i, u, comp)
                    for head in range(4):
                        for b in range(A.batches):
                            if Q == turn_time(A, head, b):
                                keep_head(A, i, head, b)
                    for u in range(NU):
                        if Q == unit_time(u) + A.turn_after:
                            keep_pT2(A, i, u)
                stored(25)
                act.wait_ge(s_st, (i + n_store) * 16)
                evacuate(i + c0, r_2, end=i * KC + (n0 + KC))
                if dst is not None:
                    store(i + c0, dst, i * CW)

            with act.Fori(0, 2) as i:
                attend_body(MLA, i, Q_BASE, 26, 3, qa_d)
            act.wait_ge(s_km_ps, 1)
            nc.scalar.activation(diff_kmT[:], turn[1][:, 0:HEADS * META], ACT.Copy).then_inc(s_km, 1)
            act.wait_ge(s_km, 1)
            attend_body(DIFF, 0, Q_BASE + 2 * KC, 28, 5, gate_d)
            attend_body(DIFF, 1, Q_BASE + 2 * KC, 28, 5, None)

            def gate_sigmoid2(src=stage):
                nc.scalar.activation(work[:], src[:], ACT.Sigmoid).then_inc(s_silu, 1)

            act.wait_ge(DIFF.pv, 2 * NU + EARLY)
            act.dma_start(gate_0[:], gate_d.rearrange("(t p) c -> p t c", p=P)).then_inc(s_gld, 16)
            for k in range(KC):
                split_hi(Q_BASE + 4 * KC, 0, k)
                if k == 0:
                    act.wait_ge(s_evac, 4 * 29 + 8)
                    gate_sigmoid2()
                if k == 2:
                    act.wait_ge(s_gld, 16)
                    act.wait_ge(s_og, 5)
                    gate_sigmoid2(gate_0)
                if 5 <= k < 9:
                    turn_hi(54 + k - 5, (k - 5) % 2, setB_hi[:, 12 + k - 5], 1.0)
                if 9 <= k < 13:
                    turn_hi(58 + k - 9, (k - 9) % 2, setB_hi[:, 8 + k - 9], 1.0)
            evacuate(30, r_2, end=Q_BASE + 5 * KC)
            for k in range(KC):
                split_hi(Q_BASE + 5 * KC, 0, k)
                if k == 0:
                    act.wait_ge(s_evac, 4 * 30 + 8)
                    gate_sigmoid2()
                if 8 <= k < 12:
                    turn_hi(62 + k - 8, k % 2, setB_hi[:, k - 8], 1.0)
            evacuate(31, r_2, end=Q_BASE + 6 * KC)

            def load_x1(c):
                cols = slice(c * CW, (c + 1) * CW) if isinstance(c, int) else bass.ds(act.snap(c * CW), CW)
                act.dma_start(x_in[:], x1_d.rearrange("(t p) c -> p t c", p=P)[:, :, cols]).then_inc(s_x1in, 16)

            for k in range(KC):
                split_hi(Q_BASE + 6 * KC, 0, k)
                if k == 0:
                    act.wait_ge(s_evac, 4 * 31 + 8)
                    gate_sigmoid2()
                    act.dma_start(w_final[:], a["final_norm_w"].partition_broadcast(P)).then_inc(s_fin_w, 16)
                if 5 <= k < 9:
                    turn_hi(66 + k - 5, (k - 5) % 2, setB_hi[:, 4 + k - 5], 1.0)
                if k == 11:
                    act.wait_ge(s_og, 8)
                    load_x1(0)
            evacuate(32, None, end=Q_BASE + 7 * KC)
            with act.Fori(0, 2) as i:
                for k in range(KC):
                    split_hi(Q_BASE + 7 * KC, i, k)
                    if k == 11:
                        act.wait_ge(s_h2, i + 1)
                        load_x1(i + 1)
                act.wait_ge(s_h2, i + 1)
                evacuate(i + 33, None, end=i * KC + (Q_BASE + 8 * KC))
            for k in range(KC):
                split_hi(Q_BASE + 9 * KC, 0, k)
                if k == 11:
                    act.wait_ge(s_h2, 3)
                    load_x1(3)
            for t in range(NT):
                act.wait_ge(s_sum, t + 1)
                nc.scalar.activation(x_in[:, t], stage[:, t], ACT.Square, accum_out=ss_c[:, t:t + 1]).then_inc(s_sq, 1)
            act.wait_ge(s_h2, 4)
            act.wait_ge(s_root, ROOT_3)
            last = NT - 1
            nc.scalar.activation(h2[:, :, last], h2[:, :, last], ACT.Copy, scale=r_3[:, last:NT]).then_inc(s_fin_last, 1)
            act.wait_ge(s_fin_last, 1)
            act.dma_start(out[last * P:S, :].rearrange("p (c w) -> p c w", c=4), h2[:, :, last]).then_inc(s_out, 16)

        @block.gpsimd
        def _(pool):
            def split_lo(n0, i, k):
                f = n0 + k + AHEAD
                if isinstance(i, int) and f + i * KC >= PIECES:
                    return
                pool.wait_ge(s_hi, i * KC + f + 1)
                nc.gpsimd.tensor_tensor(w_lo[:, f % 4], w_raw[:, (f // 4) % 2, f % 4], w_hi[:, f % 4].bitcast(F32),
                                        ALU.subtract).then_inc(s_lo, 1)

            def root(dst, src, n, count, rows=P):
                pool.wait_ge(s_var, count)
                nc.gpsimd.tensor_tensor(dst, src, half[0:rows, 0:n], ALU.pow).then_inc(s_root, 1)

            pool.sem_inc(s_lo, 8)
            nc.gpsimd.memset(ident[:], 0.0).then_inc(s_ident, 1)
            nc.gpsimd.memset(half[:], -0.5).then_inc(s_half, 1)
            pool.wait_ge(s_ident, 1)
            nc.gpsimd.affine_select(out=ident[:], in_=ident[:], compare_op=ALU.not_equal, fill=1.0, base=0,
                                    pattern=[[-1, P]], channel_multiplier=1).then_inc(s_ident, 1)
            for f in range(AHEAD):
                pool.wait_ge(s_hi, f + 1)
                nc.gpsimd.tensor_tensor(w_lo[:, f], w_raw[:, 0, f], w_hi[:, f].bitcast(F32), ALU.subtract).then_inc(s_lo, 1)
            for k in range(KC):
                split_lo(0, 0, k)
            pool.wait_ge(s_half, 1)
            root(r_x[:], ss_x[:], NT, ROOT_X)
            for k in range(KC):
                split_lo(KC, 0, k)
                if k == 8:
                    root(r_q[:, 0:16], ss_q[:, 0:16], 16, ROOT_K)

            with pool.Fori(0, 4) as g:
                for H in range(32):
                    if H % 2 == 0:
                        split_lo(2 * KC, g, H // 2)
                    if H in (1, 2):
                        cols = slice(16 * (H - 1), 16 * H)
                        root(r_q[:, cols], ss_q[:, cols], 16, g * 2 + (ROOT_Q + H - 1))
            with pool.Fori(0, 3) as i:
                for k in range(KC):
                    split_lo(6 * KC, i, k)
            for k in range(KC):
                split_lo(9 * KC, 0, k)
                if k == 8:
                    root(r_m[:], ss_m[:], 1, ROOT_M, META)
            with pool.Fori(0, 3) as i:
                for k in range(KC):
                    split_lo(10 * KC, i, k)
            for c in (13, 14, 15):
                for k in range(KC):
                    split_lo(c * KC, 0, k)
                    if c == 13 and k == 9:
                        root(r_2[:], ss_1[:], NT, ROOT_2)
                    if c == 14 and k == 3:
                        root(r_kv[:], ss_kv[:], NT + 1, ROOT_KV)
                    if c == 15 and k == 3:
                        root(r_cq[:], ss_cq[:], NT, ROOT_CQ)
            with pool.Fori(0, 3) as i:
                for k in range(KC):
                    split_lo(16 * KC, i, k)
            def by_rows(d, cols):
                return d[0:S, cols].rearrange("(t p) c -> p t c", p=P)

            def load_qk(A, i, head):
                buf = head % 2
                if not (A.mla and i == 0 and head < 2):
                    B, n, last = before(A, i, head)
                    pool.wait_ge(B.free, n * (4 * B.batches + NU) + (turned_by[B][last] + 1))
                q, k = (QB, 2 * VD) if A.mla else (VD, VD)
                qd, kd = (qb_d, kvb_d) if A.mla else (qa_d, kv_d)
                head += 4 * i
                pool.dma_start(nat_q[:, buf, :, 0:q], by_rows(qd, slice(head * q, (head + 1) * q))).then_inc(A.ld_qk[buf], 16)
                keys = slice(head * k, head * k + VD)
                pool.dma_start(nat_k[:, buf], by_rows(kd, keys)).then_inc(A.ld_qk[buf], 16)
                if A.mla:
                    pool.dma_start(natm_k[:, buf], kd[S:KEYS, keys]).then_inc(A.ld_qk[buf], 16)

            def load_v(A, i, head):
                buf = head % 2
                if not (A.mla and i == 0 and head < 2):
                    B, n, last = before(A, i, head)
                    pool.wait_ge(B.pv, n * NU + ((last + 1) * NT + EARLY))
                kd, at_ = (kvb_d, (4 * i + head) * 2 * VD + VD) if A.mla else (kv_d, (HEADS + 4 * i + head) * VD)
                cols = slice(at_, at_ + VD)
                pool.dma_start(nat_v[:, buf], by_rows(kd, cols)).then_inc(A.ld_v[buf], 16)
                pool.dma_start(natm_v[0:META, buf], kd[S:KEYS, cols]).then_inc(A.ld_v[buf], 16)

            def before(A, i, head):
                if head >= 2:
                    return A, i, head - 2
                return (A, i - 1, head + 2) if i else (MLA, 1, head + 2)

            def turn_uses(A):
                uses = sorted([(turn_time(A, h, b), 0, h) for h in range(4) for b in range(A.batches)]
                              + [(unit_time(u) + A.turn_after, 1, u) for u in range(NU)])
                return [max(n for n, (_, kind, h) in enumerate(uses) if kind == 0 and h == head) + 1 for head in range(4)]

            turned_by = {A: turn_uses(A) for A in (MLA, DIFF)}

            def weigh_distances(i, head):
                n = 4 * i + head
                if n < 2:
                    pool.wait_ge(MLA.m, 2 * NU + 1)
                    pool.wait_ge(s_km_ps, 1)
                else:
                    pool.wait_ge(DIFF.m, (n - 1) * NT * 2 + 1)
                nc.gpsimd.tensor_scalar(alibi_h[:, head % 2], alibi[:], slopes[:, n:n + 1], None, ALU.mult).then_inc(DIFF.slope, 1)

            def attend_loads(A, i, n0, then):
                for Q in range(4 * KC):
                    if Q % 4 == 0:
                        split_lo(n0 + i * KC, 0, Q // 4)
                    if A.mla and i == 1 and Q == 60:
                        pool.wait_ge(MLA.m, 2 * NU + 1)
                        pool.dma_start(alibi[:], a["alibi"]).then_inc(s_alibi, 16)
                    for head in range(4):
                        if not A.mla and Q == max(12 * head - 4, 0):
                            weigh_distances(i, head)
                    for n, head in enumerate([(A, i, 2), (A, i, 3)] + ([(*then, 0), (*then, 1)] if then else [])):
                        if Q == 12 * n + 12:
                            load_qk(*head)
                        if Q == 12 * n + 25:
                            load_v(*head)

            for k in range(Q_BASE - UQ):
                split_lo(UQ, 0, k)
                if k == 17:
                    pool.wait_ge(s_used, UKV + 4)
                    pool.wait_ge(s_short[1], 2 * 16)
                    pool.wait_ge(s_short[0], 3 * 16)
                    pool.wait_ge(s_mst, 5 * 16)
                    load_qk(MLA, 0, 0)
            load_qk(MLA, 0, 1)
            pool.wait_ge(s_zero, 1)
            load_v(MLA, 0, 0)
            load_v(MLA, 0, 1)
            for signal in s_short:
                pool.wait_ge(signal, 4 * 16)
            pool.wait_ge(s_mst, 8 * 16)
            pool.dma_start(diff_km[:], kv_d[S:KEYS, 0:HEADS * VD]).then_inc(s_km_in, 16)
            attend_loads(MLA, 0, Q_BASE, (MLA, 1))
            pool.wait_ge(s_st, 4 * 16)
            attend_loads(MLA, 1, Q_BASE, (DIFF, 0))
            pool.wait_ge(s_st, 5 * 16)
            pool.wait_ge(s_alibi, 16)
            pool.wait_ge(s_small2, 9 * 16)
            attend_loads(DIFF, 0, Q_BASE + 2 * KC, (DIFF, 1))
            attend_loads(DIFF, 1, Q_BASE + 2 * KC, None)
            for c in range(6):
                for k in range(KC):
                    split_lo(Q_BASE + 4 * KC, c, k)
                    if (c, k) == (1, 0):
                        root(r_o, ss_o, NT * 4, ROOT_O)
                    if (c, k) == (1, 14):
                        root(r_o, ss_o, NT * 4, ROOT_O + 1)
            root(r_3[:], ss_2[:], NT, ROOT_3)

        @block.vector
        def _(dve):
            V = nc.vector

            def turn_lo(b, bank, dst, hi, gain):
                dve.wait_ge(s_turn_hi, b + 1)
                V.scalar_tensor_tensor(dst, turn[bank][:], gain, hi.bitcast(F32), ALU.mult, ALU.subtract).then_inc(s_turn_lo, 1)

            dve.sem_inc(s_turn_lo, EARLY)
            dve.sem_inc(s_m, EARLY)
            dve.sem_inc(s_qT, EARLY)
            dve.sem_inc(s_o, 1)
            dve.sem_inc(s_mevac, 1)
            for A in (MLA, DIFF):
                dve.sem_inc(A.m, 1)
                dve.sem_inc(A.o, 1)
            V.memset(metaT[:].bitcast(F32), 0.0)
            V.memset(ckvmT[:].bitcast(F32), 0.0)
            V.memset(ss_kv[:], 1.0)
            V.memset(rel[32:33, :], BANNED).then_inc(s_rel, 1)
            for b in range(KC):
                turn_lo(b, b % 2, setA_lo[:, b], setA_hi[:, b], gain_in[:, b:b + 1])
                if b % 3 == 0 and 0 < b < KC - 1:
                    if b == 3:
                        for signal in s_x:
                            dve.wait_ge(signal, 16)
                    t = b // 3 - 1
                    after(dve, V.tensor_tensor_reduce(work[:].rearrange("p t c -> p (t c)"), x_nat[:, t], x_nat[:, t], 1.0, 0.0,
                                                      ALU.mult, ALU.add, ss_x[:, t:t + 1]))
            V.tensor_scalar(ss_x[:], ss_x[:], 1.0 / D, EPS, ALU.mult, ALU.add).then_inc(s_var, 1)

            dve.wait_ge(s_small, 96)
            after(dve, V.tensor_tensor(gain_qk[:, 0], gain_qk[:, 0], gain_qk[:, 1], ALU.mult))
            after(dve, V.tensor_scalar(gain_qk[:, 0], gain_qk[:, 0], HD ** -0.5, None, ALU.mult))
            dve.wait_ge(s_evac, 8)
            k_st = stage[:, :, 0:256]
            after(dve, V.tensor_tensor(work[:, :, 0:256], k_st, k_st, ALU.mult))
            after(dve, V.tensor_reduce(ss_q[:, 0:16].rearrange("p (t h) -> p t h", t=NT),
                                       work[:, :, 0:256].rearrange("p t (h d) -> p t h d", d=HD), AX.X, ALU.add))
            V.tensor_scalar(ss_q[:, 0:16], ss_q[:, 0:16], 1.0 / HD, EPS, ALU.mult, ALU.add).then_inc(s_var, 1)
            V.tensor_copy(v_nat[:], stage[:, :, 256:512].rearrange("p t (h d) -> p t h d", d=HD)).then_inc(s_kn, 1)
            dve.wait_ge(s_root, ROOT_K)
            for t in range(NT):
                last = V.tensor_tensor(kn[:, t], stage[:, t, 0:256].rearrange("p (h d) -> p h d", d=HD),
                                       r_q[:, 4 * t:4 * t + 4].unsqueeze(2).to_broadcast([P, KVH, HD]), ALU.mult)
            last.then_inc(s_kn, 1)
            dve.wait_ge(s_kn, 2)
            for t in range(NT):
                last = V.tensor_tensor(kn[:, t], kn[:, t], gain_qk[:, 0].unsqueeze(1).to_broadcast([P, KVH, HD]), ALU.mult)
            after(dve, last)

            def low_qT(g, b):
                dve.wait_ge(s_qhi, g * 5 + b + 1)
                if b == 0:
                    V.tensor_tensor(kT_lo[:], turn[1][:], kT_hi[:].bitcast(F32), ALU.subtract).then_inc(s_qT, 1)
                    return
                for h in range(2):
                    rows, rest = slice(h * HD, (h + 1) * HD), slice((1 - h) * HD, (2 - h) * HD)
                    last = V.tensor_tensor(head_T(b, h)[rest], turn[(b + 1) % 2][rows], head_T(b, h)[rows].bitcast(F32), ALU.subtract)
                last.then_inc(s_qT, 1)

            def soften(g, u):
                dve.wait_ge(s_score, g * UNITS + u + 1)
                if u == 0:
                    dve.wait_ge(s_bias, (g + 1) * (16 * P // SKEW))
                hp, first = u // NT, P if u % NT == 0 else 0
                V.tensor_copy(sink_p[:, u % 2], sink_g[:, 2 * hp:2 * hp + 2])
                for h in range(2):
                    head = 2 * hp + h
                    last = V.tensor_tensor_reduce(sm[:, u % 2, h, first:], sc[h][:, first:256],
                                                  bias[:, head, first:], -1.0, sink_g[:, head:head + 1],
                                                  ALU.add, ALU.min, negm[:, u % 2, h:h + 1])
                after(dve, last)
                V.tensor_tensor(sink_d[:, u % 2], negm[:, u % 2], sink_p[:, u % 2], ALU.subtract).then_inc(s_m, 1)

            def denominators(g, u):
                dve.wait_ge(s_p, g * UNITS + u + 1)
                after(dve, V.tensor_tensor(den[:, u % 2], den[:, u % 2], sink_e[:, u % 2], ALU.add))
                after(dve, V.reciprocal(rden[:, u % 2], den[:, u % 2]))

            def keep_o(g, u):
                dve.wait_ge(s_pv, g * UNITS + u + 1 + EARLY)
                hp, j = u // NT, u % NT
                dst = o_nat[:, bass.ds(g, 1), j, hp * P:(hp + 1) * P].rearrange("p o (h d) -> p (o h) d", h=2)
                V.tensor_tensor(dst, o_ps[:, 0:P].rearrange("p (h d) -> p h d", h=2),
                                rden[:, u % 2].unsqueeze(2).to_broadcast([P, 2, HD]), ALU.mult).then_inc(s_o, 1)

            BODY = NT + 3 + UNITS * 3
            start = link.n
            with dve.Fori(0, 4) as g:
                link.base, link.n = g * BODY + start, 0
                for H in range(32):
                    if H == 0:
                        for h in range(2):
                            last = V.tensor_copy(k_twice[:, :, h:h + 1], kn[:, :, bass.ds(g, 1)])
                        last.then_inc(s_kdup, 1)
                        V.tensor_copy(vg[:].unsqueeze(2), v_nat[:, :, bass.ds(g, 1)])
                        after(dve, V.tensor_scalar(sink_g[:], sinks[:, bass.ds(g * GROUP, GROUP)], -1.0, None, ALU.mult))
                        for pair in ((0, 1), (2, 3)):
                            cols = slice(GROUP * pair[0], GROUP * (pair[1] + 1))
                            for t in pair:
                                dve.wait_ge(s_evac, 4 * g + (9 + t))
                                after(dve, V.tensor_tensor(work[:, t], stage[:, t], stage[:, t], ALU.mult))
                                last = V.tensor_reduce(ss_q[:, GROUP * t:GROUP * (t + 1)],
                                                       work[:, t].rearrange("p (h d) -> p h d", d=HD), AX.X, ALU.add)
                            after(dve, last)
                            V.tensor_scalar(ss_q[:, cols], ss_q[:, cols], 1.0 / HD, EPS, ALU.mult, ALU.add).then_inc(s_var, 1)
                    if H == 3:
                        low_qT(g, 0)
                    if H == 4:
                        for t in range(NT):
                            if t % 2 == 0:
                                dve.wait_ge(s_root, g * 2 + (ROOT_Q + t // 2))
                            st = stage[:, t].rearrange("p (h d) -> p h d", d=HD)
                            last = V.tensor_tensor(st, st, r_q[:, 8 * t:8 * t + 8].unsqueeze(2).to_broadcast([P, GROUP, HD]), ALU.mult)
                        last.then_inc(s_qn, 1)
                    if 0 <= H - 16 < UNITS:
                        keep_o(g, H - 16)
                    if 0 <= H - 14 < UNITS:
                        denominators(g, H - 14)
                    if 0 <= H - 12 < UNITS:
                        soften(g, H - 12)
                    if 10 <= H < 14:
                        low_qT(g, H - 9)
                n_body = link.n
            assert n_body == BODY
            link.base, link.n = 0, start + 4 * BODY

            def gate(g, o_g, dst=stage):
                dve.wait_ge(s_silu, g + 1)
                after(dve, V.tensor_tensor(dst[:], dst[:], work[:], ALU.mult))
                V.tensor_tensor(dst[:], dst[:], o_g, ALU.mult).then_inc(s_og, 1)

            start2 = link.n
            with dve.Fori(0, 3) as i:
                link.base, link.n = i + start2, 0
                gate(i, o_nat[:, bass.ds(i, 1)].rearrange("p o t c -> p (o t) c"))
                for f in range(4):
                    slot = bass.ds(i * 4 + f, 1)
                    turn_lo(i * 4 + (16 + f), f % 2, setB_lo[:, slot].rearrange("p o s -> p (o s)"),
                            setB_hi[:, slot].rearrange("p o s -> p (o s)"), 1.0)
            link.base, link.n = 0, start2 + 3
            gate(3, o_nat[:, 3])
            for f in range(4):
                turn_lo(28 + f, f % 2, setB_lo[:, 12 + f], setB_hi[:, 12 + f], 1.0)
            dve.wait_ge(s_meta_in, 16)
            after(dve, V.tensor_tensor_reduce(meta_sq[:], meta_nat[:], meta_nat[:], 1.0, 0.0, ALU.mult, ALU.add, ss_m[:]))
            V.tensor_scalar(ss_m[:], ss_m[:], 1.0 / D, EPS, ALU.mult, ALU.add).then_inc(s_var, 1)
            dve.wait_ge(s_mturn, 1)
            dve.wait_ge(s_small, 112)
            V.tensor_tensor(meta_f[:], sc[1][:, 0:KC * META].rearrange("p (k m) -> p k m", k=KC),
                            gain_2[:].unsqueeze(2).to_broadcast([P, KC, META]), ALU.mult).then_inc(s_metaF, 1)
            dve.wait_ge(s_metaH, 1)
            V.tensor_tensor(metaT[:, :, 32:32 + META], meta_f[:], metaT[:, :, 0:META].bitcast(F32),
                            ALU.subtract).then_inc(s_metaT, 1)
            def residual(c):
                dve.wait_ge(s_evac, 4 * c + 44)
                dve.wait_ge(s_xin, 16 * c + 16)
                after(dve, V.tensor_tensor(stage[:], stage[:], x_in[:], ALU.add))
                for t in range(NT):
                    last = V.tensor_tensor_reduce(x_in[:, t], stage[:, t], stage[:, t], 1.0, 0.0,
                                                  ALU.mult, ALU.add, ss_c[:, t:t + 1])
                last.then_inc(s_x1, 1)
                dve.wait_ge(s_x1, c + 1)
                after(dve, V.tensor_tensor(ss_1[:], ss_1[:], ss_c[:], ALU.add))
                if isinstance(c, int):
                    last = V.tensor_copy(gain_c[:], gain_2[:, 4 * c:4 * c + 4])
                else:
                    last = V.tensor_copy(gain_c[:], gain_2[:, bass.ds(c * 4, 4)])
                last.then_inc(s_gain_c, 1)
                dve.wait_ge(s_gain_c, c + 1)

            def x1_lo(c):
                for f in range(4):
                    if isinstance(c, int):
                        lo, hi = setA_lo[:, 4 * c + f], setA_hi[:, 4 * c + f]
                    else:
                        lo, hi = (s_[:, bass.ds(c * 4 + f, 1)].rearrange("p o s -> p (o s)") for s_ in (setA_lo, setA_hi))
                    turn_lo(c * 4 + (32 + f), f % 2, lo, hi, gain_c[:, f:f + 1])

            after(dve, V.memset(ss_1[:], 0.0))
            start3 = link.n
            with dve.Fori(0, 3) as i:
                link.base, link.n = i * 2 + start3, 0
                residual(i)
                x1_lo(i)
            link.base, link.n = 0, start3 + 6
            residual(3)
            V.tensor_scalar(ss_1[:], ss_1[:], 1.0 / D, EPS, ALU.mult, ALU.add).then_inc(s_var, 1)
            x1_lo(3)

            def keep_meta(m, r, cols=CW, stores=0):
                dve.wait_ge(s_mtmp, m + 1)
                V.tensor_tensor(sum_m[:, 0:cols], sc[0][0:META, 0:cols], tmp_m[:, 0:cols], ALU.add).then_inc(s_mevac, 1)
                dve.wait_ge(s_mevac, m + 2)
                dve.wait_ge(s_mst, stores * 16)
                V.tensor_scalar(stage_m[:, 0:cols], sum_m[:, 0:cols], r, None, ALU.mult).then_inc(s_mstage, 1)

            def rotate(dst, src, c, s_, tmp):
                x1, x2_ = src
                V.tensor_tensor(tmp[0], x1, c, ALU.mult)
                V.tensor_tensor(tmp[1], x2_, s_, ALU.mult)
                V.tensor_tensor(tmp[2], x1, s_, ALU.mult)
                after(dve, V.tensor_tensor(tmp[3], x2_, c, ALU.mult))
                V.tensor_tensor(dst[0], tmp[0], tmp[1], ALU.subtract)
                return V.tensor_tensor(dst[1], tmp[2], tmp[3], ALU.add)

            HR = ROPE // 2
            keep_meta(0, r_m[:, 0:1], 320)
            dve.wait_ge(s_mstage, 1)
            dve.wait_ge(s_evac, 4 * 13 + 8)
            for t in range(NT):
                V.tensor_tensor_reduce(work[:, t, 0:CKV], stage[:, t, 0:CKV], stage[:, t, 0:CKV], 1.0, 0.0,
                                       ALU.mult, ALU.add, ss_kv[:, t:t + 1])
            after(dve, V.tensor_tensor_reduce(sum_m[:, 0:CKV], stage_m[:, 0:CKV], stage_m[:, 0:CKV], 1.0, 0.0,
                                              ALU.mult, ALU.add, ss_kv[0:META, NT:NT + 1]))
            V.tensor_scalar(ss_kv[:], ss_kv[:], 1.0 / CKV, EPS, ALU.mult, ALU.add).then_inc(s_var, 1)
            dve.wait_ge(s_small2, 9 * 16)
            rotate((kpe[:, :, 0:HR], kpe[:, :, HR:ROPE]), (stage[:, :, CKV:CKV + HR], stage[:, :, CKV + HR:CKV + ROPE]),
                   cos[:], sin[:], [rope_t[:, n] for n in range(4)])
            after(dve, V.tensor_scalar(subln[:], subln[:], 1.0 - LAM0, None, ALU.mult))
            rotate((kpe_m[:, 0:HR], kpe_m[:, HR:ROPE]), (stage_m[:, CKV:CKV + HR], stage_m[:, CKV + HR:CKV + ROPE]),
                   cos_m[:], sin_m[:], [rope_t[0:META, n, 0] for n in range(4)]).then_inc(s_kpe, 1)
            dve.wait_ge(s_lam, 16)
            for n in range(2):
                last = V.tensor_tensor_reduce(work[:, n, 0:QKD], lam_in[:, 2 * n], lam_in[:, 2 * n + 1], 1.0, 0.0,
                                              ALU.mult, ALU.add, lam_s[:, n:n + 1])
            last.then_inc(s_lam, 1)
            for f in range(2):
                if f == 0:
                    dve.wait_ge(s_kpeT, 2)
                    for half in (slice(0, ROPE), slice(ROPE, P)):
                        V.tensor_tensor(kpeT_lo[half, META:KEYS], sc[1][0:ROPE, :], kpeT_hi[0:ROPE, META:KEYS].bitcast(F32), ALU.subtract)
                        V.tensor_tensor(kpeT_lo[half, 0:META], sc[0][0:ROPE, 0:META], kpeT_hi[0:ROPE, 0:META].bitcast(F32), ALU.subtract)
                last = V.scalar_tensor_tensor(ckvmT[:, f, 32:32 + META], sc[0][:, (f + 1) * META:(f + 2) * META],
                                              gain_ckv[:, f:f + 1], ckvmT[:, f, 0:META].bitcast(F32), ALU.mult, ALU.subtract)
                last.then_inc(s_ckvm, 1)
            for f in range(2):
                turn_lo(48 + f, f % 2, ckvT_lo[:, f], ckvT_hi[:, f], gain_ckv[:, f:f + 1])
            dve.wait_ge(s_lam, 18)
            after(dve, V.tensor_tensor(neglam[:], lam_s[:, 1:2], lam_s[:, 0:1], ALU.subtract))
            V.tensor_scalar(neglam[:], neglam[:], LAM0, None, ALU.subtract)
            dve.wait_ge(s_evac, 4 * 14 + 8)
            for t in range(NT):
                last = V.tensor_tensor_reduce(work[:, t], stage[:, t], stage[:, t], 1.0, 0.0, ALU.mult, ALU.add, ss_cq[:, t:t + 1])
            after(dve, last)
            V.tensor_scalar(ss_cq[:], ss_cq[:], 1.0 / CQ, EPS, ALU.mult, ALU.add).then_inc(s_var, 1)
            for f in range(4):
                turn_lo(50 + f, f % 2, cqT_lo[:, f], cqT_hi[:, f], gain_cq[:, f:f + 1])
            for m in range(1, 9):
                keep_meta(m, r_m[:, 0:1] if m < 5 else r_kv[0:META, NT:NT + 1], stores=m - 1)

            dve.wait_ge(s_used, Q_BASE + 4)
            V.memset(natm_v[:], 0.0)
            dve.wait_ge(s_short[0], 4 * 16)
            after(dve, V.memset(pTm[:], 0.0))
            V.memset(tick[:], 0.0).then_inc(s_zero, 1)

            def soften2(A, i, u, comp):
                head, j = u // NT, u % NT
                lo, slot = S - (j + 1) * P, u % 2 if A.mla else comp
                if not A.mla and j == 0 and comp == 0:
                    dve.wait_ge(A.slope, i * 4 + (head + 1))
                dve.wait_ge(A.score, i * NU * A.comps + (u * A.comps + comp + 1))
                n = 2 * (u % 2) + comp
                V.memset(tick[:, n:n + 1], 0.0)
                add = mask[:, lo:] if A.mla else alibi_h[:, head % 2, ALIBI_AT[j]:ALIBI_AT[j + 1]]
                start = score_at(A, u, comp)
                V.tensor_tensor_reduce(sm2[:, slot, lo:], sc2[:, start:start + width(j)], add, -1.0, CEILING, ALU.add, ALU.min,
                                       negm_2[:, u % 2, comp:comp + 1]).then_inc(A.m, 1)

            def combine(A, i, u):
                b, lo = u % 2, S - (u % NT + 1) * P
                dve.wait_ge(A.p, i * NU * A.comps + (u + 1) * A.comps)
                after(dve, V.reciprocal(rden_2[:, b, 0:A.comps], den_2[:, b, 0:A.comps]))
                if not A.mla:
                    after(dve, V.scalar_tensor_tensor(coef[:, b:b + 1], den_2[:, b, 0:1], neglam[:, 0:1], rden_2[:, b, 1:2],
                                                      ALU.mult, ALU.mult))
                    V.scalar_tensor_tensor(p2[:, b, 0, lo:], p2[:, b, 1, lo:], coef[:, b:b + 1], p2[:, b, 0, lo:],
                                           ALU.mult, ALU.add).then_inc(A.w, 1)

            def keep_o2(A, i, u):
                head, j = u // NT, u % NT
                dve.wait_ge(A.pv, i * NU + (u + 1 + EARLY))
                dst = o_nat[:, bass.ds(i + (2 if A.mla else 0), 1), j, head * VD:(head + 1) * VD].rearrange("p o c -> p (o c)")
                V.tensor_scalar(dst, turn[1][:, 2 * P:3 * P], rden_2[:, u % 2, 0:1], None, ALU.mult).then_inc(A.o, 1)

            def attend_body(A, i):
                for Q in range(4 * KC):
                    for u in range(NU):
                        if Q == unit_time(u) + A.values_after:
                            keep_o2(A, i, u)
                    for u in range(NU):
                        if Q == unit_time(u) + 2:
                            combine(A, i, u)
                    for head in range(4):
                        if A.mla and Q == max(12 * head, 4):
                            buf = head % 2
                            dve.wait_ge(MLA.ld_qk[buf], (i * 2 + (head // 2 + 1)) * 48)
                            x1, x2_ = nat_q[:, buf, :, VD:VD + HR], nat_q[:, buf, :, VD + HR:QB]
                            rotate((x1, x2_), (x1, x2_), cos[:], sin[:], [rope_t[:, n] for n in range(4)]).then_inc(MLA.rope, 1)
                            dve.wait_ge(MLA.rope, i * 4 + (head + 1))
                        if A.mla and Q == turn_time(A, head, 1):
                            dve.wait_ge(s_qp_hi, i * 4 + (head + 1))
                            V.scalar_tensor_tensor(qpT[0:ROPE, head % 2], turn[0][ROPE:P, :], B_SCALE,
                                                   qpT[ROPE:P, head % 2].bitcast(F32), ALU.mult, ALU.subtract).then_inc(MLA.free, 1)
                    for u in range(NU):
                        for comp in range(A.comps):
                            if Q == unit_time(u) + comp:
                                soften2(A, i, u, comp)

            for A, body in ((MLA, 4 + NU), (DIFF, 2 * NU)):
                first = link.n
                with dve.Fori(0, 2) as i:
                    link.base, link.n = i * body + first, 0
                    attend_body(A, i)
                    assert link.n == body, (link.n, body)
                link.base, link.n = 0, first + 2 * body

            def sub_norm(c, root):
                o = o_nat[:, c].rearrange("p t (h d) -> p t h d", d=VD)
                after(dve, V.tensor_tensor(o_sq[:], o_nat[:, c], o_nat[:, c], ALU.mult))
                after(dve, V.tensor_reduce(ss_o.rearrange("p (t h) -> p t h", t=NT),
                                           o_sq[:].rearrange("p t (h d) -> p t h d", d=VD), AX.X, ALU.add))
                V.tensor_scalar(ss_o, ss_o, 1.0 / VD, EPS, ALU.mult, ALU.add).then_inc(s_var, 1)
                dve.wait_ge(s_root, root)
                for t in range(NT):
                    last = V.tensor_tensor(o[:, t], o[:, t], r_o[:, 4 * t:4 * t + 4].unsqueeze(2).to_broadcast([P, 4, VD]), ALU.mult)
                after(dve, last)
                for t in range(NT):
                    last = V.tensor_tensor(o[:, t], o[:, t], subln[:].unsqueeze(1).to_broadcast([P, 4, VD]), ALU.mult)
                after(dve, last)

            def gated_lo(b, kc):
                for f in range(4):
                    turn_lo(b + f, f % 2, setB_lo[:, kc + f], setB_hi[:, kc + f], 1.0)

            gate(4, o_nat[:, 3])
            gate(5, o_nat[:, 2], gate_0)
            gated_lo(54, 12)
            gated_lo(58, 8)
            sub_norm(0, ROOT_O)
            gate(6, o_nat[:, 0])
            gated_lo(62, 0)
            sub_norm(1, ROOT_O + 1)
            gate(7, o_nat[:, 1])
            gated_lo(66, 4)

            def residual2(c):
                dst = h2[:, c] if isinstance(c, int) else h2[:, bass.ds(c, 1)].rearrange("p o t c -> p (o t) c")
                dve.wait_ge(s_evac, 4 * c + (4 * 32 + 8))
                dve.wait_ge(s_x1in, 16 * c + 16)
                after(dve, V.tensor_tensor(stage[:], stage[:], x_in[:], ALU.add))
                for t in range(NT):
                    V.tensor_tensor_reduce(x_in[:, t], stage[:, t], stage[:, t], 1.0, 0.0, ALU.mult, ALU.add, ss_c[:, t:t + 1])
                V.tensor_tensor(dst, stage[:], w_final[:, bass.ds(c * CW, CW)].unsqueeze(1).to_broadcast([P, NT, CW]),
                                ALU.mult).then_inc(s_h2, 1)
                dve.wait_ge(s_h2, c + 1)
                after(dve, V.tensor_tensor(ss_2[:], ss_2[:], ss_c[:], ALU.add))

            dve.wait_ge(s_fin_w, 16)
            after(dve, V.memset(ss_2[:], 0.0))
            first = link.n
            with dve.Fori(0, 3) as i:
                link.base, link.n = i * 2 + first, 0
                residual2(i)
            link.base, link.n = 0, first + 6
            dve.wait_ge(s_x1in, 64)
            for t in range(NT):
                if t < NT - 1:
                    dve.wait_ge(s_acc, 3 * 35 + t + 1)
                else:
                    dve.wait_ge(s_used, PIECES + 4)
                V.tensor_tensor(stage[:, t], acc[t][:], x_in[:, t], ALU.add).then_inc(s_sum, 1)
            for t in range(NT):
                if t == 2:
                    dve.wait_ge(s_sq, NT)
                    after(dve, V.tensor_tensor(ss_2[:], ss_2[:], ss_c[:], ALU.add))
                    V.tensor_scalar(ss_2[:], ss_2[:], 1.0 / D, EPS, ALU.mult, ALU.add).then_inc(s_var, 1)
                dve.wait_ge(s_sum, t + 1)
                V.tensor_tensor(h2[:, 3, t], stage[:, t], w_final[:, 3 * CW:D], ALU.mult)
            V.memset(tick[:, 0:1], 0.0).then_inc(s_h2, 1)
            dve.wait_ge(s_h2, 4)
            dve.wait_ge(s_root, ROOT_3)
            for t in range(NT - 1):
                V.tensor_scalar(h2[:, :, t], h2[:, :, t], r_3[:, t:t + 1], None, ALU.mult).then_inc(s_fin, 1)


_BY_PARTITION = ["swa_norm", "attn_norm_w", "mla_q_norm_w", "mla_kv_norm_w"]
_INS = ["x", "rel_bias", "swa_norm", "swa_w_in", "swa_q_gain", "swa_k_gain", "swa_sinks", "swa_w_out", "meta_tokens_2",
        "attn_norm_w_2", "w_in_2", "diff_lambda_2", "diff_subln_w_2", "mla_q_norm_w_2", "w_uq_2", "mla_kv_norm_w_2",
        "w_ukv_2", "w_out_2", "final_norm_w_2"]


def kernel(**inputs):
    import numpy as _np
    import concourse.bacc as _bacc
    from concourse import mybir as _mybir
    from concourse.bass_utils import run_bass_kernel_spmd as _run

    nc = _bacc.Bacc("TRN2", target_bir_lowering=False, num_devices=1)
    arrays, args = {}, {}

    def give(name, v):
        arrays[f"in_{name}"] = v
        args[name] = nc.dram_tensor(f"in_{name}", v.shape, _mybir.dt.float32, kind="ExternalInput").ap()

    for name in _INS:
        v = _np.ascontiguousarray(inputs[name])
        name = name.removesuffix("_2")
        v = v[0] if v.shape[0] == 1 else v
        give(name, _np.ascontiguousarray(v.reshape(-1, P).T) if name in _BY_PARTITION else v)
    give("t5_marks", t5_onehot())
    for name, v in zip(("cos", "cos_m", "sin", "sin_m"), rotations()):
        give(name, v)
    give("mask", causal_mask())
    give("alibi", alibi_distance())
    give("slopes", _np.tile(_np.exp2(-8.0 * _np.arange(1, HEADS + 1) / HEADS).astype(_np.float32), (P, 1)))
    out = nc.dram_tensor("out0", (S, D), _mybir.dt.float32, kind="ExternalOutput").ap()
    build(nc, args, out)
    r = _run(nc, [arrays], core_ids=[0])
    return r.results[0]["out0"].reshape(1, S, D)
```
